# Optimizing a Trainium2 kernel written in Bass

```python
import jax, jax.numpy as jnp
from jax import lax
import numpy as np
import math

D_MODEL = 1024
BATCH = 1
SEQ = 512
DEPTH = 2

N_MIXERS = 2
N_POOL_GROUPS = 4
POOL_GROUP = D_MODEL // N_POOL_GROUPS
POOL_WINDOWS = (2, 4, 8, 16)
N_HEADS = 16
QK_NOPE = 64
QK_ROPE = 32
V_HEAD = 64
Q_LORA = D_MODEL // 4
KV_LORA = D_MODEL // 8
ROPE_THETA = 10000.0
D_FF = 11 * D_MODEL // 4
Q_BLOCK = 128
EPS = 1e-6
N_MOD = 9
N_POOL_LAYERS = (DEPTH + 1) // 2
N_MLA_LAYERS = DEPTH // 2
ATTN_SCALE = (QK_NOPE + QK_ROPE) ** -0.5


def rmsnorm(x, g):
    xf = x.astype(jnp.float32)
    y = xf * lax.rsqrt(jnp.mean(xf * xf, axis=-1, keepdims=True) + EPS)
    return (y * g.astype(jnp.float32)).astype(x.dtype)

def swiglu(h, w_in, w_out):
    gate, up = jnp.split(h @ w_in, 2, axis=-1)
    return (jax.nn.silu(gate) * up) @ w_out

def centred_mean(x, window):
    s = x.shape[1]
    cs = lax.cumsum(x.astype(jnp.float32), axis=1)
    cs = jnp.pad(cs, ((0, 0), (1, 0), (0, 0)))
    t = jnp.arange(s)
    hi = jnp.clip(t + window // 2, 0, s)
    lo = jnp.clip(t - window // 2, 0, s)
    tot = jnp.take(cs, hi, axis=1) - jnp.take(cs, lo, axis=1)
    cnt = (hi - lo).astype(jnp.float32)[None, :, None]
    return (tot / cnt).astype(x.dtype)

def pool_mixer(h, w, b, scale):
    B, S, _ = h.shape
    hg = h.reshape(B, S, N_POOL_GROUPS, POOL_GROUP)
    pooled = jnp.stack([centred_mean(hg[:, :, g], POOL_WINDOWS[g]) for g in range(N_POOL_GROUPS)], axis=2)
    y = jnp.einsum('bsgc,gcd->bsgd', pooled - hg, w) + b
    return y.reshape(B, S, D_MODEL) * scale

def rope_tables(s, dtype):
    inv = 1.0 / (ROPE_THETA ** (jnp.arange(0, QK_ROPE, 2, dtype=jnp.float32) / QK_ROPE))
    ang = jnp.arange(s, dtype=jnp.float32)[:, None] * inv[None, :]
    return jnp.cos(ang).astype(dtype), jnp.sin(ang).astype(dtype)

def apply_rope(x, cos, sin):
    x1, x2 = jnp.split(x, 2, axis=-1)
    return jnp.concatenate([x1 * cos - x2 * sin, x2 * cos + x1 * sin], axis=-1)

def mla_mixer(h, w_in, q_norm, kv_norm, w_uq, w_uk, w_uv, w_o, cos, sin):
    B, S, _ = h.shape
    lat = h @ w_in
    c_q, c_kv, k_r = jnp.split(lat, [Q_LORA, Q_LORA + KV_LORA], axis=-1)
    c_q = rmsnorm(c_q, q_norm)
    c_kv = rmsnorm(c_kv, kv_norm)
    q = jnp.einsum('bsc,chd->bshd', c_q, w_uq)
    q_nope, q_rope = q[..., :QK_NOPE], q[..., QK_NOPE:]
    q_rope = apply_rope(q_rope, cos[:, None, :], sin[:, None, :]) * ATTN_SCALE
    k_rope = apply_rope(k_r, cos, sin)
    q_lat = jnp.einsum('bshn,chn->bshc', q_nope, w_uk) * ATTN_SCALE
    nb = S // Q_BLOCK
    qlb = q_lat.reshape(B, nb, Q_BLOCK, N_HEADS, KV_LORA).transpose(1, 0, 2, 3, 4)
    qrb = q_rope.reshape(B, nb, Q_BLOCK, N_HEADS, QK_ROPE).transpose(1, 0, 2, 3, 4)

    def block(args):
        ql, qr = args
        s = (jnp.einsum('bqhc,bkc->bhqk', ql, c_kv)
             + jnp.einsum('bqhr,bkr->bhqk', qr, k_rope))
        p = jax.nn.softmax(s.astype(jnp.float32), axis=-1).astype(c_kv.dtype)
        return jnp.einsum('bhqk,bkc->bqhc', p, c_kv)

    o_lat = lax.map(block, (qlb, qrb))
    o_lat = o_lat.transpose(1, 0, 2, 3, 4).reshape(B, S, N_HEADS, KV_LORA)
    o = jnp.einsum('bshc,chv->bshv', o_lat, w_uv)
    return o.reshape(B, S, N_HEADS * V_HEAD) @ w_o

def modulated_sublayer(x, mod, g_pre, g_post, fn, weight):
    shift, scale, gate = mod[:, 0], mod[:, 1], mod[:, 2]
    h = rmsnorm(x, g_pre) * (1.0 + scale) + shift
    y = rmsnorm(fn(h), g_post)
    return x + weight * (1.0 + gate) * y

def first_inputs(seed: int = 0) -> dict:
    key = jax.random.key(seed)
    ks = jax.random.split(key, 20)
    n = jax.random.normal
    f32 = jnp.float32
    return {
        "x": n(ks[0], (BATCH, SEQ, D_MODEL), f32),
        "c": n(ks[1], (BATCH, D_MODEL), f32),
        "ada_w": n(ks[2], (DEPTH, D_MODEL, N_MOD * D_MODEL), f32) * (0.5 * D_MODEL ** -0.5),
        "ada_b": n(ks[3], (DEPTH, N_MOD * D_MODEL), f32) * 0.01,
        "norm_g": 1.0 + 0.05 * n(ks[4], (DEPTH, 6, D_MODEL), f32),
        "ffn_w_in": n(ks[5], (DEPTH, 2, D_MODEL, 2 * D_FF), f32) * D_MODEL ** -0.5,
        "ffn_w_out": n(ks[6], (DEPTH, 2, D_FF, D_MODEL), f32) * D_FF ** -0.5,
        "pool_w": n(ks[7], (N_POOL_LAYERS, N_POOL_GROUPS, POOL_GROUP, POOL_GROUP), f32) * POOL_GROUP ** -0.5,
        "pool_b": n(ks[8], (N_POOL_LAYERS, N_POOL_GROUPS, POOL_GROUP), f32) * 0.01,
        "pool_scale": 1.0 + 0.05 * n(ks[9], (N_POOL_LAYERS, D_MODEL), f32),
        "mla_w_in": n(ks[10], (N_MLA_LAYERS, D_MODEL, Q_LORA + KV_LORA + QK_ROPE), f32) * D_MODEL ** -0.5,
        "mla_q_norm": 1.0 + 0.05 * n(ks[11], (N_MLA_LAYERS, Q_LORA), f32),
        "mla_kv_norm": 1.0 + 0.05 * n(ks[12], (N_MLA_LAYERS, KV_LORA), f32),
        "mla_w_uq": n(ks[13], (N_MLA_LAYERS, Q_LORA, N_HEADS, QK_NOPE + QK_ROPE), f32) * Q_LORA ** -0.5,
        "mla_w_uk": n(ks[14], (N_MLA_LAYERS, KV_LORA, N_HEADS, QK_NOPE), f32) * KV_LORA ** -0.5,
        "mla_w_uv": n(ks[15], (N_MLA_LAYERS, KV_LORA, N_HEADS, V_HEAD), f32) * KV_LORA ** -0.5,
        "mla_w_o": n(ks[16], (N_MLA_LAYERS, N_HEADS * V_HEAD, D_MODEL), f32) * (N_HEADS * V_HEAD) ** -0.5,
    }

def first_block(x, c, ada_w, ada_b, norm_g, ffn_w_in, ffn_w_out, pool_w, pool_b, pool_scale,
              mla_w_in, mla_q_norm, mla_kv_norm, mla_w_uq, mla_w_uk, mla_w_uv, mla_w_o):
    B = x.shape[0]
    cos, sin = rope_tables(x.shape[1], x.dtype)
    sc = jax.nn.silu(c)
    for i in range(DEPTH):
        mod = (sc @ ada_w[i] + ada_b[i]).reshape(B, N_MOD, D_MODEL)[:, :, None, :]
        g = norm_g[i]
        x = modulated_sublayer(x, mod[:, 0:3], g[0], g[1],
                               lambda h: swiglu(h, ffn_w_in[i, 0], ffn_w_out[i, 0]), 0.5)
        if i % N_MIXERS == 0:
            li = i // N_MIXERS
            mixer = lambda h: pool_mixer(h, pool_w[li], pool_b[li], pool_scale[li])
        else:
            li = i // N_MIXERS
            mixer = lambda h: mla_mixer(h, mla_w_in[li], mla_q_norm[li], mla_kv_norm[li],
                                        mla_w_uq[li], mla_w_uk[li], mla_w_uv[li], mla_w_o[li],
                                        cos, sin)
        x = modulated_sublayer(x, mod[:, 3:6], g[2], g[3], mixer, 1.0)
        x = modulated_sublayer(x, mod[:, 6:9], g[4], g[5],
                               lambda h: swiglu(h, ffn_w_in[i, 1], ffn_w_out[i, 1]), 0.5)
    return x


HEAD_DIM = 64
SB_HEADS = 8
SB_WIDTH = SB_HEADS * HEAD_DIM
NSA_HEADS = 8
NSA_KV_HEADS = 2
NSA_GROUP = NSA_HEADS // NSA_KV_HEADS
NSA_WIDTH = NSA_HEADS * HEAD_DIM
NSA_KV_WIDTH = NSA_KV_HEADS * HEAD_DIM
NSA_BRANCHES = 3
CMP_LEN = 32
CMP_STRIDE = 16
CMP_HIDDEN = 256
SEL_BLOCK = 64
SEL_TOP_N = 8
WINDOW = 512
NORM_EPS = 1e-6
FORCED_BONUS = 1e4
NEG_INF = -1e30

IN_SPLITS = (SB_WIDTH, SB_WIDTH, SB_WIDTH, SB_WIDTH,
             NSA_WIDTH,
             NSA_KV_WIDTH, NSA_KV_WIDTH,
             NSA_KV_WIDTH, NSA_KV_WIDTH,
             NSA_KV_WIDTH, NSA_KV_WIDTH,
             NSA_BRANCHES * NSA_HEADS,
             NSA_WIDTH,
             D_MODEL, D_MODEL)
N_IN = 4 * SB_WIDTH + NSA_WIDTH + 6 * NSA_KV_WIDTH + NSA_BRANCHES * NSA_HEADS + NSA_WIDTH + 2 * D_MODEL


def rms_norm(x, g):
    xf = x.astype(jnp.float32)
    y = xf * lax.rsqrt(jnp.mean(xf * xf, axis=-1, keepdims=True) + NORM_EPS)
    return (y * g.astype(jnp.float32)).astype(x.dtype)

def rope(x, pos):
    half = HEAD_DIM // 2
    inv_freq = ROPE_THETA ** (-jnp.arange(half, dtype=jnp.float32) / half)
    ang = pos.astype(jnp.float32)[:, None, :, None] * inv_freq
    cos, sin = jnp.cos(ang), jnp.sin(ang)
    xf = x.astype(jnp.float32)
    x1, x2 = xf[..., :half], xf[..., half:]
    return jnp.concatenate([x1 * cos - x2 * sin, x2 * cos + x1 * sin], axis=-1).astype(x.dtype)

def split_heads(t, n):
    b, l, _ = t.shape
    return t.reshape(b, l, n, HEAD_DIM).transpose(0, 2, 1, 3)

def merge_heads(t):
    b, n, l, d = t.shape
    return t.transpose(0, 2, 1, 3).reshape(b, l, n * d)

def masked_softmax(s, mask):
    return jax.nn.softmax(jnp.where(mask, s.astype(jnp.float32), NEG_INF), axis=-1)

def stick_breaking_attention(q, k, v):
    s_len = q.shape[2]
    scale = HEAD_DIM ** -0.5
    outs = []
    for i in range(s_len // Q_BLOCK):
        end = (i + 1) * Q_BLOCK
        qb = q[:, :, i * Q_BLOCK:end]
        kb, vb = k[:, :, :end], v[:, :, :end]
        z = jnp.einsum('bhqd,bhkd->bhqk', qb, kb).astype(jnp.float32) * scale
        t = i * Q_BLOCK + jnp.arange(Q_BLOCK)
        s = jnp.arange(end)
        mask = s[None, :] < t[:, None]
        log_1m = jnp.where(mask, jax.nn.log_sigmoid(-z), 0.0)
        between = lax.cumsum(log_1m, axis=3, reverse=True) - log_1m
        w = jnp.where(mask, jnp.exp(jax.nn.log_sigmoid(z) + between), 0.0)
        outs.append(jnp.einsum('bhqk,bhkd->bhqd', w.astype(vb.dtype), vb))
    return jnp.concatenate(outs, axis=2)

def compress_blocks(x, idx, pe, w1, b1, w2):
    blocks = x[:, :, idx] + pe
    flat = blocks.reshape(blocks.shape[:3] + (CMP_LEN * HEAD_DIM,))
    return jax.nn.silu(flat @ w1 + b1) @ w2

def nsa_attention(q, k_cmp, v_cmp, k_slc, v_slc, k_win, v_win, branch_gate, pos,
                  k_cmp_norm_g, cmp_pe, cmp_w1, cmp_b1, cmp_w2):
    b, _, s_len, _ = q.shape
    g_n, r_n = NSA_KV_HEADS, NSA_GROUP
    scale = HEAD_DIM ** -0.5
    t = jnp.arange(s_len)
    qg = q.reshape(b, g_n, r_n, s_len, HEAD_DIM)

    n_cmp = (s_len - CMP_LEN) // CMP_STRIDE + 1
    cmp_start = jnp.arange(n_cmp) * CMP_STRIDE
    idx = cmp_start[:, None] + jnp.arange(CMP_LEN)[None, :]
    kc = compress_blocks(k_cmp, idx, cmp_pe[0], cmp_w1[0], cmp_b1[0], cmp_w2[0])
    vc = compress_blocks(v_cmp, idx, cmp_pe[1], cmp_w1[1], cmp_b1[1], cmp_w2[1])
    kc = rope(rms_norm(kc, k_cmp_norm_g), jnp.mean(pos[:, idx].astype(jnp.float32), axis=-1))
    s_cmp = jnp.einsum('bgrqd,bgcd->bgrqc', qg, kc) * scale
    mask_c = (cmp_start + CMP_LEN - 1)[None, :] <= t[:, None]
    p_cmp = masked_softmax(s_cmp, mask_c) * jnp.any(mask_c, axis=-1)[:, None]
    o_cmp = jnp.einsum('bgrqc,bgcd->bgrqd', p_cmp.astype(vc.dtype), vc)

    n_sel = s_len // SEL_BLOCK
    top_n = min(SEL_TOP_N, n_sel)
    sel_start = jnp.arange(n_sel) * SEL_BLOCK
    overlap = ((cmp_start[:, None] < sel_start[None, :] + SEL_BLOCK)
               & (cmp_start[:, None] + CMP_LEN > sel_start[None, :])).astype(jnp.float32)
    imp = jnp.einsum('bgrqc,cj->bgqj', p_cmp, overlap)
    cur = t // SEL_BLOCK
    j = jnp.arange(n_sel)
    forced = (j[None, :] == 0) | (j[None, :] == cur[:, None]) | (j[None, :] == cur[:, None] - 1)
    imp = jnp.where(sel_start[None, :] <= t[:, None],
                    imp + jnp.where(forced, FORCED_BONUS, 0.0), NEG_INF)
    _, sel_idx = lax.top_k(imp, top_n)

    nb = s_len // Q_BLOCK
    q_blocks = qg.reshape(b, g_n, r_n, nb, Q_BLOCK, HEAD_DIM).transpose(3, 0, 1, 2, 4, 5)
    idx_blocks = sel_idx.reshape(b, g_n, nb, Q_BLOCK, top_n).transpose(2, 0, 1, 3, 4)
    pad = ((0, 0), (0, 0), (WINDOW, 0), (0, 0))
    kw_pad, vw_pad = jnp.pad(k_win, pad), jnp.pad(v_win, pad)
    gather = jax.vmap(jax.vmap(lambda arr, ii: arr[ii]))
    n_keys = top_n * SEL_BLOCK

    def block_step(args):
        qb, ib, i = args
        tq = i * Q_BLOCK + jnp.arange(Q_BLOCK)
        tok = (ib[..., None] * SEL_BLOCK + jnp.arange(SEL_BLOCK)).reshape(b, g_n, Q_BLOCK * n_keys)
        ks = gather(k_slc, tok).reshape(b, g_n, Q_BLOCK, n_keys, HEAD_DIM)
        vs = gather(v_slc, tok).reshape(b, g_n, Q_BLOCK, n_keys, HEAD_DIM)
        tok = tok.reshape(b, g_n, Q_BLOCK, n_keys)
        ss = jnp.einsum('bgrqd,bgqkd->bgrqk', qb, ks) * scale
        ps = masked_softmax(ss, (tok <= tq[:, None])[:, :, None])
        o_s = jnp.einsum('bgrqk,bgqkd->bgrqd', ps.astype(vs.dtype), vs)
        kw = lax.dynamic_slice_in_dim(kw_pad, i * Q_BLOCK, WINDOW + Q_BLOCK, axis=2)
        vw = lax.dynamic_slice_in_dim(vw_pad, i * Q_BLOCK, WINDOW + Q_BLOCK, axis=2)
        p = i * Q_BLOCK - WINDOW + jnp.arange(WINDOW + Q_BLOCK)
        mw = (p[None, :] <= tq[:, None]) & (p[None, :] > tq[:, None] - WINDOW) & (p[None, :] >= 0)
        sw = jnp.einsum('bgrqd,bgkd->bgrqk', qb, kw) * scale
        pw = masked_softmax(sw, mw)
        o_w = jnp.einsum('bgrqk,bgkd->bgrqd', pw.astype(vw.dtype), vw)
        return o_s, o_w

    o_slc, o_win = lax.map(block_step, (q_blocks, idx_blocks, jnp.arange(nb)))
    o_slc = o_slc.transpose(1, 2, 3, 0, 4, 5).reshape(b, g_n, r_n, s_len, HEAD_DIM)
    o_win = o_win.transpose(1, 2, 3, 0, 4, 5).reshape(b, g_n, r_n, s_len, HEAD_DIM)

    gates = jax.nn.sigmoid(branch_gate.astype(jnp.float32)).reshape(b, s_len, NSA_BRANCHES, g_n, r_n)
    gates = gates.transpose(2, 0, 3, 4, 1)[..., None]
    o = gates[0] * o_cmp + gates[1] * o_slc + gates[2] * o_win
    return o.transpose(0, 3, 1, 2, 4).reshape(b, s_len, NSA_WIDTH)

def hybrid_layer(x, pos, norm_g, w_in, q_norm_g, k_norm_g, cmp_pe, cmp_w1, cmp_b1, cmp_w2,
                 w_up_a, w_up_b, w_out):
    h = rms_norm(x, norm_g)
    proj = h @ w_in
    (sb_q, sb_k, sb_v, sb_z, n_q, n_kc, n_vc, n_ks, n_vs, n_kw, n_vw,
     n_gate, n_z, gate_a, gate_b) = jnp.split(proj, list(np.cumsum(IN_SPLITS)[:-1]), axis=-1)

    o_a = stick_breaking_attention(split_heads(sb_q, SB_HEADS), split_heads(sb_k, SB_HEADS),
                                   split_heads(sb_v, SB_HEADS))
    y_a = merge_heads(o_a) * jax.nn.silu(sb_z)

    q = rope(rms_norm(split_heads(n_q, NSA_HEADS), q_norm_g), pos)
    k_slc = rope(rms_norm(split_heads(n_ks, NSA_KV_HEADS), k_norm_g[1]), pos)
    k_win = rope(rms_norm(split_heads(n_kw, NSA_KV_HEADS), k_norm_g[2]), pos)
    o_b = nsa_attention(q, split_heads(n_kc, NSA_KV_HEADS), split_heads(n_vc, NSA_KV_HEADS),
                        k_slc, split_heads(n_vs, NSA_KV_HEADS),
                        k_win, split_heads(n_vw, NSA_KV_HEADS),
                        n_gate, pos, k_norm_g[0], cmp_pe, cmp_w1, cmp_b1, cmp_w2)
    y_b = o_b * jax.nn.silu(n_z)

    merged = jax.nn.sigmoid(gate_a) * (y_a @ w_up_a) + jax.nn.sigmoid(gate_b) * (y_b @ w_up_b)
    return (x + merged @ w_out).astype(x.dtype)

def second_inputs(seed: int = 0) -> dict:
    key = jax.random.key(seed)
    ks = jax.random.split(key, 14)
    f32 = jnp.float32
    x = jax.random.normal(ks[0], (BATCH, SEQ, D_MODEL), f32)
    offsets = jax.random.randint(ks[1], (BATCH, 1), 0, SEQ, dtype=jnp.int32)
    positions = (jnp.arange(SEQ, dtype=jnp.int32)[None, :] + offsets).astype(jnp.int32)
    norm_g = 1.0 + 0.02 * jax.random.normal(ks[2], (DEPTH, D_MODEL), f32)
    w_in = jax.random.normal(ks[3], (DEPTH, D_MODEL, N_IN), f32) * D_MODEL ** -0.5
    q_norm_g = 1.0 + 0.02 * jax.random.normal(ks[4], (DEPTH, HEAD_DIM), f32)
    k_norm_g = 1.0 + 0.02 * jax.random.normal(ks[5], (DEPTH, NSA_BRANCHES, HEAD_DIM), f32)
    cmp_pe = 0.1 * jax.random.normal(ks[6], (DEPTH, 2, CMP_LEN, HEAD_DIM), f32)
    cmp_w1 = jax.random.normal(ks[7], (DEPTH, 2, CMP_LEN * HEAD_DIM, CMP_HIDDEN), f32) * (CMP_LEN * HEAD_DIM) ** -0.5
    cmp_b1 = 0.01 * jax.random.normal(ks[8], (DEPTH, 2, CMP_HIDDEN), f32)
    cmp_w2 = jax.random.normal(ks[9], (DEPTH, 2, CMP_HIDDEN, HEAD_DIM), f32) * CMP_HIDDEN ** -0.5
    w_up_a = jax.random.normal(ks[10], (DEPTH, SB_WIDTH, D_MODEL), f32) * SB_WIDTH ** -0.5
    w_up_b = jax.random.normal(ks[11], (DEPTH, NSA_WIDTH, D_MODEL), f32) * NSA_WIDTH ** -0.5
    w_out = jax.random.normal(ks[12], (DEPTH, D_MODEL, D_MODEL), f32) * D_MODEL ** -0.5
    return {'x': x, 'positions': positions, 'norm_g': norm_g, 'w_in': w_in,
            'q_norm_g': q_norm_g, 'k_norm_g': k_norm_g, 'cmp_pe': cmp_pe,
            'cmp_w1': cmp_w1, 'cmp_b1': cmp_b1, 'cmp_w2': cmp_w2,
            'w_up_a': w_up_a, 'w_up_b': w_up_b, 'w_out': w_out}

def second_block(x, positions, norm_g, w_in, q_norm_g, k_norm_g, cmp_pe, cmp_w1, cmp_b1, cmp_w2,
              w_up_a, w_up_b, w_out):
    for layer in range(DEPTH):
        x = hybrid_layer(x, positions, norm_g[layer], w_in[layer], q_norm_g[layer], k_norm_g[layer],
                         cmp_pe[layer], cmp_w1[layer], cmp_b1[layer], cmp_w2[layer],
                         w_up_a[layer], w_up_b[layer], w_out[layer])
    return x


def setup_inputs(seed=0):
    out = dict(first_inputs(seed))
    for name, value in second_inputs(seed + 1).items():
        if name != "x":
            out[name + "_2"] = value
    return out


def reference(
    x, c, ada_w, ada_b, norm_g, ffn_w_in, ffn_w_out, pool_w, pool_b, pool_scale, mla_w_in,
    mla_q_norm, mla_kv_norm, mla_w_uq, mla_w_uk, mla_w_uv, mla_w_o, positions_2, norm_g_2,
    w_in_2, q_norm_g_2, k_norm_g_2, cmp_pe_2, cmp_w1_2, cmp_b1_2, cmp_w2_2, w_up_a_2, w_up_b_2,
    w_out_2,
):
    x = first_block(
        x, c, ada_w, ada_b, norm_g, ffn_w_in, ffn_w_out, pool_w, pool_b, pool_scale, mla_w_in,
        mla_q_norm, mla_kv_norm, mla_w_uq, mla_w_uk, mla_w_uv, mla_w_o,
    )
    return second_block(
        x, positions_2, norm_g_2, w_in_2, q_norm_g_2, k_norm_g_2, cmp_pe_2, cmp_w1_2, cmp_b1_2,
        cmp_w2_2, w_up_a_2, w_up_b_2, w_out_2,
    )


_drawn_inputs = setup_inputs


def setup_inputs(seed=0):
    import zlib

    import numpy as np

    out = dict(_drawn_inputs(seed))
    spreads = {}
    factors = {'pool_b': 3.956,
     'mla_q_norm': 6.183,
     'norm_g_2': 8.0,
     'q_norm_g_2': 8.0,
     'k_norm_g_2': 8.0,
     'cmp_pe_2': 8.0,
     'cmp_b1_2': 8.0}
    for name, (base, spread) in spreads.items():
        noise = np.random.default_rng([zlib.crc32(name.encode()), seed]).standard_normal(out[name].shape)
        drawn = base * np.exp(spread * noise) if base else spread * noise
        out[name] = __import__('jax').numpy.asarray(drawn.astype(out[name].dtype))
    for name, factor in factors.items():
        out[name] = (out[name] * factor).astype(out[name].dtype)
    return out
```

```python
from contextlib import ExitStack
import numpy as np

import concourse.bass as bass
from concourse import mybir

ALU = mybir.AluOpType
ACT = mybir.ActivationFunctionType
AXX = mybir.AxisListType.X
F32 = mybir.dt.float32
F32R = mybir.dt.float32r
I32 = mybir.dt.int32

P = 128
D = 1024
S = 512
NC = D // P
FF = 2816
NF = FF // P
UNIT = NC * P
RAW, RING, LEAD = 2, 4, 2
HEADS = 16
EPS = 1e-6
ATTN_SCALE = 96 ** -0.5
NEG = -1e30
NCMP = 31
NAT2 = 280


class Signal:

    def __init__(self, sem):
        self.sem, self.values, self.planned, self.given = sem, {}, 0, 0

    def plan(self, *labels):
        for label in labels:
            assert label not in self.values, label
            self.planned += 1
            self.values[label] = self.planned

    def plan_loop(self, label, total):
        self.values[label] = self.planned
        self.planned += total

    def at(self, label):
        return self.values[label]

    def give(self, instruction, label):
        self.given += 1
        assert self.values[label] == self.given, (label, self.values[label], self.given)
        instruction.then_inc(self.sem, 1)

    def give_loop(self, label, total):
        assert self.values[label] == self.given, label
        self.given += total


class Chain:

    def __init__(self, engine, sem):
        self.engine, self.sem, self.base, self.n, self.i, self.per = engine, sem, 0, 0, None, 0

    def link(self, instruction):
        instruction.then_inc(self.sem, 1)
        self.n += 1

    def sync(self):
        value = self.base + self.n
        if self.i is not None:
            value = self.i * self.per + value
        self.engine.wait_ge(self.sem, value)

    def step(self, instruction):
        self.link(instruction)
        self.sync()

    def enter(self, i, per):
        self.base, self.n, self.i, self.per = self.base + self.n, 0, i, per

    def leave(self, times):
        assert self.n == self.per, (self.n, self.per)
        self.base, self.n, self.i = self.base + times * self.per, 0, None


class Columns:

    def __init__(self):
        self.at, self.n = {}, 0

    def add(self, name, n):
        self.at[name] = self.n
        self.n += n


def param_columns():
    c = Columns()
    for name, n in (("c", 8), ("ada_b", 144), ("norm_g", 96), ("pool_b", 8), ("pool_scale", 8),
                    ("q_norm", 2), ("kv_norm", 1), ("norm_g_2", 16), ("q_norm_2", 2),
                    ("k_norm_2", 6), ("cmp_b1", 8), ("cmp_pe", 64)):
        c.add(name, n)
    return c


IDENT, ONES, ONES64, PERM32, PERM64 = range(5)
NCONST = 5
R_IDENT, R_CAUSAL, R_STRICT_T, R_NEGTRI, R_NEGONES, R_NEG31 = range(6)
NCONSTR = 6


def kernel_program(nc, stream, ada, xT, params, consts, constsr, pool_count, mla_rope, rope_cst,
                   pos, w2, out, NU):
    col = param_columns()
    with ExitStack() as ctx:
        top = [(nc.sbuf_base + 63) // 64 * 64]

        def at(name, shape, dt=F32):
            size = 4 * int(np.prod(shape[1:]))
            made = nc.alloc_sbuf_tensor_at(name, shape, dt, offset=top[0])
            top[0] += (size + 31) // 32 * 32
            return made

        X = at("X", [P, NC, S])
        raw = at("raw", [P, RAW, UNIT])
        w_hi = at("w_hi", [P, RING, UNIT], F32R)
        w_lo = at("w_lo", [P, RING, UNIT], F32R)
        sq = at("sq", [P, 2, S])
        std = at("std", [P, S])
        rstd = at("rstd", [P, S])
        ta = at("ta", [P, 2, S])
        tb = at("tb", [P, 2, S])
        par = at("par", [P, col.n])
        mod_base = top[0]
        mod = at("mod", [P, 18, NC])
        acol = at("acol", [P, NC])
        bcol = at("bcol", [P, NC])
        silu_c = at("silu_c", [P, NC])
        eps = at("eps", [P, 8])
        small = at("small", [P, 4, 4])
        ones = at("ones", [P, P])
        h_base = top[0]
        h_hi = at("h_hi", [P, NC, S], F32R)
        h_lo = at("h_lo", [P, NC, S], F32R)
        region = top[0]
        top[0] = h_base
        y_ffn = at("y_ffn", [P, NC, S])
        top[0] = h_base
        pt2_hi = at("pt2_hi", [P, 2, 4, S], F32R)
        pt2_lo = at("pt2_lo", [P, 2, 4, S], F32R)
        top[0] = region
        a_hi = at("a_hi", [P, NF, S], F32R)
        a_lo = at("a_lo", [P, NF, S], F32R)
        ada_raw = at("ada_raw", [P, 2, D])
        ada_acc = at("ada_acc", [P, D])
        top[0] = region
        hp = at("hp", [P, 2, S + 16])
        win = at("win", [P, 2, S + 16])
        y_pool = at("y_pool", [P, NC, S])
        cnt = at("cnt", [P, 4, S])

        psum = ctx.enter_context(nc.psum_tensor("psum", [P, 8, S], F32))

        def sem(name):
            return ctx.enter_context(nc.semaphore(name))

        raw_loaded = [sem("raw_loaded%d" % i) for i in range(RAW)]
        ada_loaded = [sem("ada_loaded%d" % i) for i in range(2)]
        small_loaded = sem("small_loaded")
        stage_loaded = sem("stage_loaded")
        hi_ready, lo_ready = sem("hi_ready"), sem("lo_ready")
        ada_used, ada_sum, mod_ready = sem("ada_used"), sem("ada_sum"), sem("mod_ready")
        stored = sem("stored")
        act_own, dve_own = sem("act_own"), sem("dve_own")
        prod = Signal(sem("products"))
        evac = Signal(sem("evacuated"))
        evac_hi = Signal(sem("evacuated_hi"))
        sq_ready = Signal(sem("squares"))
        sums = Signal(sem("sums"))
        ysum = Signal(sem("square_sums"))
        std_ready = Signal(sem("std_ready"))
        rstd_ready = Signal(sem("rstd_ready"))
        x_ready = Signal(sem("x_ready"))
        scaled = Signal(sem("scaled"))
        part_hi = Signal(sem("part_hi"))
        h_ready = Signal(sem("h_ready"))
        value = Signal(sem("values"))

        ysum.plan("start")
        own = {}

        def bank(g):
            return psum[:, g % 4]

        class Cursor:
            u, g, last_norm = 0, 4, None

        cur = Cursor()
        evac.plan(*[("g", g) for g in range(4)])

        def plan_unit(*groups):
            prod.plan(("u", cur.u))
            for g in groups:
                prod.values[("g", g)] = prod.planned
            cur.u += 1

        def plan_norm(L, n):
            for c in range(n):
                sq_ready.plan((L, c))
                sums.plan((L, c))
            own[L, "before"] = cur.last_norm
            cur.last_norm = L
            std_ready.plan(L)
            rstd_ready.plan(L)

        def plan_ynorm(L):
            ysum.plan((L, "zero"))
            sq_ready.plan_loop(L, NC)
            ysum.plan_loop(L, NC)
            sums.plan(L)
            own[L, "before"] = cur.last_norm
            cur.last_norm = L
            std_ready.plan(L)
            rstd_ready.plan(L)

        def plan_pre(L, split=True):
            plan_norm((L, "pre"), NC)
            if split:
                for c in range(NC):
                    scaled.plan((L, c))
                    part_hi.plan((L, c))
                    h_ready.plan((L, c))

        def plan_post(L):
            for c in range(NC):
                x_ready.plan((L, c))

        def plan_ffn(L):
            own[L, "u"], own[L, "g"] = cur.u, cur.g
            plan_pre(L)
            for k in range(2 * NF):
                prod.values[("u", cur.u + k)] = prod.values[("g", cur.g + k)] = prod.planned + k + 1
            prod.plan_loop((L, "gate_up"), 2 * NF)
            for k in range(2 * NF):
                evac.values[("g", cur.g + k)] = evac.planned + k + 1
            evac.plan_loop((L, "gate_up"), 2 * NF)
            value.plan_loop((L, "silu"), NF)
            part_hi.plan_loop((L, "a"), NF)
            cur.u += 2 * NF
            cur.g += 2 * NF
            for k in range(24):
                prod.values[("u", cur.u + k)] = prod.planned + k + 1
            for n in range(NC):
                prod.values[("g", cur.g + n)] = prod.planned + 3 * n + 3
                evac.values[("g", cur.g + n)] = evac.planned + n + 1
            prod.plan_loop((L, "down"), 24)
            evac.plan_loop((L, "down"), NC)
            plan_ynorm((L, "post"))
            cur.u += 24
            cur.g += NC
            plan_post(L)

        def plan_pool(L):
            own[L, "u"], own[L, "g"] = cur.u, cur.g
            plan_pre(L)
            plan_ynorm((L, "post"))
            for c in range(NC):
                if c % 4 == 3:
                    plan_unit(cur.g)
                else:
                    prod.plan(("g", cur.g))
                evac.plan(("g", cur.g))
                cur.g += 1
            plan_post(L)

        def split_hi(act, u):
            if u >= NU:
                return
            act.wait_ge(raw_loaded[u % RAW], 16 * (u // RAW + 1))
            if u >= RING:
                act.wait_ge(prod.sem, prod.at(("u", u - RING)))
            act.activation(w_hi[:, u % RING], raw[:, u % RAW], ACT.Copy).then_inc(hi_ready, 1)

        def split_lo(dve, u):
            if u >= NU:
                return
            dve.wait_ge(hi_ready, u + 1)
            dve.tensor_tensor(w_lo[:, u % RING], raw[:, u % RAW], w_hi[:, u % RING].bitcast(F32),
                              ALU.subtract).then_inc(lo_ready, 1)

        def split_hi_loop(act, i, per, u, products):
            act.wait_ge(raw_loaded[u % RAW], i * (16 * per // RAW) + 16 * (u // RAW + 1))
            act.wait_ge(prod.sem, products)
            act.activation(w_hi[:, u % RING], raw[:, u % RAW], ACT.Copy).then_inc(hi_ready, 1)

        def split_lo_loop(dve, i, per, u):
            dve.wait_ge(hi_ready, i * per + (u + 1))
            dve.tensor_tensor(w_lo[:, u % RING], raw[:, u % RAW], w_hi[:, u % RING].bitcast(F32),
                              ALU.subtract).then_inc(lo_ready, 1)

        def three_passes(pe, dst, weights, moving, first=True, last=True, skip=False):
            n, total = 0, 3 * len(weights)
            for wi, mi in ((0, 0), (1, 0), (0, 1)):
                for w, m in zip(weights, moving):
                    mm = pe.matmul(dst, w[wi], m[mi], start=(first and n == 0),
                                   stop=(last and n == total - 1), skip_group_check=skip)
                    n += 1
            return mm

        def unit_blocks(u, blocks, width=P):
            s = u % RING
            return [(w_hi[:, s, b * width:(b + 1) * width], w_lo[:, s, b * width:(b + 1) * width])
                    for b in blocks]

        def chunks_of(hi, lo, ks):
            return [(hi[:, k], lo[:, k]) for k in ks]

        def free_bank(pe, g):
            pe.wait_ge(evac.sem, evac.at(("g", g - 4)))

        def dense(pe, u, g):
            pe.wait_ge(lo_ready, u + 1)
            free_bank(pe, g)
            mm = three_passes(pe, bank(g), unit_blocks(u, range(NC)), chunks_of(h_hi, h_lo, range(NC)))
            prod.give(mm, ("u", u))

        def norm_act(act, L, sources, n_of, width=S):
            for c, (src, wait) in enumerate(sources):
                if wait:
                    act.wait_ge(*wait)
                if c >= 2:
                    act.wait_ge(sums.sem, sums.at((L, c - 2)))
                v = sq_ready.at((L, c))
                sq_ready.give(act.activation(sq[:, v % 2, :width], src, ACT.Square), (L, c))
            act.wait_ge(sums.sem, sums.at((L, len(sources) - 1)))
            root_act(act, L, n_of, width)

        def root_act(act, L, n_of, width=S):
            if own[L, "before"] is not None:
                act.wait_ge(rstd_ready.sem, rstd_ready.at(own[L, "before"]))
            std_ready.give(act.activation(std[:, :width], psum[:, 7, :width], ACT.Sqrt,
                                          scale=1.0 / n_of, bias=eps[:, 0:1]), L)

        def norm_pe(pe, L, n, matrix, width=S):
            if own[L, "before"] is not None:
                pe.wait_ge(std_ready.sem, std_ready.at(own[L, "before"]))
            for c in range(n):
                v = sq_ready.at((L, c))
                pe.wait_ge(sq_ready.sem, v)
                sums.give(pe.matmul(psum[:, 7, :width], matrix, sq[:, v % 2, :width],
                                    start=(c == 0), stop=(c == n - 1)), (L, c))

        def norm_dve(dve, L, width=S):
            dve.wait_ge(std_ready.sem, std_ready.at(L))
            rstd_ready.give(dve.reciprocal(rstd[:, :width], std[:, :width]), L)
            dve.wait_ge(rstd_ready.sem, rstd_ready.at(L))

        def ynorm_pe(pe, L):
            pe.wait_ge(ysum.sem, ysum.at(L) + NC)
            pe.wait_ge(std_ready.sem, std_ready.at(own[L, "before"]))
            sums.give(pe.matmul(psum[:, 7], ones[:], std[:], start=True, stop=True), L)

        def pre_act(act, L, before, shift=None, split=True):
            norm_act(act, (L, "pre"), [(X[:, c], (x_ready.sem, x_ready.at((before, c))) if before is not None
                                        else None) for c in range(NC)], D)
            if split:
                for c in range(NC):
                    act.wait_ge(scaled.sem, scaled.at((L, c)))
                    if shift is None:
                        op = act.activation(h_hi[:, c], tb[:, c % 2], ACT.Copy)
                    else:
                        op = act.activation(h_hi[:, c], tb[:, c % 2], ACT.Identity,
                                            bias=mod[:, shift, c:c + 1])
                    part_hi.give(op, (L, c))

        def pre_dve(dve, own_order, L, gains, scale=None, shift=None, split=True):
            if scale is not None:
                dve.wait_ge(mod_ready, scale + 1)
                own_order.step(dve.scalar_tensor_tensor(out=acol[:], in0=mod[:, scale], scalar=1.0,
                                                        in1=gains, op0=ALU.add, op1=ALU.mult))
                a = acol
            norm_dve(dve, (L, "pre"))

            def scale_chunk(c):
                a = acol[:, c:c + 1] if scale is not None else gains[:, c:c + 1]
                if c >= 2:
                    dve.wait_ge(h_ready.sem, h_ready.at((L, c - 2)))
                scaled.give(dve.scalar_tensor_tensor(out=tb[:, c % 2], in0=X[:, c], scalar=a,
                                                     in1=rstd[:], op0=ALU.mult, op1=ALU.mult), (L, c))
            if split:
                scale_chunk(0)
                for c in range(NC):
                    if c + 1 < NC:
                        scale_chunk(c + 1)
                    dve.wait_ge(part_hi.sem, part_hi.at((L, c)))
                    if shift is None:
                        op = dve.tensor_tensor(h_lo[:, c], tb[:, c % 2], h_hi[:, c].bitcast(F32),
                                               ALU.subtract)
                    else:
                        op = dve.scalar_tensor_tensor(out=h_lo[:, c], in0=tb[:, c % 2],
                                                      scalar=mod[:, shift, c:c + 1],
                                                      in1=h_hi[:, c].bitcast(F32), op0=ALU.add,
                                                      op1=ALU.subtract)
                    h_ready.give(op, (L, c))

        def post_act(act, L):
            act.wait_ge(sums.sem, sums.at((L, "post")))
            root_act(act, (L, "post"), D)

        def post_dve(dve, own_order, L, y, gains, gate, weight):
            dve.wait_ge(mod_ready, gate + 1)
            own_order.step(dve.scalar_tensor_tensor(out=bcol[:], in0=mod[:, gate], scalar=1.0,
                                                    in1=gains, op0=ALU.add, op1=ALU.mult))
            norm_dve(dve, (L, "post"))

            def scale_chunk(c):
                if c >= 2:
                    dve.wait_ge(x_ready.sem, x_ready.at((L, c - 2)))
                own_order.link(dve.scalar_tensor_tensor(out=ta[:, c % 2], in0=y[:, c],
                                                        scalar=bcol[:, c:c + 1], in1=rstd[:],
                                                        op0=ALU.mult, op1=ALU.mult))
            for c in range(NC):
                scale_chunk(c)
                own_order.sync()
                x_ready.give(dve.scalar_tensor_tensor(out=X[:, c], in0=ta[:, c % 2], scalar=weight,
                                                      in1=X[:, c], op0=ALU.mult, op1=ALU.add), (L, c))

        def ada_piece(dve, j, i, k):
            t = 8 * j + k
            if i is None:
                dve.wait_ge(ada_loaded[k % 2], 16 * (t // 2 + 1))
                if t:
                    dve.wait_ge(ada_used, t)
            else:
                dve.wait_ge(ada_loaded[k % 2], i * 64 + 16 * (t // 2 + 1))
                dve.wait_ge(ada_used, i * 8 + t)
            if k == 0:
                op = dve.tensor_scalar(ada_acc[:], ada_raw[:, 0], silu_c[:, 0:1], None, ALU.mult)
            else:
                op = dve.scalar_tensor_tensor(out=ada_acc[:], in0=ada_raw[:, k % 2],
                                              scalar=silu_c[:, k:k + 1], in1=ada_acc[:],
                                              op0=ALU.mult, op1=ALU.add)
            op.then_inc(ada_used, 1)

        def ada_close_pe(pe, j, i):
            if i is None:
                pe.wait_ge(ada_used, 8 * j + 8)
                if j:
                    pe.wait_ge(mod_ready, j)
            else:
                pe.wait_ge(ada_used, i * 8 + (8 * j + 8))
                pe.wait_ge(mod_ready, i + j)
            for n in range(NC):
                mm = pe.matmul(psum[:, 6, n:n + 1], ada_acc[:, n * P:(n + 1) * P], ones[:, 0:1],
                               start=True, stop=True)
                if n == 0 and i is None:
                    prod.give(mm, "start%d" % j)
            mm.then_inc(ada_sum, 1)

        def ada_close_dve(dve, j, i):
            b = col.at["ada_b"]
            if i is None:
                dve.wait_ge(ada_sum, j + 1)
                dve.tensor_tensor(mod[:, j], psum[:, 6, 0:NC], par[:, b + 8 * j:b + 8 * j + 8],
                                  ALU.add).then_inc(mod_ready, 1)
            else:
                dve.wait_ge(ada_sum, i + (j + 1))
                dve.tensor_tensor(mod[:, bass.ds(i + j, 1), :].rearrange("p a n -> p (a n)"),
                                  psum[:, 6, 0:NC], par[:, bass.ds(i * 8 + (b + 8 * j), 8)],
                                  ALU.add).then_inc(mod_ready, 1)

        def ffn_pe(pe, L, segments):
            u0, g0 = own[L, "u"], own[L, "g"]
            norm_pe(pe, (L, "pre"), NC, ones[:])
            pe.wait_ge(h_ready.sem, h_ready.at((L, NC - 1)))
            b = 0
            for times, j in segments:
                with pe.Fori(0, times) as i:
                    for k in range(4):
                        pe.wait_ge(lo_ready, i * 4 + (u0 + 4 * b + k + 1))
                        pe.wait_ge(evac.sem, i * 4 + (g0 + 4 * b + k - 4 + 1))
                        three_passes(pe, bank(g0 + k), unit_blocks(u0 + k, range(NC)),
                                     chunks_of(h_hi, h_lo, range(NC))).then_inc(prod.sem, 1)
                    if j is not None:
                        ada_close_pe(pe, j, i)
                b += times
            prod.give_loop((L, "gate_up"), 2 * NF)
            u1, g1 = u0 + 2 * NF, g0 + 2 * NF
            pe.wait_ge(evac.sem, evac.at(("g", g1 - 1)))
            with pe.Fori(0, 2) as i:
                for n in range(4):
                    for m in range(3):
                        ks = range(8 * m, min(8 * m + 8, NF))
                        pe.wait_ge(lo_ready, i * 12 + (u1 + 3 * n + m + 1))
                        if m == 0:
                            pe.wait_ge(evac.sem, i * 4 + (g1 + n - 4 + 1))
                        three_passes(pe, bank(g1 + n), unit_blocks(u1 + 3 * n + m, range(len(ks))),
                                     chunks_of(a_hi, a_lo, ks), first=(m == 0),
                                     last=(m == 2)).then_inc(prod.sem, 1)
            prod.give_loop((L, "down"), 24)
            ynorm_pe(pe, (L, "post"))

        def ffn_act(act, L, before, shift, segments):
            u0, g0 = own[L, "u"], own[L, "g"]
            pre_act(act, L, before, shift)
            base, b = prod.at((L, "gate_up")), 0
            for times, j in segments:
                with act.Fori(0, times) as i:
                    for s in range(2):
                        for m in range(2):
                            k = 2 * s + m
                            split_hi_loop(act, i, 4, u0 + 4 * b + k + LEAD, i * 4 + (base + 4 * b + k - 1))
                        act.wait_ge(prod.sem, i * 4 + (base + 4 * b + 2 * s + 1))
                        act.wait_ge(evac.sem, i * 4 + (g0 + 4 * b + 2 * s - 4 + 1))
                        act.activation(ta[:, s], bank(g0 + 2 * s), ACT.Silu).then_inc(value.sem, 1)
                        act.wait_ge(evac.sem, i * 4 + (g0 + 4 * b + 2 * s + 1))
                        act.activation(a_hi[:, bass.ds(i * 2 + (2 * b + s), 1), :].rearrange("p a n -> p (a n)"),
                                       tb[:, s], ACT.Copy).then_inc(part_hi.sem, 1)
                b += times
            value.give_loop((L, "silu"), NF)
            part_hi.give_loop((L, "a"), NF)
            u1, g1, base = u0 + 2 * NF, g0 + 2 * NF, prod.at((L, "down"))
            q0, y0 = sq_ready.at((L, "post")), ysum.at((L, "post"))
            with act.Fori(0, 2) as i:
                for n in range(4):
                    for m in range(3):
                        k = 3 * n + m
                        split_hi_loop(act, i, 12, u1 + k + LEAD, i * 12 + (base + k - 1))
                    act.wait_ge(evac.sem, i * 4 + (g1 + n + 1))
                    act.wait_ge(ysum.sem, i * 4 + (y0 + n - 1))
                    act.activation(sq[:, (q0 + n) % 2],
                                   y_ffn[:, bass.ds(i * 4 + n, 1), :].rearrange("p a n -> p (a n)"),
                                   ACT.Square).then_inc(sq_ready.sem, 1)
            sq_ready.give_loop((L, "post"), NC)
            post_act(act, L)

        def ffn_dve(dve, own_order, L, gains, mods, segments):
            u0, g0 = own[L, "u"], own[L, "g"]
            pre_dve(dve, own_order, L, gains(0), scale=mods + 1, shift=mods)
            base, b = prod.at((L, "gate_up")), 0
            v0, p0 = value.at((L, "silu")), part_hi.at((L, "a"))
            for times, j in segments:
                with dve.Fori(0, times) as i:
                    for s in range(2):
                        for m in range(2):
                            split_lo_loop(dve, i, 4, u0 + 4 * b + 2 * s + m + LEAD)
                        if j is not None:
                            for k in range(4):
                                ada_piece(dve, j, i, 4 * s + k)
                        dve.wait_ge(value.sem, i * 2 + (v0 + 2 * b + s + 1))
                        dve.wait_ge(prod.sem, i * 4 + (base + 4 * b + 2 * s + 2))
                        dve.wait_ge(evac.sem, i * 4 + (g0 + 4 * b + 2 * s - 2))
                        dve.tensor_tensor(tb[:, s], ta[:, s], bank(g0 + 2 * s + 1),
                                          ALU.mult).then_inc(evac.sem, 1)
                        dve.wait_ge(part_hi.sem, i * 2 + (p0 + 2 * b + s + 1))
                        f = bass.ds(i * 2 + (2 * b + s), 1)
                        dve.tensor_tensor(a_lo[:, f, :].rearrange("p a n -> p (a n)"), tb[:, s],
                                          a_hi[:, f, :].bitcast(F32).rearrange("p a n -> p (a n)"),
                                          ALU.subtract).then_inc(evac.sem, 1)
                    if j is not None:
                        ada_close_dve(dve, j, i)
                b += times
            evac.give_loop((L, "gate_up"), 2 * NF)
            u1, g1, base = u0 + 2 * NF, g0 + 2 * NF, prod.at((L, "down"))
            q0, y0 = sq_ready.at((L, "post")), ysum.at((L, "post"))
            ysum.give(dve.memset(std[:], 0.0), ((L, "post"), "zero"))
            with dve.Fori(0, 2) as i:
                for n in range(4):
                    for m in range(3):
                        split_lo_loop(dve, i, 12, u1 + 3 * n + m + LEAD)
                    dve.wait_ge(prod.sem, i * 12 + (base + 3 * n + 3))
                    dve.tensor_copy(y_ffn[:, bass.ds(i * 4 + n, 1), :].rearrange("p a n -> p (a n)"),
                                    bank(g1 + n)).then_inc(evac.sem, 1)
                    dve.wait_ge(sq_ready.sem, i * 4 + (q0 + n + 1))
                    dve.wait_ge(ysum.sem, i * 4 + (y0 + n))
                    dve.tensor_tensor(std[:], std[:], sq[:, (q0 + n) % 2], ALU.add).then_inc(ysum.sem, 1)
            evac.give_loop((L, "down"), NC)
            ysum.give_loop((L, "post"), NC)
            post_dve(dve, own_order, L, y_ffn, gains(1), mods + 2, 0.5)

        def pool_pe(pe, L):
            norm_pe(pe, (L, "pre"), NC, ones[:])
            u, g = own[L, "u"], own[L, "g"]
            for c in range(NC):
                group = 2 * (c // 2)
                if c % 4 == 0:
                    pe.wait_ge(lo_ready, u + c // 4 + 1)
                pe.wait_ge(h_ready.sem, h_ready.at((L, group + 1)))
                free_bank(pe, g + c)
                mm = three_passes(pe, bank(g + c), unit_blocks(u + c // 4, (2 * (c % 4), 2 * (c % 4) + 1)),
                                  chunks_of(h_hi, h_lo, (group, group + 1)))
                prod.give(mm, ("u", u + c // 4) if c % 4 == 3 else ("g", g + c))
            ynorm_pe(pe, (L, "post"))

        def pool_act(act, L, before):
            act.wait_ge(x_ready.sem, x_ready.at((before, 0)))
            act.dma_start(cnt[:], pool_count).then_inc(stage_loaded, 16)
            norm_act(act, (L, "pre"), [(X[:, c], (x_ready.sem, x_ready.at((before, c)))) for c in range(NC)], D)
            for c in range(NC):
                act.wait_ge(scaled.sem, scaled.at((L, c)))
                part_hi.give(act.activation(h_hi[:, c], tb[:, c % 2], ACT.Copy), (L, c))
            u, g = own[L, "u"], own[L, "g"]
            split_hi(act, u + 2)
            split_hi(act, u + 3)
            q0, y0 = sq_ready.at((L, "post")), ysum.at((L, "post"))
            for c in range(NC):
                act.wait_ge(evac.sem, evac.at(("g", g + c)))
                if c >= 2:
                    act.wait_ge(ysum.sem, y0 + c - 1)
                act.activation(sq[:, (q0 + c) % 2], y_pool[:, c], ACT.Square).then_inc(sq_ready.sem, 1)
            sq_ready.give_loop((L, "post"), NC)
            post_act(act, L)

        def pool_dve(dve, own_order, L, gains):
            dve.wait_ge(mod_ready, 5)
            own_order.step(dve.scalar_tensor_tensor(out=acol[:], in0=mod[:, 4], scalar=1.0,
                                                    in1=gains(0), op0=ALU.add, op1=ALU.mult))
            own_order.link(dve.memset(hp[:, :, 0:8], 0.0))
            own_order.step(dve.memset(hp[:, :, S + 8:S + 16], 0.0))
            norm_dve(dve, (L, "pre"))
            dve.wait_ge(stage_loaded, 16)
            body = slice(8, S + 8)

            def lo_half(c):
                dve.wait_ge(part_hi.sem, part_hi.at((L, c)))
                h_ready.give(dve.tensor_tensor(h_lo[:, c], tb[:, c % 2], h_hi[:, c].bitcast(F32),
                                               ALU.subtract), (L, c))
            for c in range(NC):
                h = hp[:, c % 2]
                own_order.step(dve.scalar_tensor_tensor(out=ta[:, 0], in0=X[:, c], scalar=acol[:, c:c + 1],
                                                        in1=rstd[:], op0=ALU.mult, op1=ALU.mult))
                own_order.step(dve.tensor_scalar(h[:, body], ta[:, 0], mod[:, 3, c:c + 1], None, ALU.add))
                own_order.step(dve.tensor_tensor(win[:, 0, 1:S + 16], h[:, 0:S + 15], h[:, 1:S + 16], ALU.add))
                have, first, end = 0, 1, S + 16
                for level in range(c // 2):
                    half = 1 << level
                    first, end = first + half, end - half
                    own_order.step(dve.tensor_tensor(win[:, 1 - have, first:end],
                                                     win[:, have, first - half:end - half],
                                                     win[:, have, first + half:end + half], ALU.add))
                    have = 1 - have
                own_order.step(dve.tensor_tensor(ta[:, 1], win[:, have, body], cnt[:, c // 2], ALU.mult))
                scaled.give(dve.tensor_tensor(tb[:, c % 2], ta[:, 1], h[:, body], ALU.subtract), (L, c))
                if c:
                    lo_half(c - 1)
            lo_half(NC - 1)
            u, g = own[L, "u"], own[L, "g"]
            split_lo(dve, u + 2)
            split_lo(dve, u + 3)
            q0, y0 = sq_ready.at((L, "post")), ysum.at((L, "post"))
            ysum.give(dve.memset(std[:], 0.0), ((L, "post"), "zero"))
            b, s = col.at["pool_b"], col.at["pool_scale"]
            for c in range(NC):
                dve.wait_ge(prod.sem, prod.at(("g", g + c)))
                evac.give(dve.tensor_scalar(y_pool[:, c], bank(g + c), par[:, b + c:b + c + 1],
                                            par[:, s + c:s + c + 1], ALU.add, ALU.mult), ("g", g + c))
                dve.wait_ge(sq_ready.sem, q0 + c + 1)
                dve.wait_ge(ysum.sem, y0 + c)
                dve.tensor_tensor(std[:], std[:], sq[:, (q0 + c) % 2], ALU.add).then_inc(ysum.sem, 1)
            ysum.give_loop((L, "post"), NC)
            post_dve(dve, own_order, L, y_pool, gains(1), 5, 1.0)

        def plan_softmax(L, A):
            for k in range(4 * A["tasks"]):
                for signal in (scores, peak, probs, probs_scaled, turned, turned_hi, turned_lo):
                    signal.plan((L, k))

        def softmax_pe(pe, L, A, extra):
            last = 4 * A["tasks"]

            def do_scores(k):
                if k >= last:
                    return
                t, i = divmod(k, 4)
                if k >= 2:
                    pe.wait_ge(probs.sem, probs.at((L, k - 2)))
                scores.give(A["scores"](pe, t, i, psum[:, 4 + k % 2, 0:A["width"](t, i)]), (L, k))

            def turn(k):
                t, i = divmod(k, 4)
                pe.wait_ge(probs_scaled.sem, probs_scaled.at((L, k)))
                if k >= 2:
                    pe.wait_ge(turned_lo.sem, turned_lo.at((L, k - 2)))
                elif A["bank7"] and k == 1:
                    pe.wait_ge(std_ready.sem, std_ready.at(A["bank7"]))
                w = A["width"](t, i)
                n = -(-w // P)
                for b in range(n):
                    m = min(P, w - b * P)
                    mm = pe.transpose(psum[0:m, 6 + k % 2, b * P:b * P + P],
                                      A["p"][:, k % 2, b * P:b * P + m], A["ident"])
                turned.give(mm, (L, k))

            extra(pe, "pe", -1)
            do_scores(0)
            do_scores(1)
            for k in range(last):
                do_scores(k + 2)
                extra(pe, "pe", k, 0)
                turn(k)
                if k % 4 == 1 and k >= 4:
                    values_pe(pe, L, A, k // 4 - 1)
                extra(pe, "pe", k, 1)
            values_pe(pe, L, A, A["tasks"] - 1)
            extra(pe, "pe", last)

        def values_pe(pe, L, A, t):
            g, first, final = A["group"](t)
            pe.wait_ge(turned_lo.sem, turned_lo.at((L, 4 * t + 3)))
            if first:
                free_bank(pe, g)
            slot = t % A["slots"]
            rows = A["rows"](t)
            n = A["blocks"](t)
            count = 0
            for wi, mi in ((0, 0), (1, 0), (0, 1)):
                for j in range(n):
                    q = A["start"](t, j)
                    mm = pe.matmul(bank(g)[:, q:S], A["values"](t, j)[wi],
                                   A["pt"][mi][0:rows, slot, j, q:S], start=(first and count == 0),
                                   stop=(final and count == 3 * n - 1), skip_group_check=True)
                    count += 1
            prod.give(mm, ("pv", L, t))

        def softmax_act(act, L, A, extra):
            last = 4 * A["tasks"]

            def hi(k):
                t, i = divmod(k, 4)
                act.wait_ge(turned.sem, turned.at((L, k)))
                if i == 0 and t >= A["slots"]:
                    act.wait_ge(prod.sem, prod.at(("pv", L, t - A["slots"])))
                rows = A["rows"](t)
                n = -(-A["width"](t, i) // P)
                turned_hi.give(act.activation(
                    A["pt"][0][0:rows, t % A["slots"], 0:n, i * P:(i + 1) * P],
                    psum[0:rows, 6 + k % 2, 0:n * P].rearrange("p (a n) -> p a n", n=P), ACT.Copy), (L, k))
            extra(act, "act", -1)
            for k in range(last):
                t, i = divmod(k, 4)
                w = A["width"](t, i)
                act.wait_ge(peak.sem, peak.at((L, k)))
                if k >= 2:
                    act.wait_ge(turned.sem, turned.at((L, k - 2)))
                probs.give(act.activation(A["p"][:, k % 2, 0:w], psum[:, 4 + k % 2, 0:w], ACT.Exp,
                                          bias=small[:, 1, k % 4:k % 4 + 1], scale=A["scale"],
                                          accum_out=small[:, 2, k % 4:k % 4 + 1]), (L, k))
                extra(act, "act", k, 0)
                if k:
                    hi(k - 1)
                extra(act, "act", k, 1)
            hi(last - 1)
            extra(act, "act", last)

        def softmax_dve(dve, order, L, A, extra):
            last = 4 * A["tasks"]

            def maximum(k):
                if k >= last:
                    return
                t, i = divmod(k, 4)
                dve.wait_ge(scores.sem, scores.at((L, k)))
                m = small[:, 0, k % 4:k % 4 + 1]
                order.step(dve.reduce_max(m, psum[:, 4 + k % 2, 0:A["width"](t, i)], AXX))
                if k >= 4:
                    dve.wait_ge(probs.sem, probs.at((L, k - 4)))
                peak.give(dve.tensor_scalar(small[:, 1, k % 4:k % 4 + 1], m, -A["scale"], None,
                                            ALU.mult), (L, k))

            def scale(k):
                t, i = divmod(k, 4)
                w = A["width"](t, i)
                dve.wait_ge(probs.sem, probs.at((L, k)))
                r = small[:, 3, k % 4:k % 4 + 1]
                order.step(dve.reciprocal(r, small[:, 2, k % 4:k % 4 + 1]))
                g = A["gate"](t, i)
                p = A["p"][:, k % 2, 0:w]
                probs_scaled.give(dve.tensor_scalar(p, p, r, g, ALU.mult, ALU.mult if g is not None
                                                    else ALU.bypass), (L, k))

            def lo(k):
                t, i = divmod(k, 4)
                dve.wait_ge(turned_hi.sem, turned_hi.at((L, k)))
                rows = A["rows"](t)
                n = -(-A["width"](t, i) // P)
                dst = (slice(0, rows), t % A["slots"], slice(0, n), slice(i * P, (i + 1) * P))
                turned_lo.give(dve.tensor_tensor(
                    A["pt"][1][dst], psum[0:rows, 6 + k % 2, 0:n * P].rearrange("p (a n) -> p a n", n=P),
                    A["pt"][0][dst].bitcast(F32), ALU.subtract), (L, k))
            extra(dve, "dve", -1)
            maximum(0)
            for k in range(last):
                maximum(k + 1)
                scale(k)
                extra(dve, "dve", k, 0)
                if k:
                    lo(k - 1)
                extra(dve, "dve", k, 1)
            lo(last - 1)
            extra(dve, "dve", last)

        scores = Signal(sem("scores"))
        peak = Signal(sem("peaks"))
        probs = Signal(sem("probabilities"))
        probs_scaled = Signal(sem("probabilities_scaled"))
        turned = Signal(sem("turned"))
        turned_hi = Signal(sem("turned_hi"))
        turned_lo = Signal(sem("turned_lo"))

        def evac_split_act(act, g, hi, factor=1.0):
            act.wait_ge(prod.sem, prod.at(("g", g)))
            evac_hi.give(act.activation(hi, bank(g), ACT.Copy, scale=factor), g)

        def evac_split_dve(dve, g, hi, lo, factor=1.0):
            dve.wait_ge(evac_hi.sem, evac_hi.at(g))
            evac.give(dve.scalar_tensor_tensor(out=lo, in0=bank(g), scalar=factor, in1=hi.bitcast(F32),
                                               op0=ALU.mult, op1=ALU.subtract), ("g", g))

        top[0] = region
        lat = at("lat", [P, 4, S])
        top[0] = region
        ql_hi = at("ql_hi", [P, 2, S], F32R)
        ql_lo = at("ql_lo", [P, 2, S], F32R)
        cq_hi = at("cq_hi", [P, 2, S], F32R)
        cq_lo = at("cq_lo", [P, 2, S], F32R)
        kv_hi = at("kv_hi", [P, S], F32R)
        kv_lo = at("kv_lo", [P, S], F32R)
        kr_hi = at("kr_hi", [P, S], F32R)
        kr_lo = at("kr_lo", [P, S], F32R)
        v_hi = at("v_hi", [P, 4, P], F32R)
        v_lo = at("v_lo", [P, 4, P], F32R)
        qn_hi = at("qn_hi", [P, 8, S], F32R)
        qn_lo = at("qn_lo", [P, 8, S], F32R)
        qr_hi = at("qr_hi", [P, 4, S], F32R)
        qr_lo = at("qr_lo", [P, 4, S], F32R)
        pm = at("pm", [P, 2, S])
        ol_hi = at("ol_hi", [P, 2, S], F32R)
        ol_lo = at("ol_lo", [P, 2, S], F32R)
        mrope = at("mrope", [P, 2, S])
        mconst = at("mconst", [P, 2, P])
        assert top[0] <= nc.sbuf_usable_end, (top[0], nc.sbuf_usable_end)

        stage_loads = [1]

        def plan_mla(L):
            u, g = cur.u, cur.g
            own[L, "u"], own[L, "g"] = u, g
            plan_pre(L)
            own[L, "loaded"] = 16 * (stage_loads[0] + 3)
            stage_loads[0] += 3
            for k in range(4):
                plan_unit(cur.g)
                evac.plan(("g", cur.g))
                cur.g += 1
            plan_norm((L, "nq"), 2)
            plan_norm((L, "nkv"), 1)
            for c in range(2):
                scaled.plan((L, "cq", c))
                part_hi.plan((L, "cq", c))
                h_ready.plan((L, "cq", c))
            scaled.plan((L, "kv"))
            part_hi.plan((L, "kv"))
            h_ready.plan((L, "kv"))
            sums.plan((L, "turned_kv"), (L, "rot", "k"))
            part_hi.plan((L, "v"))
            h_ready.plan((L, "v"))
            scaled.plan((L, "rot", "k"))
            part_hi.plan((L, "rot", "k"))
            h_ready.plan((L, "rot", "k"))
            for c in range(8):
                if c % 4 == 3:
                    plan_unit(cur.g)
                else:
                    prod.plan(("g", cur.g))
                evac_hi.plan(cur.g)
                evac.plan(("g", cur.g))
                cur.g += 1
            for c in range(4):
                if c == 3:
                    plan_unit(cur.g)
                else:
                    prod.plan(("g", cur.g))
                evac.plan(("g", cur.g))
                cur.g += 1
            for c in range(4):
                sums.plan((L, "rot", c))
                scaled.plan((L, "rot", c))
                part_hi.plan((L, "rot", c))
                h_ready.plan((L, "rot", c))
            events = own[L, "events"] = {}
            uk, uv = cur.u, cur.u + 1

            def group(kind, n, unit_end=None):
                label = cur.g
                if unit_end is not None:
                    prod.plan(("u", unit_end))
                    prod.values[("g", label)] = prod.planned
                else:
                    prod.plan(("g", label))
                if kind == "pv":
                    prod.values[("pv", L, n)] = prod.planned
                if kind != "uv":
                    evac_hi.plan(label)
                else:
                    evac_hi.plan(label)
                evac.plan(("g", label))
                events[kind, n] = label
                cur.g += 1
            group("ql", 0)
            for k in range(4 * HEADS):
                t, i = divmod(k, 4)
                if i == 0 and t + 1 < HEADS:
                    group("ql", t + 1, uk + 2 * ((t + 1) // 8) if (t + 1) % 8 == 7 else None)
                if i == 1 and t >= 1:
                    group("pv", t - 1)
                if i == 3 and t >= 1 and (t - 1) % 2 == 1:
                    p = (t - 1) // 2
                    group("uv", p, uv + 2 * (p // 4) if p % 4 == 3 else None)
            group("pv", HEADS - 1)
            group("uv", HEADS // 2 - 1, uv + 2)
            own[L, "uk"], own[L, "uv"] = uk, uv
            cur.u += 4
            plan_softmax(L, {"tasks": HEADS})
            own[L, "wo"], own[L, "wog"] = cur.u, cur.g
            plan_ynorm((L, "post"))
            for n in range(NC):
                plan_unit(cur.g)
                evac.plan(("g", cur.g))
                cur.g += 1
            plan_post(L)

        def mla_scores(pe, t, i, dst):
            q = slice(i * P, (i + 1) * P)
            r, row = t // 4, 32 * (t % 4)
            if i == 0:
                pe.wait_ge(evac.sem, evac.at(("g", own["mla", "events"]["ql", t])))
            three_passes(pe, dst, [(ql_hi[:, t % 2, q], ql_lo[:, t % 2, q])], [(kv_hi[:], kv_lo[:])],
                         last=False, skip=True)
            rows = slice(row, row + 32)
            return three_passes(pe, dst, [(qr_hi[rows, r, q], qr_lo[rows, r, q])],
                                [(kr_hi[rows, :], kr_lo[rows, :])], first=False, skip=True)

        mla_attention = {
            "tasks": HEADS, "width": lambda t, i: S, "scores": mla_scores, "scale": ATTN_SCALE,
            "gate": lambda t, i: None, "p": pm, "pt": (pt2_hi, pt2_lo), "slots": 2,
            "rows": lambda t: P, "blocks": lambda t: 4, "start": lambda t, j: 0,
            "values": lambda t, j: (v_hi[:, j], v_lo[:, j]), "ident": mconst[:, 0],
            "group": lambda t: (own["mla", "events"]["pv", t], True, True),
            "bank7": ("mla", "nkv"),
        }

        def mla_extra(L):
            def run(eng, who, k, phase=0):
                ev, uk, uv = own[L, "events"], own[L, "uk"], own[L, "uv"]
                todo = []
                if k == -1:
                    todo.append(("ql", 0))
                elif k == 4 * HEADS:
                    if who != "pe":
                        todo.append(("pv", HEADS - 1))
                    todo.append(("uv", HEADS // 2 - 1))
                else:
                    t, i = divmod(k, 4)
                    if phase == 0 and i == 0 and t + 1 < HEADS:
                        todo.append(("ql", t + 1))
                    if phase == 1 and i == 1 and t >= 1 and who != "pe":
                        todo.append(("pv", t - 1))
                    if phase == 1 and i == 3 and t >= 1 and (t - 1) % 2 == 1:
                        todo.append(("uv", (t - 1) // 2))
                for kind, n in todo:
                    g = ev[kind, n]
                    if who == "pe":
                        free_bank(eng, g)
                        if kind == "ql":
                            u = uk + 2 * (n // 8)
                            eng.wait_ge(lo_ready, u + 1)
                            mm = three_passes(eng, bank(g), unit_blocks(u, [n % 8]),
                                              chunks_of(qn_hi, qn_lo, [n // 2]))
                            prod.give(mm, ("g", g) if n % 8 != 7 else ("u", u))
                        else:
                            u = uv + 2 * (n // 4)
                            eng.wait_ge(lo_ready, u + 1)
                            eng.wait_ge(evac.sem, evac.at(("g", ev["pv", 2 * n + 1])))
                            mm = three_passes(eng, bank(g), unit_blocks(u, [2 * (n % 4), 2 * (n % 4) + 1]),
                                              chunks_of(ol_hi, ol_lo, [0, 1]))
                            prod.give(mm, ("g", g) if n % 4 != 3 else ("u", u))
                        continue
                    if kind == "ql":
                        dst = (ql_hi[:, n % 2], ql_lo[:, n % 2])
                        if n >= 2 and who == "act":
                            eng.wait_ge(scores.sem, scores.at((L, 4 * (n - 2) + 3)))
                    elif kind == "pv":
                        dst = (ol_hi[:, n % 2], ol_lo[:, n % 2])
                        if n >= 2 and who == "act":
                            eng.wait_ge(prod.sem, prod.at(("g", ev["uv", n // 2 - 1])))
                    else:
                        dst = (qn_hi[:, n], qn_lo[:, n])
                    if who == "act":
                        evac_split_act(eng, g, dst[0])
                    else:
                        evac_split_dve(eng, g, *dst)
            return run

        def mla_pe(pe, L):
            u, g = own[L, "u"], own[L, "g"]
            norm_pe(pe, (L, "pre"), NC, ones[:])
            pe.wait_ge(h_ready.sem, h_ready.at((L, NC - 1)))
            for k in range(4):
                dense(pe, u + k, g + k)
            norm_pe(pe, (L, "nq"), 2, ones[:])
            norm_pe(pe, (L, "nkv"), 1, ones[:])
            pe.wait_ge(stage_loaded, own[L, "loaded"])
            pe.wait_ge(scaled.sem, scaled.at((L, "kv")))
            for j in range(4):
                mm = pe.transpose(psum[:, 6, j * P:(j + 1) * P], tb[:, 0, j * P:(j + 1) * P], mconst[:, 0])
            sums.give(mm, (L, "turned_kv"))
            sums.give(pe.matmul(psum[:, 5], mconst[:, 1], lat[:, 3], start=True, stop=True), (L, "rot", "k"))
            u, g = u + 4, g + 4
            pe.wait_ge(h_ready.sem, h_ready.at((L, "cq", 1)))
            for c in range(12):
                if c % 4 == 0:
                    pe.wait_ge(lo_ready, u + c // 4 + 1)
                free_bank(pe, g + c)
                mm = three_passes(pe, bank(g + c), unit_blocks(u + c // 4, (2 * (c % 4), 2 * (c % 4) + 1)),
                                  chunks_of(cq_hi, cq_lo, (0, 1)))
                prod.give(mm, ("u", u + c // 4) if c % 4 == 3 else ("g", g + c))
            for r in range(4):
                pe.wait_ge(evac.sem, evac.at(("g", g + 8 + r)))
                if r:
                    pe.wait_ge(scaled.sem, scaled.at((L, "rot", r - 1)))
                else:
                    pe.wait_ge(scaled.sem, scaled.at((L, "rot", "k")))
                sums.give(pe.matmul(psum[:, 5], mconst[:, 1], ta[:, r % 2], start=True, stop=True),
                          (L, "rot", r))
            pe.wait_ge(h_ready.sem, h_ready.at((L, "rot", 3)))
            softmax_pe(pe, L, mla_attention, mla_extra(L))
            u, g = own[L, "wo"], own[L, "wog"]
            pe.wait_ge(evac.sem, evac.at(("g", own[L, "events"]["uv", 7])))
            for n in range(NC):
                pe.wait_ge(lo_ready, u + n + 1)
                free_bank(pe, g + n)
                mm = three_passes(pe, bank(g + n), unit_blocks(u + n, range(NC)),
                                  chunks_of(qn_hi, qn_lo, range(NC)))
                prod.give(mm, ("u", u + n))
            ynorm_pe(pe, (L, "post"))

        def split_value_act(act, label, src, hi):
            act.wait_ge(scaled.sem, scaled.at(label))
            part_hi.give(act.activation(hi, src, ACT.Copy), label)

        def split_value_dve(dve, label, src, hi, lo):
            dve.wait_ge(part_hi.sem, part_hi.at(label))
            h_ready.give(dve.tensor_tensor(lo, src, hi.bitcast(F32), ALU.subtract), label)

        def mla_act(act, order, L, before):
            u, g = own[L, "u"], own[L, "g"]
            act.wait_ge(x_ready.sem, x_ready.at((before, 0)))
            act.dma_start(mrope[:], mla_rope).then_inc(stage_loaded, 16)
            act.dma_start(mconst[:, 0], consts[:, IDENT * P:(IDENT + 1) * P]).then_inc(stage_loaded, 16)
            act.dma_start(mconst[:, 1], consts[:, PERM32 * P:(PERM32 + 1) * P]).then_inc(stage_loaded, 16)
            pre_act(act, L, before, 12)
            for k in range(4):
                split_hi(act, u + k + LEAD)
            norm_act(act, (L, "nq"), [(lat[:, c], (evac.sem, evac.at(("g", g + c)))) for c in range(2)], 256)
            norm_act(act, (L, "nkv"), [(lat[:, 2], (evac.sem, evac.at(("g", g + 2))))], P)
            for c in range(2):
                split_value_act(act, (L, "cq", c), ta[:, c], cq_hi[:, c])
            split_value_act(act, (L, "kv"), tb[:, 0], kv_hi[:])
            act.wait_ge(sums.sem, sums.at((L, "turned_kv")))
            part_hi.give(act.activation(v_hi[:], psum[:, 6].rearrange("p (a n) -> p a n", n=P), ACT.Copy), (L, "v"))
            split_value_act(act, (L, "rot", "k"), tb[:, 1], kr_hi[:])
            u, g = u + 4, g + 4
            split_hi(act, u + 2)
            for c in range(8):
                if c == 4:
                    split_hi(act, u + 3)
                evac_split_act(act, g + c, qn_hi[:, c])
            split_hi(act, u + 4)
            for r in range(4):
                split_value_act(act, (L, "rot", r), tb[:, r % 2], qr_hi[:, r])
            split_hi(act, u + 5)
            split_hi(act, u + 6)
            softmax_act(act, L, mla_attention, mla_extra(L))
            u, g = own[L, "wo"], own[L, "wog"]
            split_hi(act, u)
            split_hi(act, u + 1)
            out_act(act, L, u, g, y_ffn)

        def out_act(act, L, u, g, y):
            q0, y0 = sq_ready.at((L, "post")), ysum.at((L, "post"))
            for n in range(NC):
                split_hi(act, u + n + LEAD)
                act.wait_ge(evac.sem, evac.at(("g", g + n)))
                if n >= 2:
                    act.wait_ge(ysum.sem, y0 + n - 1)
                act.activation(sq[:, (q0 + n) % 2], y[:, n], ACT.Square).then_inc(sq_ready.sem, 1)
            sq_ready.give_loop((L, "post"), NC)
            post_act(act, L)

        def rotate_dve(dve, order, label, src, cos, sin, swapped, dst):
            order.step(dve.tensor_tensor(dst, src, cos, ALU.mult))
            dve.wait_ge(sums.sem, sums.at(label))
            order.step(dve.tensor_tensor(std[:, :dst.shape[1]], swapped, sin, ALU.mult))
            scaled.give(dve.tensor_tensor(dst, dst, std[:, :dst.shape[1]], ALU.add), label)

        def mla_dve(dve, order, L, gains):
            u, g = own[L, "u"], own[L, "g"]
            pre_dve(dve, order, L, gains(0), scale=13, shift=12)
            for k in range(4):
                split_lo(dve, u + k + LEAD)
            for k in range(4):
                dve.wait_ge(prod.sem, prod.at(("g", g + k)))
                evac.give(dve.tensor_copy(lat[:, k], bank(g + k)), ("g", g + k))
            qn, kn = col.at["q_norm"], col.at["kv_norm"]
            norm_dve(dve, (L, "nq"))
            for c in range(2):
                scaled.give(dve.scalar_tensor_tensor(out=ta[:, c], in0=lat[:, c], scalar=par[:, qn + c:qn + c + 1],
                                                     in1=rstd[:], op0=ALU.mult, op1=ALU.mult), (L, "cq", c))
            for c in range(2):
                split_value_dve(dve, (L, "cq", c), ta[:, c], cq_hi[:, c], cq_lo[:, c])
            dve.wait_ge(h_ready.sem, h_ready.at((L, "cq", 1)))
            norm_dve(dve, (L, "nkv"))
            scaled.give(dve.scalar_tensor_tensor(out=tb[:, 0], in0=lat[:, 2], scalar=par[:, kn:kn + 1],
                                                 in1=rstd[:], op0=ALU.mult, op1=ALU.mult), (L, "kv"))
            split_value_dve(dve, (L, "kv"), tb[:, 0], kv_hi[:], kv_lo[:])
            dve.wait_ge(part_hi.sem, part_hi.at((L, "v")))
            h_ready.give(dve.tensor_tensor(v_lo[:], psum[:, 6].rearrange("p (a n) -> p a n", n=P),
                                           v_hi[:].bitcast(F32), ALU.subtract), (L, "v"))
            dve.wait_ge(stage_loaded, own[L, "loaded"])
            rotate_dve(dve, order, (L, "rot", "k"), lat[:, 3], mrope[:, 0], mrope[:, 1], psum[:, 5], tb[:, 1])
            split_value_dve(dve, (L, "rot", "k"), tb[:, 1], kr_hi[:], kr_lo[:])
            u, g = u + 4, g + 4
            split_lo(dve, u + 2)
            for c in range(8):
                if c == 4:
                    split_lo(dve, u + 3)
                evac_split_dve(dve, g + c, qn_hi[:, c], qn_lo[:, c])
            split_lo(dve, u + 4)
            for r in range(4):
                dve.wait_ge(prod.sem, prod.at(("g", g + 8 + r)))
                if r >= 2:
                    dve.wait_ge(scaled.sem, scaled.at((L, "rot", r - 2)))
                evac.give(dve.tensor_copy(ta[:, r % 2], bank(g + 8 + r)), ("g", g + 8 + r))
                dve.wait_ge(evac.sem, evac.at(("g", g + 8 + r)))
                dve.wait_ge(h_ready.sem, h_ready.at((L, "rot", r - 2 if r >= 2 else "k")))
                rotate_dve(dve, order, (L, "rot", r), ta[:, r % 2], mrope[:, 0], mrope[:, 1], psum[:, 5],
                           tb[:, r % 2])
                split_value_dve(dve, (L, "rot", r), tb[:, r % 2], qr_hi[:, r], qr_lo[:, r])
            split_lo(dve, u + 5)
            split_lo(dve, u + 6)
            softmax_dve(dve, order, L, mla_attention, mla_extra(L))
            u, g = own[L, "wo"], own[L, "wog"]
            split_lo(dve, u)
            split_lo(dve, u + 1)
            out_dve(dve, L, u, g, y_ffn)
            post_dve(dve, order, L, y_ffn, gains(1), 14, 1.0)

        def out_dve(dve, L, u, g, y):
            q0, y0 = sq_ready.at((L, "post")), ysum.at((L, "post"))
            ysum.give(dve.memset(std[:], 0.0), ((L, "post"), "zero"))
            for n in range(NC):
                split_lo(dve, u + n + LEAD)
                dve.wait_ge(prod.sem, prod.at(("g", g + n)))
                evac.give(dve.tensor_copy(y[:, n], bank(g + n)), ("g", g + n))
                dve.wait_ge(sq_ready.sem, q0 + n + 1)
                dve.wait_ge(ysum.sem, y0 + n)
                dve.tensor_tensor(std[:], std[:], sq[:, (q0 + n) % 2], ALU.add).then_inc(ysum.sem, 1)
            ysum.give_loop((L, "post"), NC)

        TAB = S + 32
        top[0] = region
        ya_hi = at("ya_hi", [P, 4, S], F32R)
        ya_lo = at("ya_lo", [P, 4, S], F32R)
        crr = at("crr", [P, NCONSTR, P], F32R)
        crf = at("crf", [P, 3, P])
        hybrid = top[0]
        ka_hi = at("ka_hi", [P, 4, S], F32R)
        ka_lo = at("ka_lo", [P, 4, S], F32R)
        va_hi = at("va_hi", [P, 4, 4, 3, 64], F32R)
        va_lo = at("va_lo", [P, 4, 4, 3, 64], F32R)
        za = at("za", [P, 4, S])
        sp_hi = at("sp_hi", [P, 4, S], F32R)
        sp_lo = at("sp_lo", [P, 4, S], F32R)
        wt_hi = at("wt_hi", [P, 4, S], F32R)
        wt_lo = at("wt_lo", [P, 4, S], F32R)
        assert top[0] <= nc.sbuf_usable_end, (top[0], nc.sbuf_usable_end)
        top[0] = hybrid
        cload = at("cload", [P, NCONSTR, P])
        top[0] = hybrid
        nq_hi = at("nq_hi", [P, 4, S], F32R)
        nq_lo = at("nq_lo", [P, 4, S], F32R)
        after_q = top[0]
        nk_hi = at("nk_hi", [P, 2, S], F32R)
        nk_lo = at("nk_lo", [P, 2, S], F32R)
        nv_hi = at("nv_hi", [P, 4, 2, 3, 64], F32R)
        nv_lo = at("nv_lo", [P, 4, 2, 3, 64], F32R)
        zb = at("zb", [P, 4, S])
        rcos = at("rcos", [P, TAB])
        rsin = at("rsin", [P, TAB])
        f_hi = at("f_hi", [P, 992], F32R)
        f_lo = at("f_lo", [P, 992], F32R)
        hid = at("hid", [P, 2, 62])
        w2s = at("w2s", [P, 2, 256])
        kc_hi = at("kc_hi", [P, 32], F32R)
        kc_lo = at("kc_lo", [P, 32], F32R)
        vc_hi = at("vc_hi", [P, 3, 64], F32R)
        vc_lo = at("vc_lo", [P, 3, 64], F32R)
        rc = at("rc", [P, 6])
        pn = at("pn", [P, 2, S])
        pt_base = top[0]
        nf = at("nf", [P, 6, S])
        zk = at("zk", [P, 2, 2, S // 2])
        top[0] = pt_base
        pt1_hi = at("pt1_hi", [P, 1, 4, S], F32R)
        pt1_lo = at("pt1_lo", [P, 1, 4, S], F32R)
        top[0] = mod_base
        gt = at("gt", [P, 4, 24])
        kcf = at("kcf", [P, 32])
        top[0] = pt_base
        posi = at("posi", [P, S], I32)
        assert top[0] <= nc.sbuf_usable_end
        assert pt_base + 16384 <= nc.sbuf_usable_end, (pt_base + 16384, nc.sbuf_usable_end)
        top[0] = after_q
        mg_hi = at("mg_hi", [P, NC, S], F32R)
        mg_lo = at("mg_lo", [P, NC, S], F32R)

        zs = Signal(sem("sb_scores"))
        logs = Signal(sem("sb_logs"))
        softplus = Signal(sem("sb_softplus"))
        exponent = Signal(sem("sb_exponents"))
        weights = Signal(sem("sb_weights"))
        weights_lo = Signal(sem("sb_weights_split"))

        def flat(t, n):
            return t[:].rearrange("p a n -> p (a n)")[:, 0:n]

        def plan_hybrid(l):
            L = ("hy", l)

            def group():
                cur.g += 1
                return cur.g - 1
            own[L, "loaded0"] = 16 * (stage_loads[0] + 4) if l == 0 else 16 * stage_loads[0]
            if l == 0:
                stage_loads[0] += 4
                part_hi.plan("crr")
            own[L, "loaded1"] = 16 * (stage_loads[0] + 3)
            stage_loads[0] += 3
            plan_pre(L)
            own[L, "ua"], own[L, "ga"] = cur.u, cur.g
            for c in range(8):
                plan_unit(cur.g)
                evac_hi.plan(cur.g)
                evac.plan(("g", group()))
            for m in range(3):
                plan_unit()
            for t in range(3):
                prod.plan(("g", cur.g + t))
            plan_unit(cur.g + 3)
            for t in range(4):
                evac_hi.plan(cur.g)
                evac.plan(("g", group()))
            for c in range(4):
                plan_unit(cur.g)
                evac.plan(("g", group()))
                value.plan((L, "za", c))
            for k in range(32):
                for signal in (zs, logs, softplus, exponent, weights, weights_lo):
                    signal.plan((L, k))
            for h in range(8):
                if h % 2 == 0:
                    prod.plan(("sb", L, h))
                else:
                    prod.plan(("g", cur.g))
                    prod.values["sb", L, h] = prod.planned
                    evac.plan(("g", cur.g))
                    part_hi.plan((L, "ya", h // 2))
                    h_ready.plan((L, "ya", h // 2))
                    own[L, "sbg", h // 2] = group()
            own[L, "ub"], own[L, "gb"] = cur.u, cur.g
            scaled.plan((L, "angle", 0), (L, "angle", 1))
            value.plan((L, "trig", 0), (L, "trig", 1))
            for s in range(14):
                plan_unit(cur.g)
                evac.plan(("g", group()))
                if 1 <= s <= 6:
                    plan_norm((L, "n", s - 1), 1)
                    scaled.plan((L, "xn", s - 1))
                if 2 <= s <= 7:
                    for signal in (sums, scaled, part_hi, h_ready):
                        signal.plan((L, "rot", s - 2))
                if s >= 10:
                    value.plan((L, "zb", s - 10))
            for m in range(2):
                plan_unit()
            for t in range(3):
                prod.plan(("g", cur.g + t))
            plan_unit(cur.g + 3)
            for t in range(4):
                evac_hi.plan(cur.g)
                evac.plan(("g", group()))
            value.plan((L, "gates"))
            scaled.plan((L, "gates"))
            for kv in range(2):
                scaled.plan((L, "f", kv))
                part_hi.plan((L, "f", kv))
                h_ready.plan((L, "f", kv))
                for m in range(3):
                    plan_unit()
                prod.plan(("g", cur.g))
                plan_unit(cur.g + 1)
                evac.plan(("g", group()))
                evac.plan(("g", group()))
                value.plan((L, "hid", kv))
                prod.plan(("g", cur.g))
                if kv == 1:
                    evac_hi.plan(cur.g)
                else:
                    own[L, "kcg"] = cur.g
                evac.plan(("g", group()))
                if kv == 0:
                    plan_norm((L, "n", 6), 1)
                    scaled.plan((L, "xn", 6))
                    sums.plan((L, "rot", 6))
                    scaled.plan((L, "rot", 6))
                    part_hi.plan((L, "rot", 6))
                    h_ready.plan((L, "rot", 6))
                    scaled.plan((L, "vc"))
            plan_softmax(L, {"tasks": 24})
            for t in range(24):
                if t % 6 == 5:
                    prod.plan(("g", cur.g))
                    prod.values["pv", L, t] = prod.planned
                    evac.plan(("g", cur.g))
                    part_hi.plan((L, "yb", t // 6))
                    h_ready.plan((L, "yb", t // 6))
                    own[L, "ng", t // 6] = group()
                else:
                    prod.plan(("pv", L, t))
            own[L, "uc"], own[L, "gc"] = cur.u, cur.g
            for n in range(NC):
                for m, e in enumerate((1, 2, 4)):
                    prod.values["u", cur.u + 3 * n + m] = prod.planned + 4 * n + e
                for m in range(4):
                    prod.values["g", cur.g + 4 * n + m] = prod.planned + 4 * n + m + 1
                    evac.values["g", cur.g + 4 * n + m] = evac.planned + 4 * n + m + 1
            prod.plan_loop((L, "up"), 32)
            evac.plan_loop((L, "up"), 32)
            value.plan_loop((L, "up"), 16)
            part_hi.plan_loop((L, "up"), NC)
            cur.u += 24
            cur.g += 32
            own[L, "ud"], own[L, "gd"] = cur.u, cur.g
            for n in range(NC):
                plan_unit(cur.g)
                evac.plan(("g", group()))
            own[L, "after"] = cur.g - NC

        def stream_ready(before, c):
            if isinstance(before, tuple):
                return evac.sem, evac.at(("g", own[before, "after"] + c))
            return x_ready.sem, x_ready.at((before, c))

        def natural_pe(pe, u, g, per_unit, width, units_of):
            for t in range(4):
                free_bank(pe, g + t)
            for m in range(units_of):
                pe.wait_ge(lo_ready, u + m + 1)
                s = (u + m) % RING
                ks = range(per_unit * m, min(per_unit * (m + 1), NC))
                for t in range(4):
                    tok = slice(t * P, (t + 1) * P)
                    mm = three_passes(
                        pe, bank(g + t)[:, 0:width], [(h_hi[:, k, tok], h_lo[:, k, tok]) for k in ks],
                        [(w_hi[:, s, (k - ks[0]) * width:(k - ks[0] + 1) * width],
                          w_lo[:, s, (k - ks[0]) * width:(k - ks[0] + 1) * width]) for k in ks],
                        first=(m == 0), last=(m == units_of - 1))
                    if m == units_of - 1 and t < 3:
                        prod.give(mm, ("g", g + t))
                prod.give(mm, ("u", u + m))

        def sb_place(k):
            h, n = divmod(k, 4)
            j = 3 - n
            return h, j, slice(j * P, S), 4 + k % 3

        def sb_pe(pe, L):
            def z(k):
                if k >= 32:
                    return
                h, j, q, b = sb_place(k)
                rows = slice(64 * (h % 2), 64 * (h % 2) + 64)
                if k >= 3:
                    pe.wait_ge(weights.sem, weights.at((L, k - 3)))
                dst = psum[:, b, q]
                keys = slice(j * P, (j + 1) * P)
                three_passes(pe, dst, [(ka_hi[rows, h // 2, keys], ka_lo[rows, h // 2, keys])],
                             [(ya_hi[rows, h // 2, q], ya_lo[rows, h // 2, q])], last=False, skip=True)
                zs.give(pe.matmul(psum[:, b, keys], crr[:, R_IDENT], crr[:, R_STRICT_T], start=False,
                                  stop=True, skip_group_check=True), (L, k))

            def accumulate(k):
                h, j, q, b = sb_place(k)
                pe.wait_ge(softplus.sem, softplus.at((L, k)))
                for jj in range(j, 4):
                    qq = slice(jj * P, S)
                    for part in (sp_hi, sp_lo):
                        mm = pe.matmul(psum[:, b, qq], crr[:, R_NEGTRI if jj == j else R_NEGONES],
                                       part[:, jj, qq], start=False, stop=True, skip_group_check=True)
                exponent.give(mm, (L, k))

            def values(h):
                g = own[L, "sbg", h // 2]
                pe.wait_ge(weights_lo.sem, weights_lo.at((L, 4 * h + 3)))
                if h % 2 == 0:
                    free_bank(pe, g)
                n = 0
                for wi, mi in ((0, 0), (1, 0), (0, 1)):
                    for j in range(4):
                        q = slice(j * P, S)
                        v = (va_hi, va_lo)[wi][:, j, h // 2, h % 2:h % 2 + 2, :].rearrange("p a n -> p (a n)")
                        mm = pe.matmul(bank(g)[:, q], v, (wt_hi, wt_lo)[mi][:, j, q],
                                       start=(n == 0 and h % 2 == 0), stop=(n == 11 and h % 2 == 1),
                                       skip_group_check=True)
                        n += 1
                prod.give(mm, ("sb", L, h))
            z(0)
            z(1)
            for k in range(32):
                z(k + 2)
                if k % 4 == 1 and k >= 4:
                    values(k // 4 - 1)
                accumulate(k)
            values(7)

        def sb_act(act, order, L):
            def log_part(k):
                if k >= 32:
                    return
                h, j, q, b = sb_place(k)
                act.wait_ge(zs.sem, zs.at((L, k)))
                if k >= 2:
                    act.wait_ge(softplus.sem, softplus.at((L, k - 2)))
                t = ta[:, k % 2, q]
                order.step(act.activation(t, psum[:, b, q], ACT.Abs))
                order.step(act.activation(t, t, ACT.Exp, scale=-1.0))
                logs.give(act.activation(t, t, ACT.Ln, bias=1.0), (L, k))
            log_part(0)
            for k in range(32):
                log_part(k + 1)
                h, j, q, b = sb_place(k)
                act.wait_ge(exponent.sem, exponent.at((L, k)))
                if k >= 2:
                    act.wait_ge(weights_lo.sem, weights_lo.at((L, k - 2)))
                weights.give(act.activation(sq[:, k % 2, q], psum[:, b, q], ACT.Exp), (L, k))
                if k % 8 == 2 and k >= 8:
                    sb_out_act(act, L, k // 8 - 1)
            sb_out_act(act, L, 3)

        def sb_out_act(act, L, p):
            act.wait_ge(evac.sem, evac.at(("g", own[L, "sbg", p])))
            part_hi.give(act.activation(ya_hi[:, p], rstd[:], ACT.Copy), (L, "ya", p))

        def sb_dve(dve, order, L):
            def softplus_part(k):
                if k >= 32:
                    return
                h, j, q, b = sb_place(k)
                if k % 4 == 0 and k:
                    dve.wait_ge(exponent.sem, exponent.at((L, k - 1)))
                dve.wait_ge(logs.sem, logs.at((L, k)))
                if k >= 2:
                    dve.wait_ge(softplus.sem, softplus.at((L, k - 2)))
                t = tb[:, k % 2, q]
                order.step(dve.scalar_tensor_tensor(out=t, in0=psum[:, b, q], scalar=0.0,
                                                    in1=ta[:, k % 2, q], op0=ALU.max, op1=ALU.add))
                order.step(dve.tensor_copy(sp_hi[:, j, q], t))
                softplus.give(dve.tensor_tensor(sp_lo[:, j, q], t, sp_hi[:, j, q].bitcast(F32),
                                                ALU.subtract), (L, k))

            def out(p, phase):
                g = own[L, "sbg", p]
                if phase == 0:
                    dve.wait_ge(prod.sem, prod.at(("g", g)))
                    if p:
                        dve.wait_ge(h_ready.sem, h_ready.at((L, "ya", p - 1)))
                    dve.wait_ge(value.sem, value.at((L, "za", p)))
                    evac.give(dve.tensor_tensor(rstd[:], bank(g), za[:, p], ALU.mult), ("g", g))
                else:
                    dve.wait_ge(part_hi.sem, part_hi.at((L, "ya", p)))
                    h_ready.give(dve.tensor_tensor(ya_lo[:, p], rstd[:], ya_hi[:, p].bitcast(F32),
                                                   ALU.subtract), (L, "ya", p))
            softplus_part(0)
            for k in range(32):
                softplus_part(k + 1)
                h, j, q, b = sb_place(k)
                if k % 4 == 0 and k:
                    dve.wait_ge(prod.sem, prod.at(("sb", L, h - 1)))
                dve.wait_ge(weights.sem, weights.at((L, k)))
                order.step(dve.tensor_copy(wt_hi[:, j, q], sq[:, k % 2, q]))
                weights_lo.give(dve.tensor_tensor(wt_lo[:, j, q], sq[:, k % 2, q],
                                                  wt_hi[:, j, q].bitcast(F32), ALU.subtract), (L, k))
                if k >= 8 and k % 8 in (1, 3):
                    out(k // 8 - 1, 0 if k % 8 == 1 else 1)
            out(3, 0)
            out(3, 1)

        def nsa_attention(l):
            L = ("hy", l)

            def parts(t):
                return t // 6, t % 6 // 3, t % 3

            def run(pe, t, i, dst):
                c, side, b = parts(t)
                rows, q = slice(64 * side, 64 * side + 64), slice(i * P, (i + 1) * P)
                w = (i + 1) * P if b < 2 else 32
                moving = ((nk_hi[rows, b, 0:w], nk_lo[rows, b, 0:w]) if b < 2 else
                          (kc_hi[rows, :], kc_lo[rows, :]))
                three_passes(pe, dst, [(nq_hi[rows, c, q], nq_lo[rows, c, q])], [moving], last=False,
                             skip=True)
                if b < 2:
                    return pe.matmul(dst[:, i * P:(i + 1) * P], crr[:, R_IDENT], crr[:, R_CAUSAL],
                                     start=False, stop=True, skip_group_check=True)
                return pe.matmul(dst, crr[:, R_IDENT], crr[:, R_NEG31, 32 * i:32 * i + 32],
                                 start=False, stop=True, skip_group_check=True)

            def values(t, j):
                c, side, b = parts(t)
                pick = ((lambda v: v[:, j, b, side:side + 2, :]) if b < 2 else
                        (lambda v: v[0:32, side:side + 2, :]))
                pair = (nv_hi, nv_lo) if b < 2 else (vc_hi, vc_lo)
                return tuple(pick(v).rearrange("p a n -> p (a n)") for v in pair)

            def gate(t, i):
                c, side, b = parts(t)
                g = 8 * (1, 2, 0)[b] + 4 * side + c
                return gt[:, i, g:g + 1]
            return {
                "tasks": 24, "width": lambda t, i: (i + 1) * P if t % 3 < 2 else 32, "scores": run,
                "scale": 0.125, "gate": gate, "p": pn, "pt": (pt1_hi, pt1_lo), "slots": 1,
                "rows": lambda t: P if t % 3 < 2 else 32, "blocks": lambda t: 4 if t % 3 < 2 else 1,
                "start": lambda t, j: j * P, "values": values, "ident": crf[:, 0],
                "group": lambda t: (own[L, "ng", t // 6], t % 6 == 0, t % 6 == 5),
                "bank7": (L, "n", 6),
            }

        def nsa_extra(L):
            def run(eng, who, k, phase=0):
                if who == "pe" or k == -1:
                    return
                if k == 96:
                    c, steps = 3, (0, 1)
                else:
                    c, at_ = k // 24 - 1, k % 24
                    if c < 0 or phase != 1 or at_ not in (1, 2, 3):
                        return
                    if who == "act":
                        if at_ != 2:
                            return
                        steps = (1,)
                    else:
                        if at_ == 2:
                            return
                        steps = (0,) if at_ == 1 else (1,)
                g = own[L, "ng", c]
                if who == "act":
                    eng.wait_ge(evac.sem, evac.at(("g", g)))
                    part_hi.give(eng.activation(nq_hi[:, c], rstd[:], ACT.Copy), (L, "yb", c))
                    return
                for s in steps:
                    if s == 0:
                        eng.wait_ge(prod.sem, prod.at(("g", g)))
                        if c:
                            eng.wait_ge(h_ready.sem, h_ready.at((L, "yb", c - 1)))
                        eng.wait_ge(value.sem, value.at((L, "zb", c)))
                        evac.give(eng.tensor_tensor(rstd[:], bank(g), zb[:, c], ALU.mult), ("g", g))
                    else:
                        eng.wait_ge(part_hi.sem, part_hi.at((L, "yb", c)))
                        h_ready.give(eng.tensor_tensor(nq_lo[:, c], rstd[:], nq_hi[:, c].bitcast(F32),
                                                       ALU.subtract), (L, "yb", c))
            return run

        def item(n):
            if n < 4:
                return nf[:, n], nq_hi[:, n], nq_lo[:, n], S, 0
            if n < 6:
                return nf[:, n], nk_hi[:, n - 4], nk_lo[:, n - 4], S, 0
            return kcf[:], kc_hi[:], kc_lo[:], 32, S

        def item_gain(l, n):
            c = col.at["q_norm_2"] + l if n < 4 else col.at["k_norm_2"] + 3 * l + (1, 2, 0)[n - 4]
            return par[:, c:c + 1]

        def item_rotate_pe(pe, L, n):
            w = item(n)[3]
            pe.wait_ge(scaled.sem, scaled.at((L, "xn", n)))
            if n >= 2:
                pe.wait_ge(scaled.sem, scaled.at((L, "rot", n - 2)))
            sums.give(pe.matmul(psum[:, 4 + n % 2, 0:w], crf[:, 2], ta[:, n % 2, 0:w], start=True,
                                stop=True), (L, "rot", n))

        def item_norm_act(act, l, n):
            L = ("hy", l)
            src, _, _, w, _ = item(n)
            g = own[L, "gb"] + n if n < 6 else own[L, "kcg"]
            norm_act(act, (L, "n", n), [(src, (evac.sem, evac.at(("g", g))))], 64, w)

        def item_hi_act(act, L, n):
            src, hi, _, w, _ = item(n)
            split_value_act(act, (L, "rot", n), tb[:, n % 2, 0:w], hi)

        def item_norm_dve(dve, l, n):
            L = ("hy", l)
            src, _, _, w, _ = item(n)
            if n:
                dve.wait_ge(scaled.sem, scaled.at((L, "xn", n - 1)))
            norm_dve(dve, (L, "n", n), w)
            if n >= 2:
                dve.wait_ge(sums.sem, sums.at((L, "rot", n - 2)))
                dve.wait_ge(scaled.sem, scaled.at((L, "rot", n - 2)))
            scaled.give(dve.scalar_tensor_tensor(out=ta[:, n % 2, 0:w], in0=src, scalar=item_gain(l, n),
                                                 in1=rstd[:, 0:w], op0=ALU.mult, op1=ALU.mult),
                        (L, "xn", n))

        def item_rotate_dve(dve, order, L, n):
            src, hi, lo, w, off = item(n)
            dve.wait_ge(scaled.sem, scaled.at((L, "xn", n)))
            if n >= 2:
                dve.wait_ge(h_ready.sem, h_ready.at((L, "rot", n - 2)))
            dst = tb[:, n % 2, 0:w]
            order.step(dve.tensor_tensor(dst, ta[:, n % 2, 0:w], rcos[:, off:off + w], ALU.mult))
            dve.wait_ge(sums.sem, sums.at((L, "rot", n)))
            order.step(dve.tensor_tensor(pn[:, 0, 0:w], psum[:, 4 + n % 2, 0:w], rsin[:, off:off + w],
                                         ALU.mult))
            scaled.give(dve.tensor_tensor(dst, dst, pn[:, 0, 0:w], ALU.add), (L, "rot", n))
            split_value_dve(dve, (L, "rot", n), dst, hi, lo)

        def hybrid_pe(pe, l):
            L = ("hy", l)
            attention = nsa_attention(l)
            norm_pe(pe, (L, "pre"), NC, ones[:])
            pe.wait_ge(h_ready.sem, h_ready.at((L, NC - 1)))
            u, g = own[L, "ua"], own[L, "ga"]
            for c in range(8):
                dense(pe, u + c, g + c)
            natural_pe(pe, u + 8, g + 8, 2, S, 4)
            for c in range(4):
                dense(pe, u + 12 + c, g + 12 + c)
            if l == 0:
                pe.wait_ge(part_hi.sem, part_hi.at("crr"))
                pe.wait_ge(stage_loaded, own[L, "loaded0"])
            pe.wait_ge(evac.sem, evac.at(("g", g + 15)))
            sb_pe(pe, L)
            u, g = own[L, "ub"], own[L, "gb"]
            for s in range(14):
                dense(pe, u + s, g + s)
                if 1 <= s <= 6:
                    norm_pe(pe, (L, "n", s - 1), 1, crf[:, 1])
                if 2 <= s <= 7:
                    item_rotate_pe(pe, L, s - 2)
            natural_pe(pe, u + 14, g + 14, 3, NAT2, 3)
            u, g = u + 17, g + 18
            for kv in range(2):
                pe.wait_ge(h_ready.sem, h_ready.at((L, "f", kv)))
                free_bank(pe, g)
                free_bank(pe, g + 1)
                for m in range(4):
                    pe.wait_ge(lo_ready, u + m + 1)
                    s = (u + m) % RING
                    for half in range(2):
                        ws = [tuple(w[:, s, 256 * a + P * half:256 * a + P * half + P] for w in (w_hi, w_lo))
                              for a in range(4)]
                        fs = [tuple(f[:, 62 * (4 * m + a):62 * (4 * m + a) + 62] for f in (f_hi, f_lo))
                              for a in range(4)]
                        mm = three_passes(pe, bank(g + half)[:, 0:62], ws, fs, first=(m == 0),
                                          last=(m == 3))
                        if m == 3 and half == 0:
                            prod.give(mm, ("g", g))
                    prod.give(mm, ("u", u + m))
                u, g = u + 4, g + 2
                pe.wait_ge(value.sem, value.at((L, "hid", kv)))
                pe.wait_ge(stage_loaded, own[L, "loaded1"])
                free_bank(pe, g)
                for side in range(2):
                    for half in range(2):
                        blocks_of = hid[:, half, 31 * side:31 * side + 31]
                        if kv == 0:
                            mm = pe.matmul(bank(g)[:, 0:NCMP], w2s[:, half, 64 * (1 - side):64 * (1 - side) + P],
                                           blocks_of, start=(side == 0 and half == 0),
                                           stop=(side == 1 and half == 1))
                        else:
                            mm = pe.matmul(bank(g)[0:NCMP, 64 * side:64 * side + 64], blocks_of,
                                           w2s[:, half, 192:256], start=(half == 0), stop=(half == 1))
                prod.give(mm, ("g", g))
                g += 1
                if kv == 0:
                    norm_pe(pe, (L, "n", 6), 1, crf[:, 1], 32)
                    item_rotate_pe(pe, L, 6)
            pe.wait_ge(h_ready.sem, h_ready.at((L, "rot", 6)))
            pe.wait_ge(evac.sem, evac.at(("g", g - 1)))
            pe.wait_ge(scaled.sem, scaled.at((L, "gates")))
            softmax_pe(pe, L, attention, nsa_extra(L))
            u, g = own[L, "uc"], own[L, "gc"]
            pe.wait_ge(h_ready.sem, h_ready.at((L, "yb", 3)))
            with pe.Fori(0, 2) as i:
                for n in range(4):
                    for m in range(4):
                        pe.wait_ge(evac.sem, i * 16 + (g + 4 * n + m - 8 + 1))
                        if m < 3:
                            pe.wait_ge(lo_ready, i * 12 + (u + 3 * n + m + 1))
                        b = psum[:, 4 * (n % 2) + m]
                        if m < 2:
                            mm = three_passes(pe, b, unit_blocks(u + 3 * n + m, range(NC)),
                                              chunks_of(h_hi, h_lo, range(NC)))
                        else:
                            y_hi, y_lo = ((ya_hi, ya_lo), (nq_hi, nq_lo))[m - 2]
                            mm = three_passes(pe, b, unit_blocks(u + 3 * n + 2, range(4 * (m - 2), 4 * (m - 1))),
                                              chunks_of(y_hi, y_lo, range(4)))
                        mm.then_inc(prod.sem, 1)
            prod.give_loop((L, "up"), 32)
            u, g = own[L, "ud"], own[L, "gd"]
            pe.wait_ge(evac.sem, evac.at(("g", g - 1)))
            for n in range(NC):
                pe.wait_ge(lo_ready, u + n + 1)
                mm = three_passes(pe, bank(g + n), unit_blocks(u + n, range(NC)),
                                  chunks_of(mg_hi, mg_lo, range(NC)))
                prod.give(mm, ("u", u + n))
                if n + 1 < NC:
                    free_bank(pe, g + n + 1)

        def hybrid_act(act, order, l, before):
            L = ("hy", l)
            attention = nsa_attention(l)
            if l == 0:
                act.wait_ge(*stream_ready(before, 0))
                for k, c in enumerate((IDENT, ONES64, PERM64)):
                    act.dma_start(crf[:, k], consts[:, c * P:(c + 1) * P]).then_inc(stage_loaded, 16)
                act.dma_start(cload[:].rearrange("p a n -> p (a n)"), constsr).then_inc(stage_loaded, 16)
                act.wait_ge(stage_loaded, own[L, "loaded0"])
                part_hi.give(act.activation(crr[:], cload[:], ACT.Copy), "crr")
            norm_act(act, (L, "pre"), [(X[:, c], stream_ready(before, c)) for c in range(NC)], D)
            for c in range(NC):
                split_value_act(act, (L, c), tb[:, c % 2], h_hi[:, c])
            u, g = own[L, "ua"], own[L, "ga"]
            for c in range(8):
                split_hi(act, u + c + LEAD)
                hi = (ya_hi if c < 4 else ka_hi)[:, c % 4]
                evac_split_act(act, g + c, hi, 0.125 if c < 4 else 1.0)
            for m in range(4):
                split_hi(act, u + 8 + m + LEAD)
            for t in range(4):
                act.wait_ge(prod.sem, prod.at(("g", g + 8 + t)))
                evac_hi.give(act.activation(
                    va_hi[:, t, :, 0:3:2, :], bank(g + 8 + t).rearrange("p (a b n) -> p a b n", a=4, b=2),
                    ACT.Copy), g + 8 + t)
            for c in range(4):
                split_hi(act, u + 12 + c + LEAD)
                act.wait_ge(evac.sem, evac.at(("g", g + 12 + c)))
                value.give(act.activation(za[:, c], za[:, c], ACT.Silu), (L, "za", c))
            sb_act(act, order, L)
            u, g = own[L, "ub"], own[L, "gb"]
            act.wait_ge(prod.sem, prod.at(("sb", L, 7)))
            act.wait_ge(evac.sem, evac.at(("g", g - 1)))
            act.dma_start(posi[:], pos).then_inc(stage_loaded, 16)
            act.dma_start(w2s[:], w2[l]).then_inc(stage_loaded, 16)
            act.dma_start(rc[:], rope_cst).then_inc(stage_loaded, 16)
            act.wait_ge(scaled.sem, scaled.at((L, "angle", 0)))
            for k in range(2):
                act.wait_ge(scaled.sem, scaled.at((L, "angle", k)))
                value.give(act.activation((rsin, rcos)[k][:], flat((tb, sq)[k], TAB), ACT.Sin), (L, "trig", k))
            for s in range(14):
                split_hi(act, u + s + LEAD)
                if s == 1:
                    act.wait_ge(value.sem, value.at((L, "trig", 1)))
                if 1 <= s <= 6:
                    item_norm_act(act, l, s - 1)
                if 2 <= s <= 7:
                    item_hi_act(act, L, s - 2)
                if s >= 10:
                    act.wait_ge(evac.sem, evac.at(("g", g + s)))
                    value.give(act.activation(zb[:, s - 10], zb[:, s - 10], ACT.Silu), (L, "zb", s - 10))
            for m in range(3):
                split_hi(act, u + 14 + m + LEAD)
            for t in range(4):
                act.wait_ge(prod.sem, prod.at(("g", g + 14 + t)))
                evac_hi.give(act.activation(
                    nv_hi[:, t, :, 0:3:2, :], bank(g + 14 + t)[:, 0:256].rearrange("p (a b n) -> p a b n", a=2, b=2),
                    ACT.Copy), g + 14 + t)
            act.wait_ge(evac.sem, evac.at(("g", g + 17)))
            value.give(act.activation(gt[:], gt[:], ACT.Sigmoid), (L, "gates"))
            u, g = u + 17, g + 18
            for kv in range(2):
                split_value_act(act, (L, "f", kv), flat(ta, 992), f_hi[:])
                for m in range(4):
                    split_hi(act, u + m + LEAD)
                b1 = col.at["cmp_b1"] + 4 * l + 2 * kv
                act.wait_ge(evac.sem, evac.at(("g", g + 1)))
                order.link(act.activation(hid[:, 0], hid[:, 0], ACT.Silu, bias=par[:, b1:b1 + 1]))
                value.give(act.activation(hid[:, 1], hid[:, 1], ACT.Silu, bias=par[:, b1 + 1:b1 + 2]),
                           (L, "hid", kv))
                u, g = u + 4, g + 2
                if kv == 0:
                    item_norm_act(act, l, 6)
                    item_hi_act(act, L, 6)
                else:
                    act.wait_ge(prod.sem, prod.at(("g", g)))
                    act.wait_ge(scaled.sem, scaled.at((L, "vc")))
                    evac_hi.give(act.activation(vc_hi[0:NCMP, 0:3:2, :],
                                                bank(g)[0:NCMP, 0:P].rearrange("p (a n) -> p a n", a=2),
                                                ACT.Copy), g)
                g += 1
            softmax_act(act, L, attention, nsa_extra(L))
            u, g = own[L, "uc"], own[L, "gc"]
            base = prod.at((L, "up"))
            with act.Fori(0, 2) as i:
                for n in range(4):
                    for m in range(3):
                        split_hi_loop(act, i, 12, u + 3 * n + m + LEAD, i * 16 + (base + 4 * n + (-1, 0, 1)[m]))
                    for m in range(2):
                        act.wait_ge(prod.sem, i * 16 + (base + 4 * n + m + 1))
                        act.wait_ge(evac.sem, i * 16 + (g + 4 * n - 1))
                        act.activation(ta[:, m], psum[:, 4 * (n % 2) + m], ACT.Sigmoid).then_inc(value.sem, 1)
                    act.wait_ge(evac.sem, i * 16 + (g + 4 * n + 3))
                    act.activation(mg_hi[:, bass.ds(i * 4 + n, 1), :].rearrange("p a n -> p (a n)"),
                                   tb[:, 0], ACT.Copy).then_inc(part_hi.sem, 1)
            value.give_loop((L, "up"), 16)
            part_hi.give_loop((L, "up"), NC)
            u = own[L, "ud"]
            for n in range(NC):
                split_hi(act, u + n + LEAD)

        def tables_dve(dve, order, L):
            a, t = flat(ta, TAB), flat(pn, TAB)
            dve.wait_ge(stage_loaded, own[L, "loaded1"])
            order.step(dve.tensor_copy(a[:, 0:S], posi[:]))
            order.step(dve.tensor_reduce(t[:, 0:32], a[:, 0:S].rearrange("p (a b) -> p a b", b=16), AXX, ALU.add))
            order.link(dve.tensor_scalar(a[:, S + 31:S + 32], t[:, 31:32], 1.0 / 32, None, ALU.mult))
            order.step(dve.tensor_tensor(a[:, S:S + 31], t[:, 0:31], t[:, 1:32], ALU.add))
            order.step(dve.tensor_scalar(a[:, S:S + 31], a[:, S:S + 31], 1.0 / 32, None, ALU.mult))
            order.step(dve.tensor_scalar(a, a, rc[:, 0:1], None, ALU.mult))
            magic = 1.5 * 2 ** 23
            two_pi = 6.283185307179586
            c1 = 6.28125
            c2 = 2029.0 / 2 ** 20
            c3 = two_pi - c1 - c2
            for k in range(2):
                r = flat((tb, sq)[k], TAB)
                order.step(dve.tensor_scalar(t, a, 1 / two_pi, 0.25 * k, ALU.mult, ALU.add))
                order.step(dve.tensor_scalar(t, t, magic, None, ALU.add))
                order.step(dve.tensor_scalar(t, t, magic, None, ALU.subtract))
                order.step(dve.scalar_tensor_tensor(out=r, in0=t, scalar=-c1, in1=a, op0=ALU.mult, op1=ALU.add))
                order.step(dve.scalar_tensor_tensor(out=r, in0=t, scalar=-c2, in1=r, op0=ALU.mult, op1=ALU.add))
                order.step(dve.scalar_tensor_tensor(out=r, in0=t, scalar=-c3, in1=r, op0=ALU.mult, op1=ALU.add))
                if k:
                    order.step(dve.tensor_scalar(r, r, two_pi / 4, None, ALU.add))
                scaled.give(dve.tensor_scalar(r, r, 3.1415925, -3.1415925, ALU.min, ALU.max), (L, "angle", k))
            dve.wait_ge(value.sem, value.at((L, "trig", 1)))
            order.step(dve.tensor_scalar(rsin[:], rsin[:], rc[:, 1:2], None, ALU.mult))

        def hybrid_dve(dve, order, l):
            L = ("hy", l)
            attention = nsa_attention(l)
            ng = col.at["norm_g_2"] + 8 * l
            pre_dve(dve, order, L, par[:, ng:ng + 8])
            u, g = own[L, "ua"], own[L, "ga"]
            order.link(dve.memset(va_hi[:, :, :, 1, :].bitcast(F32), 0.0))
            order.step(dve.memset(va_lo[:, :, :, 1, :].bitcast(F32), 0.0))
            for c in range(8):
                split_lo(dve, u + c + LEAD)
                hi, lo = ((ya_hi, ya_lo) if c < 4 else (ka_hi, ka_lo))
                evac_split_dve(dve, g + c, hi[:, c % 4], lo[:, c % 4], 0.125 if c < 4 else 1.0)
            for m in range(4):
                split_lo(dve, u + 8 + m + LEAD)
            for t in range(4):
                dve.wait_ge(evac_hi.sem, evac_hi.at(g + 8 + t))
                evac.give(dve.tensor_tensor(
                    va_lo[:, t, :, 0:3:2, :], bank(g + 8 + t).rearrange("p (a b n) -> p a b n", a=4, b=2),
                    va_hi[:, t, :, 0:3:2, :].bitcast(F32), ALU.subtract), ("g", g + 8 + t))
            for c in range(4):
                split_lo(dve, u + 12 + c + LEAD)
                dve.wait_ge(prod.sem, prod.at(("g", g + 12 + c)))
                evac.give(dve.tensor_copy(za[:, c], bank(g + 12 + c)), ("g", g + 12 + c))
            sb_dve(dve, order, L)
            u, g = own[L, "ub"], own[L, "gb"]
            order.link(dve.memset(nv_hi[:, :, :, 1, :].bitcast(F32), 0.0))
            order.link(dve.memset(nv_lo[:, :, :, 1, :].bitcast(F32), 0.0))
            order.link(dve.memset(kcf[:], 0.0))
            order.link(dve.memset(vc_lo[:].bitcast(F32), 0.0))
            order.sync()
            tables_dve(dve, order, L)
            for s in range(14):
                split_lo(dve, u + s + LEAD)
                dve.wait_ge(prod.sem, prod.at(("g", g + s)))
                b = bank(g + s)
                if s < 6:
                    evac.give(dve.tensor_copy(nf[:, s], b), ("g", g + s))
                elif s < 10:
                    kv, side = divmod(s - 6, 2)
                    order.link(dve.tensor_copy(zk[0:64, kv, side], b[0:64, 0:S:2]))
                    evac.give(dve.tensor_copy(zk[64:128, kv, side], b[64:128, 1:S:2]), ("g", g + s))
                else:
                    evac.give(dve.tensor_copy(zb[:, s - 10], b), ("g", g + s))
                if 1 <= s <= 6:
                    item_norm_dve(dve, l, s - 1)
                if 2 <= s <= 7:
                    item_rotate_dve(dve, order, L, s - 2)
            for m in range(3):
                split_lo(dve, u + 14 + m + LEAD)
            for t in range(4):
                dve.wait_ge(evac_hi.sem, evac_hi.at(g + 14 + t))
                order.link(dve.tensor_tensor(
                    nv_lo[:, t, :, 0:3:2, :], bank(g + 14 + t)[:, 0:256].rearrange("p (a b n) -> p a b n", a=2, b=2),
                    nv_hi[:, t, :, 0:3:2, :].bitcast(F32), ALU.subtract))
                evac.give(dve.tensor_copy(gt[:, t], bank(g + 14 + t)[:, 256:NAT2]), ("g", g + 14 + t))
            dve.wait_ge(value.sem, value.at((L, "gates")))
            for t in range(4):
                op = dve.tensor_scalar(gt[:, t, 0:8], gt[:, t, 0:8], rc[:, 2 + t:3 + t], None, ALU.mult)
                if t < 3:
                    order.link(op)
                else:
                    scaled.give(op, (L, "gates"))
            u, g = u + 17, g + 18
            for kv in range(2):
                pe_col = col.at["cmp_pe"] + 32 * l + 16 * kv
                dve.wait_ge(h_ready.sem, h_ready.at((L, "rot", 6 if kv else 5)))
                if kv == 0:
                    dve.wait_ge(sums.sem, sums.at((L, "rot", 5)))
                else:
                    dve.wait_ge(prod.sem, prod.at(("g", g - 1)))
                for side in range(2):
                    for a in range(2):
                        blocks_of = zk[:, kv, side].rearrange("p (j b) -> p b j", b=8)[:, :, a:a + 31]
                        dst = flat(ta, 992).rearrange("p (q s j) -> p q s j", q=16, s=2)[:, 8 * a:8 * a + 8, side]
                        op = dve.tensor_tensor(dst, blocks_of,
                                               par[:, pe_col + 8 * a:pe_col + 8 * a + 8].unsqueeze(2).broadcast_to((P, 8, 31)),
                                               ALU.add)
                        if side == 1 and a == 1:
                            scaled.give(op, (L, "f", kv))
                        else:
                            order.link(op)
                order.sync()
                split_value_dve(dve, (L, "f", kv), flat(ta, 992), f_hi[:], f_lo[:])
                for m in range(4):
                    split_lo(dve, u + m + LEAD)
                for half in range(2):
                    dve.wait_ge(prod.sem, prod.at(("g", g + half)))
                    evac.give(dve.tensor_copy(hid[:, half], bank(g + half)[:, 0:62]), ("g", g + half))
                u, g = u + 4, g + 2
                if kv == 0:
                    dve.wait_ge(prod.sem, prod.at(("g", g)))
                    evac.give(dve.tensor_copy(kcf[:, 0:NCMP], bank(g)[:, 0:NCMP]), ("g", g))
                    item_norm_dve(dve, l, 6)
                    item_rotate_dve(dve, order, L, 6)
                    scaled.give(dve.memset(vc_hi[:].bitcast(F32), 0.0), (L, "vc"))
                else:
                    dve.wait_ge(evac_hi.sem, evac_hi.at(g))
                    evac.give(dve.tensor_tensor(
                        vc_lo[0:NCMP, 0:3:2, :], bank(g)[0:NCMP, 0:P].rearrange("p (a n) -> p a n", a=2),
                        vc_hi[0:NCMP, 0:3:2, :].bitcast(F32), ALU.subtract), ("g", g))
                g += 1
            dve.wait_ge(scaled.sem, scaled.at((L, "gates")))
            softmax_dve(dve, order, L, attention, nsa_extra(L))
            u, g = own[L, "uc"], own[L, "gc"]
            base, v0, p0 = prod.at((L, "up")), value.at((L, "up")), part_hi.at((L, "up"))
            with dve.Fori(0, 2) as i:
                for n in range(4):
                    for m in range(3):
                        split_lo_loop(dve, i, 12, u + 3 * n + m + LEAD)
                    dve.wait_ge(value.sem, i * 8 + (v0 + 2 * n + 2))
                    dve.wait_ge(prod.sem, i * 16 + (base + 4 * n + 4))
                    dve.wait_ge(evac.sem, i * 16 + (g + 4 * n))
                    b = 4 * (n % 2)
                    dve.tensor_tensor(tb[:, 0], ta[:, 0], psum[:, b + 2], ALU.mult).then_inc(evac.sem, 1)
                    dve.tensor_tensor(tb[:, 1], ta[:, 1], psum[:, b + 3], ALU.mult).then_inc(evac.sem, 1)
                    dve.wait_ge(evac.sem, i * 16 + (g + 4 * n + 2))
                    dve.tensor_tensor(tb[:, 0], tb[:, 0], tb[:, 1], ALU.add).then_inc(evac.sem, 1)
                    dve.wait_ge(part_hi.sem, i * 4 + (p0 + n + 1))
                    c = bass.ds(i * 4 + n, 1)
                    dve.tensor_tensor(mg_lo[:, c, :].rearrange("p a n -> p (a n)"), tb[:, 0],
                                      mg_hi[:, c, :].bitcast(F32).rearrange("p a n -> p (a n)"),
                                      ALU.subtract).then_inc(evac.sem, 1)
            evac.give_loop((L, "up"), 32)
            u, g = own[L, "ud"], own[L, "gd"]
            for n in range(NC):
                split_lo(dve, u + n + LEAD)
                dve.wait_ge(prod.sem, prod.at(("g", g + n)))
                evac.give(dve.tensor_tensor(X[:, n], X[:, n], bank(g + n), ALU.add), ("g", g + n))

        value.plan("silu_c")
        prod.plan("start0", "start1")
        plan_ffn("ffn0")
        plan_pool("pool")
        plan_ffn("ffn1")
        plan_ffn("ffn2")
        plan_mla("mla")
        plan_ffn("ffn3")
        plan_hybrid(0)
        plan_hybrid(1)
        last = ("hy", 1)
        assert cur.u == NU, (cur.u, NU)

        def gains(layer, sub):
            g = col.at["norm_g"] + 48 * layer + 16 * sub
            return lambda k: par[:, g + 8 * k:g + 8 * k + 8]

        with_ada = {"ffn0": [(6, 2), (5, None)], "ffn1": [(5, 8), (6, None)],
                    "ffn2": [(5, 13), (6, None)], "ffn3": [(11, None)]}

        block = ctx.enter_context(nc.Block())

        @block.sync
        def _(sp):
            sp.dma_start(par[:], params).then_inc(small_loaded, 16)
            sp.dma_start(ones[:], consts[:, ONES * P:(ONES + 1) * P]).then_inc(small_loaded, 16)
            sp.dma_start(X[:], xT).then_inc(small_loaded, 16)
            for u in range(RAW):
                sp.dma_start(raw[:, u], stream[u]).then_inc(raw_loaded[u], 16)
            with sp.Fori(0, (NU - RAW) // RAW) as i:
                for k in range(RAW):
                    sp.wait_ge(lo_ready, i * RAW + (k + 1))
                    sp.dma_start(raw[:, k], stream[bass.ds(i * RAW + (k + RAW), 1)]
                                 .rearrange("a p n -> p (a n)")).then_inc(raw_loaded[k], 16)
            if NU % RAW:
                sp.wait_ge(lo_ready, NU - RAW)
                sp.dma_start(raw[:, (NU - 1) % RAW], stream[NU - 1]).then_inc(raw_loaded[(NU - 1) % RAW], 16)
            for c in range(NC):
                sp.wait_ge(*stream_ready(last, c))
                sp.dma_start(out[:, c], X[:, c]).then_inc(stored, 16)
            sp.wait_ge(stored, 16 * NC)

        @block.gpsimd
        def _(pool):
            pieces = 18 * NC
            for t in range(2):
                pool.dma_start(ada_raw[:, t], ada[t]).then_inc(ada_loaded[t], 16)
            with pool.Fori(0, (pieces - 2) // 2) as i:
                for k in range(2):
                    pool.wait_ge(ada_used, i * 2 + (k + 1))
                    pool.dma_start(ada_raw[:, k], ada[bass.ds(i * 2 + (k + 2), 1)]
                                   .rearrange("a p n -> p (a n)")).then_inc(ada_loaded[k], 16)

        @block.tensor
        def _(pe):
            pe.wait_ge(small_loaded, 48)
            ada_close_pe(pe, 0, None)
            ada_close_pe(pe, 1, None)
            ffn_pe(pe, "ffn0", with_ada["ffn0"])
            pool_pe(pe, "pool")
            ffn_pe(pe, "ffn1", with_ada["ffn1"])
            ffn_pe(pe, "ffn2", with_ada["ffn2"])
            mla_pe(pe, "mla")
            ffn_pe(pe, "ffn3", with_ada["ffn3"])
            hybrid_pe(pe, 0)
            hybrid_pe(pe, 1)

        @block.scalar
        def _(act):
            order = Chain(act, act_own)
            act.wait_ge(small_loaded, 48)
            value.give(act.activation(silu_c[:], par[:, 0:8], ACT.Silu), "silu_c")
            act.wait_ge(evac.sem, 4)
            split_hi(act, 0)
            split_hi(act, 1)
            ffn_act(act, "ffn0", None, 0, with_ada["ffn0"])
            pool_act(act, "pool", "ffn0")
            ffn_act(act, "ffn1", "pool", 6, with_ada["ffn1"])
            ffn_act(act, "ffn2", "ffn1", 9, with_ada["ffn2"])
            mla_act(act, order, "mla", "ffn2")
            ffn_act(act, "ffn3", "mla", 15, with_ada["ffn3"])
            hybrid_act(act, order, 0, "ffn3")
            hybrid_act(act, order, 1, ("hy", 0))

        @block.vector
        def _(dve):
            order = Chain(dve, dve_own)
            for g in range(4):
                evac.give(dve.memset(eps[:, 2 * g:2 * g + 2], EPS), ("g", g))
            ysum.give(dve.memset(std[:], 0.0), "start")
            dve.wait_ge(small_loaded, 48)
            dve.wait_ge(value.sem, value.at("silu_c"))
            for j in range(2):
                for k in range(8):
                    ada_piece(dve, j, None, k)
                ada_close_dve(dve, j, None)
            split_lo(dve, 0)
            split_lo(dve, 1)
            ffn_dve(dve, order, "ffn0", gains(0, 0), 0, with_ada["ffn0"])
            pool_dve(dve, order, "pool", gains(0, 1))
            ffn_dve(dve, order, "ffn1", gains(0, 2), 6, with_ada["ffn1"])
            ffn_dve(dve, order, "ffn2", gains(1, 0), 9, with_ada["ffn2"])
            mla_dve(dve, order, "mla", gains(1, 1))
            ffn_dve(dve, order, "ffn3", gains(1, 2), 15, with_ada["ffn3"])
            hybrid_dve(dve, order, 0)
            hybrid_dve(dve, order, 1)



def mla_units(units, blocks, w_in, w_uq, w_uk, w_uv, w_o):
    f = np.float32
    rotary = np.tile(w_in[:, 384:416], (1, 4))
    latents = blocks(np.concatenate([w_in[:, :384], rotary], 1))
    nope = w_uq[:, :, :64].reshape(256, 1024)
    rope = w_uq[:, :, 64:].reshape(256, 512)
    lift = np.zeros((HEADS, P, P), f)
    project = np.zeros((HEADS, P, P), f)
    for h in range(HEADS):
        half = slice(64 * (h % 2), 64 * (h % 2) + 64)
        lift[h, half] = w_uk[:, h].T
        project[h, :, half] = w_uv[:, h]
    return [units(latents), units(blocks(nope)), units(blocks(rope)), units(lift[:8]),
            units(project[:8]), units(lift[8:]), units(project[8:]), units(blocks(w_o))]


def hybrid_units(units, blocks, w_in, cmp_w1, w_up_a, w_up_b, w_out):
    f = np.float32
    names = ("sb_q", "sb_k", "sb_v", "sb_z", "n_q", "n_kc", "n_vc", "n_ks", "n_vs", "n_kw", "n_vw",
             "n_gate", "n_z", "gate_a", "gate_b")
    widths = (512, 512, 512, 512, 512, 128, 128, 128, 128, 128, 128, 24, 512, D, D)
    w, start = {}, 0
    for name, n in zip(names, widths):
        w[name] = w_in[:, start:start + n]
        start += n

    def dense(m):
        return units(blocks(m))

    def paired(m):
        return m.reshape(-1, 2, 4, 64).transpose(0, 2, 1, 3).reshape(-1, 512)

    def by_rows(m, per):
        n = m.shape[1]
        b = m.reshape(NC, P, n)
        made = []
        for k in range(0, NC, per):
            part = b[k:k + per].transpose(1, 0, 2).reshape(P, -1)
            made.append(np.concatenate([part, np.zeros((P, UNIT - part.shape[1]), f)], 1))
        return np.stack(made)

    def both_halves(m):
        return np.concatenate([m[:, :64], m[:, :64], m[:, 64:], m[:, 64:]], 1)

    def hidden(m):
        return m.reshape(4, 4, P, 256).transpose(0, 2, 1, 3).reshape(4, P, UNIT)
    up_b = paired(w_up_b.T).T
    gate_a, gate_b, a, b = blocks(w["gate_a"]), blocks(w["gate_b"]), blocks(w_up_a), blocks(up_b)
    merge = units(np.concatenate([gate_a, gate_b, a, b], 1))
    nat2 = np.concatenate([w["n_vs"], w["n_vw"], w["n_gate"]], 1)
    return [dense(w["sb_q"]), dense(w["sb_k"]), by_rows(w["sb_v"], 2), dense(w["sb_z"]),
            dense(paired(w["n_q"])), dense(w["n_ks"]), dense(w["n_kw"]), dense(both_halves(w["n_kc"])),
            dense(both_halves(w["n_vc"])), dense(paired(w["n_z"])), by_rows(nat2, 3),
            hidden(cmp_w1[0]), hidden(cmp_w1[1]), merge, dense(w_out)]


def constants():
    f = np.float32
    eye = np.eye(P, dtype=f)
    r = np.arange(P)

    def rotation(width):
        m = np.zeros((P, P), f)
        m[r // width * width + (r + width // 2) % width, r] = 1
        return m
    same = (r[:, None] // 64 == r[None, :] // 64).astype(f)
    consts = np.concatenate([eye, np.ones((P, P), f), same, rotation(32), rotation(64)], 1)
    k, q = r[:, None], r[None, :]
    cmp_mask = np.zeros((P, 4, 32), f)
    t = np.arange(S).reshape(4, P).T[:, :, None]
    b = np.arange(32)[None, None, :]
    cmp_mask[(16 * b + 31 > t) | (b >= NCMP)] = NEG
    constsr = np.concatenate([eye, np.where(q > k, f(NEG), f(0)),
                              np.where(k >= q, f(NEG), f(0)),
                              np.where(k >= q, f(-1), f(0)), -np.ones((P, P), f),
                              cmp_mask.reshape(P, P)], 1)
    pos = np.arange(S)
    cnt = np.stack([1.0 / (np.minimum(pos + w // 2, S) - np.maximum(pos - w // 2, 0)) for w in (2, 4, 8, 16)])
    pool_count = np.broadcast_to(cnt.astype(f), (P, 4, S))
    inv = (1.0 / (f(10000.0) ** (np.arange(0, 32, 2, dtype=f) / f(32)))).astype(f)
    ang = (pos.astype(f)[:, None] * inv[None, :]).astype(f)
    cos, sin = np.cos(ang).astype(f).T, np.sin(ang).astype(f).T
    mla_rope = np.stack([np.tile(np.concatenate([cos, cos]), (4, 1)),
                         np.tile(np.concatenate([-sin, sin]), (4, 1))], 1)
    inv2 = (f(10000.0) ** (-np.arange(32, dtype=f) / f(32))).astype(f)
    sign = np.tile(np.concatenate([-np.ones(32, f), np.ones(32, f)]), 2)
    visible = (np.arange(S).reshape(4, P).T >= 31).astype(f)
    rope_cst = np.concatenate([np.tile(inv2, 4)[:, None], sign[:, None], visible], 1)
    return {"consts": consts, "constsr": constsr.astype(f), "pool_count": pool_count,
            "mla_rope": mla_rope, "rope_cst": rope_cst}


def kernel(x, c, ada_w, ada_b, norm_g, ffn_w_in, ffn_w_out, pool_w, pool_b, pool_scale, mla_w_in,
           mla_q_norm, mla_kv_norm, mla_w_uq, mla_w_uk, mla_w_uv, mla_w_o, positions_2, norm_g_2,
           w_in_2, q_norm_g_2, k_norm_g_2, cmp_pe_2, cmp_w1_2, cmp_b1_2, cmp_w2_2, w_up_a_2,
           w_up_b_2, w_out_2):
    import concourse.bacc as bacc
    from concourse.bass_utils import run_bass_kernel_spmd

    f = np.float32

    def a_(v):
        return np.asarray(v)

    def blocks(w):
        k, n = w.shape
        return w.reshape(k // P, P, n // P, P).transpose(2, 0, 1, 3)

    def units(b):
        b = b.reshape(-1, P, P)
        n = -(-len(b) // 8)
        if len(b) % 8:
            b = np.concatenate([b, np.zeros((8 * n - len(b), P, P), f)])
        return b.reshape(n, 8, P, P).transpose(0, 2, 1, 3).reshape(n, P, UNIT)

    def ffn_units(layer, sub):
        w_in, w_out = a_(ffn_w_in)[layer, sub], a_(ffn_w_out)[layer, sub]
        gate, up = blocks(w_in[:, :FF]), blocks(w_in[:, FF:])
        first = units(np.stack([gate, up], 1))
        down = blocks(w_out)
        second = np.concatenate([units(down[n]) for n in range(NC)])
        return [first, second]

    def pool_units():
        w = a_(pool_w)[0]
        return [units(np.concatenate([blocks(w[g]) for g in range(4)]))]

    stages = ffn_units(0, 0) + pool_units() + ffn_units(0, 1) + ffn_units(1, 0)
    stages += mla_units(units, blocks, *(a_(v)[0] for v in (mla_w_in, mla_w_uq, mla_w_uk, mla_w_uv, mla_w_o)))
    stages += ffn_units(1, 1)
    for layer in range(2):
        stages += hybrid_units(units, blocks, *(a_(v)[layer] for v in (w_in_2, cmp_w1_2, w_up_a_2, w_up_b_2, w_out_2)))
    stream = np.concatenate(stages)

    def columns(v):
        return a_(v).reshape(-1, P).T

    doubled = lambda v: np.concatenate([v, v], -1)
    params = np.concatenate([
        columns(c), columns(ada_b), columns(norm_g), columns(pool_b), columns(pool_scale),
        columns(mla_q_norm), columns(mla_kv_norm), columns(norm_g_2), columns(doubled(a_(q_norm_g_2))),
        columns(doubled(a_(k_norm_g_2))), columns(cmp_b1_2), columns(cmp_pe_2)], 1)
    ada = a_(ada_w).reshape(2, NC, P, 9, D).transpose(0, 3, 1, 2, 4).reshape(144, P, D)
    xT = a_(x)[0].T.reshape(NC, P, S).transpose(1, 0, 2)

    tables = constants()
    inputs = {"stream": stream, "ada": ada, "xT": xT, "params": params}
    inputs.update(tables)
    inputs["pos"] = np.broadcast_to(a_(positions_2), (P, S))
    w2 = a_(cmp_w2_2).reshape(2, 2, 2, P, 64)
    gap = np.zeros((2, 2, P, 64), f)
    inputs["w2"] = np.concatenate([gap, w2[:, 0], gap, w2[:, 1]], -1).transpose(0, 2, 1, 3)

    nc = bacc.Bacc("TRN2", target_bir_lowering=False, num_devices=1)
    arrays, aps = {}, {}
    for name, v in inputs.items():
        arrays[name + "_in"] = np.ascontiguousarray(v)
        aps[name] = nc.dram_tensor(name + "_in", v.shape, mybir.dt.from_np(v.dtype),
                                   kind="ExternalInput").ap()
    out = nc.dram_tensor("out_x", (P, NC, S), F32, kind="ExternalOutput").ap()
    kernel_program(nc, out=out, NU=len(stream), **aps)
    r = run_bass_kernel_spmd(nc, [arrays], core_ids=[0])
    return r.results[0]["out_x"].transpose(2, 1, 0).reshape(1, S, D)
```

```python
from contextlib import ExitStack
import numpy as np

import concourse.bass as bass
from concourse import mybir

ALU = mybir.AluOpType
ACT = mybir.ActivationFunctionType
AXX = mybir.AxisListType.X
F32 = mybir.dt.float32
F32R = mybir.dt.float32r
I32 = mybir.dt.int32

P = 128
D = 1024
S = 512
NC = D // P
FF = 2816
NF = FF // P
UNIT = NC * P
RAW, RING, LEAD = 2, 4, 2
HEADS = 16
EPS = 1e-6
ATTN_SCALE = 96 ** -0.5
NEG = -1e30
NCMP = 31
NAT2 = 280


class Signal:

    def __init__(self, sem):
        self.sem, self.values, self.planned, self.given = sem, {}, 0, 0

    def plan(self, *labels):
        for label in labels:
            assert label not in self.values, label
            self.planned += 1
            self.values[label] = self.planned

    def plan_loop(self, label, total):
        self.values[label] = self.planned
        self.planned += total

    def at(self, label):
        return self.values[label]

    def give(self, instruction, label):
        self.given += 1
        assert self.values[label] == self.given, (label, self.values[label], self.given)
        instruction.then_inc(self.sem, 1)

    def give_loop(self, label, total):
        assert self.values[label] == self.given, label
        self.given += total


class Chain:

    def __init__(self, engine, sem):
        self.engine, self.sem, self.n = engine, sem, 0

    def link(self, instruction):
        instruction.then_inc(self.sem, 1)
        self.n += 1

    def sync(self):
        self.engine.wait_ge(self.sem, self.n)

    def step(self, instruction):
        self.link(instruction)
        self.sync()


class Columns:

    def __init__(self):
        self.at, self.n = {}, 0

    def add(self, name, n):
        self.at[name] = self.n
        self.n += n


def param_columns():
    c = Columns()
    for name, n in (("c", 8), ("ada_b", 144), ("norm_g", 96), ("pool_b", 8), ("pool_scale", 8),
                    ("q_norm", 2), ("kv_norm", 1), ("norm_g_2", 16), ("q_norm_2", 2),
                    ("k_norm_2", 6), ("cmp_b1", 8), ("cmp_pe", 64)):
        c.add(name, n)
    return c


IDENT, ONES, ONES64, PERM32, PERM64 = range(5)
R_IDENT, R_CAUSAL, R_STRICT_T, R_NEGTRI, R_NEGONES, R_NEG31 = range(6)
NCONSTR = 6


def kernel_program(nc, stream, ada, xT, params, consts, constsr, pool_count, mla_rope, rope_cst,
                   pos, w2, out, NU):
    col = param_columns()
    with ExitStack() as ctx:
        top = [(nc.sbuf_base + 63) // 64 * 64]

        def at(name, shape, dt=F32):
            size = 4 * int(np.prod(shape[1:]))
            made = nc.alloc_sbuf_tensor_at(name, shape, dt, offset=top[0])
            top[0] += (size + 31) // 32 * 32
            return made

        X = at("X", [P, NC, S])
        raw = at("raw", [P, RAW, UNIT])
        w_hi = at("w_hi", [P, RING, UNIT], F32R)
        w_lo = at("w_lo", [P, RING, UNIT], F32R)
        sq_base = top[0]
        sq = at("sq", [P, 2, S])
        std = at("std", [P, S])
        rstd = at("rstd", [P, S])
        ta_base = top[0]
        ta = at("ta", [P, 2, S])
        tb = at("tb", [P, 2, S])
        par = at("par", [P, col.n])
        mod_base = top[0]
        mod = at("mod", [P, 18, NC])
        acol = at("acol", [P, NC])
        bcol = at("bcol", [P, NC])
        silu_c = at("silu_c", [P, NC])
        eps = at("eps", [P, 8])
        warm = at("warm", [P, 1])
        small = at("small", [P, 4, 4])
        ones = at("ones", [P, P])
        h_base = top[0]
        h_hi = at("h_hi", [P, NC, S], F32R)
        h_lo = at("h_lo", [P, NC, S], F32R)
        region = top[0]
        top[0] = h_base
        y_ffn = at("y_ffn", [P, NC, S])
        top[0] = h_base
        pt2_hi = at("pt2_hi", [P, 2, 4, S], F32R)
        pt2_lo = at("pt2_lo", [P, 2, 4, S], F32R)
        top[0] = region
        a_hi = at("a_hi", [P, NF, S], F32R)
        a_lo = at("a_lo", [P, NF, S], F32R)
        ada_first = nc.alloc_sbuf_tensor_at("ada_first", [P, 2 * NC, D], F32, offset=region)
        ada_raw = at("ada_raw", [P, 2, D])
        ada_acc = at("ada_acc", [P, D])
        top[0] = region
        hp = at("hp", [P, 2, S + 16])
        win = at("win", [P, 2, S + 16])
        y_pool = at("y_pool", [P, NC, S])
        cnt = at("cnt", [P, 4, S])

        psum = ctx.enter_context(nc.psum_tensor("psum", [P, 8, S], F32))

        def sem(name):
            return ctx.enter_context(nc.semaphore(name))

        raw_loaded = [sem("raw_loaded%d" % i) for i in range(RAW)]
        ada_loaded = [sem("ada_loaded%d" % i) for i in range(2)]
        small_loaded = sem("small_loaded")
        x_loaded = sem("x_loaded")
        first_loaded = [sem("first_loaded%d" % i) for i in range(4)]
        stage_loaded = sem("stage_loaded")
        hi_ready, lo_ready = sem("hi_ready"), sem("lo_ready")
        ada_used, ada_sum, mod_ready = sem("ada_used"), sem("ada_sum"), sem("mod_ready")
        preloaded = sem("preloaded")
        stored = sem("stored")
        act_own, dve_own = sem("act_own"), sem("dve_own")
        prod = Signal(sem("products"))
        evac = Signal(sem("evacuated"))
        evac_hi = Signal(sem("evacuated_hi"))
        sq_ready = Signal(sem("squares"))
        sums = Signal(sem("sums"))
        ysum = Signal(sem("square_sums"))
        std_ready = Signal(sem("std_ready"))
        rstd_ready = Signal(sem("rstd_ready"))
        x_ready = Signal(sem("x_ready"))
        scaled = Signal(sem("scaled"))
        part_hi = Signal(sem("part_hi"))
        h_ready = Signal(sem("h_ready"))
        value = Signal(sem("values"))

        ysum.plan("start")
        own = {}

        def bank(g):
            return psum[:, g % 4]

        class Cursor:
            u, g, last_norm = 0, 4, None

        cur = Cursor()
        evac.plan(*[("g", g) for g in range(4)])

        def plan_unit(*groups):
            prod.plan(("u", cur.u))
            for g in groups:
                prod.values[("g", g)] = prod.planned
            cur.u += 1

        def plan_norm(L, n):
            for c in range(n):
                sq_ready.plan((L, c))
                sums.plan((L, c))
            own[L, "before"] = cur.last_norm
            cur.last_norm = L
            std_ready.plan(L)
            rstd_ready.plan(L)

        def plan_ynorm(L):
            ysum.plan((L, "zero"))
            sq_ready.plan_loop(L, NC)
            ysum.plan_loop(L, NC)
            sums.plan(L)
            own[L, "before"] = cur.last_norm
            cur.last_norm = L
            std_ready.plan(L)
            rstd_ready.plan(L)

        def plan_pre(L, split=True):
            plan_norm((L, "pre"), NC)
            if split:
                for c in range(NC):
                    scaled.plan((L, c))
                    part_hi.plan((L, c))
                    h_ready.plan((L, c))

        def plan_post(L):
            for c in range(NC):
                x_ready.plan((L, c))

        def plan_ffn(L):
            own[L, "u"], own[L, "g"] = cur.u, cur.g
            plan_pre(L)
            for k in range(2 * NF):
                prod.values[("u", cur.u + k)] = prod.values[("g", cur.g + k)] = prod.planned + k + 1
            prod.planned += 4
            prod.plan_loop((L, "gate_up"), 2 * NF - 4)
            for k in range(2 * NF):
                evac.values[("g", cur.g + k)] = evac.planned + k + 1
            evac.plan_loop((L, "gate_up"), 2 * NF)
            value.plan_loop((L, "silu"), NF)
            part_hi.plan_loop((L, "a"), NF)
            cur.u += 2 * NF
            cur.g += 2 * NF
            for k in range(24):
                prod.values[("u", cur.u + k)] = prod.planned + k + 1
            for n in range(NC):
                prod.values[("g", cur.g + n)] = prod.planned + 3 * n + 3
                evac.values[("g", cur.g + n)] = evac.planned + n + 1
            prod.plan_loop((L, "down"), 24)
            evac.plan_loop((L, "down"), NC)
            plan_ynorm((L, "post"))
            cur.u += 24
            cur.g += NC
            plan_post(L)

        def plan_pool(L):
            own[L, "u"], own[L, "g"] = cur.u, cur.g
            plan_pre(L)
            plan_ynorm((L, "post"))
            for c in range(NC):
                if c % 4 == 3:
                    plan_unit(cur.g)
                else:
                    prod.plan(("g", cur.g))
                evac.plan(("g", cur.g))
                cur.g += 1
            plan_post(L)

        def split_hi(act, u):
            if u >= NU:
                return
            act.wait_ge(raw_loaded[u % RAW], 16 * (u // RAW + 1))
            if u >= RING:
                act.wait_ge(prod.sem, prod.at(("u", u - RING)))
            act.activation(w_hi[:, u % RING], raw[:, u % RAW], ACT.Copy).then_inc(hi_ready, 1)

        def split_lo(dve, u):
            if u >= NU:
                return
            dve.wait_ge(hi_ready, u + 1)
            dve.tensor_tensor(w_lo[:, u % RING], raw[:, u % RAW], w_hi[:, u % RING].bitcast(F32),
                              ALU.subtract).then_inc(lo_ready, 1)

        def split_hi_loop(act, i, per, u, products):
            act.wait_ge(raw_loaded[u % RAW], i * (16 * per // RAW) + 16 * (u // RAW + 1))
            act.wait_ge(prod.sem, products)
            act.activation(w_hi[:, u % RING], raw[:, u % RAW], ACT.Copy).then_inc(hi_ready, 1)

        def split_lo_loop(dve, i, per, u):
            dve.wait_ge(hi_ready, i * per + (u + 1))
            dve.tensor_tensor(w_lo[:, u % RING], raw[:, u % RAW], w_hi[:, u % RING].bitcast(F32),
                              ALU.subtract).then_inc(lo_ready, 1)

        def three_passes(pe, dst, weights, moving, first=True, last=True, skip=False):
            n, total = 0, 3 * len(weights)
            for wi, mi in ((0, 0), (1, 0), (0, 1)):
                for w, m in zip(weights, moving):
                    mm = pe.matmul(dst, w[wi], m[mi], start=(first and n == 0),
                                   stop=(last and n == total - 1), skip_group_check=skip)
                    n += 1
            return mm

        def unit_blocks(u, blocks, width=P):
            s = u % RING
            return [(w_hi[:, s, b * width:(b + 1) * width], w_lo[:, s, b * width:(b + 1) * width])
                    for b in blocks]

        def chunks_of(hi, lo, ks):
            return [(hi[:, k], lo[:, k]) for k in ks]

        def free_bank(pe, g):
            pe.wait_ge(evac.sem, evac.at(("g", g - 4)))

        def dense_first(pe, L, u, g):
            pe.wait_ge(lo_ready, u + 2)
            free_bank(pe, g)
            free_bank(pe, g + 1)
            for k in range(NC):
                pe.wait_ge(h_ready.sem, h_ready.at((L, k)))
                for m in range(2):
                    mm = three_passes(pe, bank(g + m), unit_blocks(u + m, [k]), chunks_of(h_hi, h_lo, [k]),
                                      first=(k == 0), last=(k == NC - 1))
                    if k == NC - 1:
                        prod.give(mm, ("u", u + m))

        def dense(pe, u, g):
            pe.wait_ge(lo_ready, u + 1)
            free_bank(pe, g)
            mm = three_passes(pe, bank(g), unit_blocks(u, range(NC)), chunks_of(h_hi, h_lo, range(NC)))
            prod.give(mm, ("u", u))

        class Preload:
            count = 0

        def preload(act, function):
            if Preload.count:
                act.wait_ge(preloaded, Preload.count)
            act.activation(warm[:], eps[:, 0:1], function).then_inc(preloaded, 1)
            Preload.count += 1

        def norm_act(act, L, sources, n_of, width=S):
            for c, (src, wait) in enumerate(sources):
                if wait:
                    act.wait_ge(*wait)
                if c >= 2:
                    act.wait_ge(sums.sem, sums.at((L, c - 2)))
                v = sq_ready.at((L, c))
                sq_ready.give(act.activation(sq[:, v % 2, :width], src, ACT.Square), (L, c))
            act.wait_ge(sums.sem, sums.at((L, len(sources) - 1)))
            root_act(act, L, n_of, width)

        def root_act(act, L, n_of, width=S):
            if own[L, "before"] is not None:
                act.wait_ge(rstd_ready.sem, rstd_ready.at(own[L, "before"]))
            std_ready.give(act.activation(std[:, :width], psum[:, 7, :width], ACT.Sqrt,
                                          scale=1.0 / n_of, bias=eps[:, 0:1]), L)

        def norm_pe(pe, L, n, matrix, width=S):
            if own[L, "before"] is not None:
                pe.wait_ge(std_ready.sem, std_ready.at(own[L, "before"]))
            for c in range(n):
                v = sq_ready.at((L, c))
                pe.wait_ge(sq_ready.sem, v)
                sums.give(pe.matmul(psum[:, 7, :width], matrix, sq[:, v % 2, :width],
                                    start=(c == 0), stop=(c == n - 1)), (L, c))

        def norm_dve(dve, L, width=S):
            dve.wait_ge(std_ready.sem, std_ready.at(L))
            rstd_ready.give(dve.reciprocal(rstd[:, :width], std[:, :width]), L)
            dve.wait_ge(rstd_ready.sem, rstd_ready.at(L))

        def ynorm_pe(pe, L):
            pe.wait_ge(ysum.sem, ysum.at(L) + NC)
            pe.wait_ge(std_ready.sem, std_ready.at(own[L, "before"]))
            sums.give(pe.matmul(psum[:, 7], ones[:], std[:], start=True, stop=True), L)

        def pre_act(act, L, before, shift=None, split=True, norm=True):
            if norm:
                norm_act(act, (L, "pre"), [(X[:, c], (x_ready.sem, x_ready.at((before, c))))
                                           for c in range(NC)], D)
            if split:
                for c in range(NC):
                    act.wait_ge(scaled.sem, scaled.at((L, c)))
                    if shift is None:
                        op = act.activation(h_hi[:, c], tb[:, c % 2], ACT.Copy)
                    else:
                        op = act.activation(h_hi[:, c], tb[:, c % 2], ACT.Identity,
                                            bias=mod[:, shift, c:c + 1])
                    part_hi.give(op, (L, c))

        def pre_dve(dve, own_order, L, gains, scale=None, shift=None, split=True, norm=True):
            if scale is not None:
                dve.wait_ge(mod_ready, scale + 1)
                own_order.step(dve.scalar_tensor_tensor(out=acol[:], in0=mod[:, scale], scalar=1.0,
                                                        in1=gains, op0=ALU.add, op1=ALU.mult))
                a = acol
            if norm:
                norm_dve(dve, (L, "pre"))

            def scale_chunk(c):
                a = acol[:, c:c + 1] if scale is not None else gains[:, c:c + 1]
                if c >= 2:
                    dve.wait_ge(h_ready.sem, h_ready.at((L, c - 2)))
                scaled.give(dve.scalar_tensor_tensor(out=tb[:, c % 2], in0=X[:, c], scalar=a,
                                                     in1=rstd[:], op0=ALU.mult, op1=ALU.mult), (L, c))
            if split:
                scale_chunk(0)
                for c in range(NC):
                    if c + 1 < NC:
                        scale_chunk(c + 1)
                    dve.wait_ge(part_hi.sem, part_hi.at((L, c)))
                    if shift is None:
                        op = dve.tensor_tensor(h_lo[:, c], tb[:, c % 2], h_hi[:, c].bitcast(F32),
                                               ALU.subtract)
                    else:
                        op = dve.scalar_tensor_tensor(out=h_lo[:, c], in0=tb[:, c % 2],
                                                      scalar=mod[:, shift, c:c + 1],
                                                      in1=h_hi[:, c].bitcast(F32), op0=ALU.add,
                                                      op1=ALU.subtract)
                    h_ready.give(op, (L, c))

        def add_square(dve, n, q0, y0):
            dve.wait_ge(sq_ready.sem, q0 + n + 1)
            dve.wait_ge(ysum.sem, y0 + n)
            dve.tensor_tensor(std[:], std[:], sq[:, (q0 + n) % 2], ALU.add).then_inc(ysum.sem, 1)

        def post_act(act, L):
            act.wait_ge(sums.sem, sums.at((L, "post")))
            root_act(act, (L, "post"), D)

        def post_dve(dve, own_order, L, y, gains, gate, weight):
            dve.wait_ge(mod_ready, gate + 1)
            own_order.step(dve.scalar_tensor_tensor(out=bcol[:], in0=mod[:, gate], scalar=1.0,
                                                    in1=gains, op0=ALU.add, op1=ALU.mult))
            norm_dve(dve, (L, "post"))

            def scale_chunk(c):
                if c >= 2:
                    dve.wait_ge(x_ready.sem, x_ready.at((L, c - 2)))
                own_order.link(dve.scalar_tensor_tensor(out=ta[:, c % 2], in0=y[:, c],
                                                        scalar=bcol[:, c:c + 1], in1=rstd[:],
                                                        op0=ALU.mult, op1=ALU.mult))
            for c in range(NC):
                scale_chunk(c)
                own_order.sync()
                x_ready.give(dve.scalar_tensor_tensor(out=X[:, c], in0=ta[:, c % 2], scalar=weight,
                                                      in1=X[:, c], op0=ALU.mult, op1=ALU.add), (L, c))

        def ada_rows(dve, j, i, ks):
            for k in ks:
                t = NC * j + k
                if i is None:
                    if t % 4 == 0:
                        dve.wait_ge(first_loaded[t // 4], 16)
                    if t:
                        dve.wait_ge(ada_used, t)
                    src = ada_first[:, t]
                else:
                    dve.wait_ge(ada_loaded[k % 2], i * 64 + 16 * ((t - 2 * NC) // 2 + 1))
                    dve.wait_ge(ada_used, i * NC + t)
                    src = ada_raw[:, k % 2]
                if k == 0:
                    op = dve.tensor_scalar(ada_acc[:], src, silu_c[:, 0:1], None, ALU.mult)
                else:
                    op = dve.scalar_tensor_tensor(out=ada_acc[:], in0=src, scalar=silu_c[:, k:k + 1],
                                                  in1=ada_acc[:], op0=ALU.mult, op1=ALU.add)
                op.then_inc(ada_used, 1)

        def ada_close_pe(pe, j, i):
            if i is None:
                pe.wait_ge(ada_used, NC * j + NC)
                if j:
                    pe.wait_ge(mod_ready, j)
            else:
                pe.wait_ge(ada_used, i * NC + (NC * j + NC))
                pe.wait_ge(mod_ready, i + j)
            for n in range(NC):
                mm = pe.matmul(psum[:, 6, n:n + 1], ada_acc[:, n * P:(n + 1) * P], ones[:, 0:1],
                               start=True, stop=True)
            mm.then_inc(ada_sum, 1)

        def ada_close_dve(dve, j, i):
            b = col.at["ada_b"]
            if i is None:
                dve.wait_ge(ada_sum, j + 1)
                dve.tensor_tensor(mod[:, j], psum[:, 6, 0:NC], par[:, b + NC * j:b + NC * (j + 1)],
                                  ALU.add).then_inc(mod_ready, 1)
            else:
                dve.wait_ge(ada_sum, i + (j + 1))
                dve.tensor_tensor(mod[:, bass.ds(i + j, 1), :].rearrange("p a n -> p (a n)"),
                                  psum[:, 6, 0:NC], par[:, bass.ds(i * NC + (b + NC * j), NC)],
                                  ALU.add).then_inc(mod_ready, 1)

        ADA_ROWS = (range(0, 3), range(3, 6), range(6, 8), ())

        def ffn_pe(pe, L, segments, j2):
            u0, g0 = own[L, "u"], own[L, "g"]
            norm_pe(pe, (L, "pre"), NC, ones[:])
            if L == "ffn0":
                ada_close_pe(pe, 0, None)
                ada_close_pe(pe, 1, None)
            dense_first(pe, L, u0, g0)
            dense(pe, u0 + 2, g0 + 2)
            dense(pe, u0 + 3, g0 + 3)
            b = 4
            for times, j in segments:
                with pe.Fori(0, times) as i:
                    for k in range(8):
                        pe.wait_ge(lo_ready, i * 8 + (u0 + b + k + 1))
                        pe.wait_ge(evac.sem, i * 8 + (g0 + b + k - 4 + 1))
                        three_passes(pe, bank(g0 + k), unit_blocks(u0 + k, range(NC)),
                                     chunks_of(h_hi, h_lo, range(NC))).then_inc(prod.sem, 1)
                        if j is not None and k == 6:
                            ada_close_pe(pe, j, i)
                b += 8 * times
            prod.give_loop((L, "gate_up"), 2 * NF - 4)
            u1, g1 = u0 + 2 * NF, g0 + 2 * NF
            pe.wait_ge(evac.sem, evac.at(("g", g1 - 7)))
            with pe.Fori(0, 2) as i:
                for n in range(4):
                    for m in range(3):
                        ks = range(8 * m, min(8 * m + 8, NF))
                        pe.wait_ge(lo_ready, i * 12 + (u1 + 3 * n + m + 1))
                        if m == 0:
                            pe.wait_ge(evac.sem, i * 4 + (g1 + n - 4 + 1))
                        if n == 0 and m == 2:
                            pe.wait_ge(evac.sem, evac.at(("g", g1 - 1)))
                        three_passes(pe, bank(g1 + n), unit_blocks(u1 + 3 * n + m, range(len(ks))),
                                     chunks_of(a_hi, a_lo, ks), first=(m == 0),
                                     last=(m == 2)).then_inc(prod.sem, 1)
                        if j2 is not None and n == 3 and m == 0:
                            ada_close_pe(pe, j2, i)
            prod.give_loop((L, "down"), 24)
            ynorm_pe(pe, (L, "post"))

        def ffn_act(act, L, before, shift, segments):
            u0, g0 = own[L, "u"], own[L, "g"]
            if before is not None:
                norm_act(act, (L, "pre"), [(X[:, c], (x_ready.sem, x_ready.at((before, c)))) for c in range(NC)], D)
            preload(act, ACT.Silu)
            pre_act(act, L, before, shift, norm=False)
            base = prod.at(("u", u0)) - 1

            def pair(i, q):
                s = q % 2
                step = (lambda per, v: v) if i is None else (lambda per, v: i * per + v)
                for m in range(2):
                    if i is None:
                        split_hi(act, u0 + 2 * q + m + LEAD)
                    else:
                        split_hi_loop(act, i, 8, u0 + 2 * q + m + LEAD, i * 8 + (base + 2 * q + m - 1))
                act.wait_ge(prod.sem, step(8, base + 2 * q + 1))
                act.wait_ge(evac.sem, step(8, g0 + 2 * q - 4 + 1))
                act.activation(ta[:, s], bank(g0 + 2 * q), ACT.Silu).then_inc(value.sem, 1)
                act.wait_ge(evac.sem, step(8, g0 + 2 * q + 1))
                dst = a_hi[:, q] if i is None else a_hi[:, bass.ds(i * 4 + q, 1), :].rearrange("p a n -> p (a n)")
                act.activation(dst, tb[:, s], ACT.Copy).then_inc(part_hi.sem, 1)
            for q in range(2):
                pair(None, q)
            b = 2
            for times, j in segments:
                with act.Fori(0, times) as i:
                    for q in range(4):
                        pair(i, b + q)
                b += 4 * times
            value.give_loop((L, "silu"), NF)
            part_hi.give_loop((L, "a"), NF)
            u1, g1, base = u0 + 2 * NF, g0 + 2 * NF, prod.at((L, "down"))
            q0, y0 = sq_ready.at((L, "post")), ysum.at((L, "post"))
            preload(act, ACT.Sqrt)
            with act.Fori(0, 2) as i:
                for n in range(4):
                    for m in range(3):
                        k = 3 * n + m
                        split_hi_loop(act, i, 12, u1 + k + LEAD, i * 12 + (base + k - 1))
                    act.wait_ge(evac.sem, i * 4 + (g1 + n + 1))
                    act.wait_ge(ysum.sem, i * 4 + (y0 + n - 1))
                    act.activation(sq[:, (q0 + n) % 2],
                                   y_ffn[:, bass.ds(i * 4 + n, 1), :].rearrange("p a n -> p (a n)"),
                                   ACT.Square).then_inc(sq_ready.sem, 1)
            sq_ready.give_loop((L, "post"), NC)
            post_act(act, L)

        def ffn_dve(dve, own_order, L, gains, mods, segments, j2):
            u0, g0 = own[L, "u"], own[L, "g"]
            pre_dve(dve, own_order, L, gains(0), scale=mods + 1, shift=mods, norm=(L != "ffn0"))
            base = prod.at(("u", u0)) - 1
            v0, p0 = value.at((L, "silu")), part_hi.at((L, "a"))

            def pair(i, q, j, rows):
                s = q % 2
                step = (lambda per, v: v) if i is None else (lambda per, v: i * per + v)
                for m in range(2):
                    if i is None:
                        split_lo(dve, u0 + 2 * q + m + LEAD)
                    else:
                        split_lo_loop(dve, i, 8, u0 + 2 * q + m + LEAD)
                if j is not None:
                    ada_rows(dve, j, i, rows)
                dve.wait_ge(value.sem, step(4, v0 + q + 1))
                dve.wait_ge(prod.sem, step(8, base + 2 * q + 2))
                dve.wait_ge(evac.sem, step(8, g0 + 2 * q - 2))
                dve.tensor_tensor(tb[:, s], ta[:, s], bank(g0 + 2 * q + 1), ALU.mult).then_inc(evac.sem, 1)
                dve.wait_ge(part_hi.sem, step(4, p0 + q + 1))
                f = slice(q, q + 1) if i is None else bass.ds(i * 4 + q, 1)
                dve.tensor_tensor(a_lo[:, f, :].rearrange("p a n -> p (a n)"), tb[:, s],
                                  a_hi[:, f, :].bitcast(F32).rearrange("p a n -> p (a n)"),
                                  ALU.subtract).then_inc(evac.sem, 1)
            for q in range(2):
                pair(None, q, None, ())
            b = 2
            for times, j in segments:
                with dve.Fori(0, times) as i:
                    for q in range(4):
                        pair(i, b + q, j, ADA_ROWS[q])
                    if j is not None:
                        ada_close_dve(dve, j, i)
                b += 4 * times
            evac.give_loop((L, "gate_up"), 2 * NF)
            u1, g1, base = u0 + 2 * NF, g0 + 2 * NF, prod.at((L, "down"))
            q0, y0 = sq_ready.at((L, "post")), ysum.at((L, "post"))
            ysum.give(dve.memset(std[:], 0.0), ((L, "post"), "zero"))
            with dve.Fori(0, 2) as i:
                for n in range(4):
                    for m in range(3):
                        split_lo_loop(dve, i, 12, u1 + 3 * n + m + LEAD)
                    if j2 is not None:
                        ada_rows(dve, j2, i, ADA_ROWS[n])
                    dve.wait_ge(prod.sem, i * 12 + (base + 3 * n + 3))
                    dve.tensor_copy(y_ffn[:, bass.ds(i * 4 + n, 1), :].rearrange("p a n -> p (a n)"),
                                    bank(g1 + n)).then_inc(evac.sem, 1)
                    dve.wait_ge(sq_ready.sem, i * 4 + (q0 + n + 1))
                    dve.wait_ge(ysum.sem, i * 4 + (y0 + n))
                    dve.tensor_tensor(std[:], std[:], sq[:, (q0 + n) % 2], ALU.add).then_inc(ysum.sem, 1)
                if j2 is not None:
                    ada_close_dve(dve, j2, i)
            evac.give_loop((L, "down"), NC)
            ysum.give_loop((L, "post"), NC)
            post_dve(dve, own_order, L, y_ffn, gains(1), mods + 2, 0.5)

        def pool_pe(pe, L):
            norm_pe(pe, (L, "pre"), NC, ones[:])
            u, g = own[L, "u"], own[L, "g"]
            for c in range(NC):
                group = 2 * (c // 2)
                if c % 4 == 0:
                    pe.wait_ge(lo_ready, u + c // 4 + 1)
                pe.wait_ge(h_ready.sem, h_ready.at((L, group + 1)))
                free_bank(pe, g + c)
                mm = three_passes(pe, bank(g + c), unit_blocks(u + c // 4, (2 * (c % 4), 2 * (c % 4) + 1)),
                                  chunks_of(h_hi, h_lo, (group, group + 1)))
                prod.give(mm, ("u", u + c // 4) if c % 4 == 3 else ("g", g + c))
            ynorm_pe(pe, (L, "post"))

        def pool_act(act, L, before):
            act.wait_ge(x_ready.sem, x_ready.at((before, 0)))
            act.dma_start(cnt[:], pool_count).then_inc(stage_loaded, 16)
            norm_act(act, (L, "pre"), [(X[:, c], (x_ready.sem, x_ready.at((before, c)))) for c in range(NC)], D)
            for c in range(NC):
                act.wait_ge(scaled.sem, scaled.at((L, c)))
                part_hi.give(act.activation(h_hi[:, c], tb[:, c % 2], ACT.Copy), (L, c))
            u, g = own[L, "u"], own[L, "g"]
            split_hi(act, u + 2)
            split_hi(act, u + 3)
            q0, y0 = sq_ready.at((L, "post")), ysum.at((L, "post"))
            for c in range(NC):
                act.wait_ge(evac.sem, evac.at(("g", g + c)))
                if c >= 2:
                    act.wait_ge(ysum.sem, y0 + c - 1)
                act.activation(sq[:, (q0 + c) % 2], y_pool[:, c], ACT.Square).then_inc(sq_ready.sem, 1)
            sq_ready.give_loop((L, "post"), NC)
            post_act(act, L)

        def pool_dve(dve, own_order, L, gains):
            dve.wait_ge(mod_ready, 5)
            own_order.step(dve.scalar_tensor_tensor(out=acol[:], in0=mod[:, 4], scalar=1.0,
                                                    in1=gains(0), op0=ALU.add, op1=ALU.mult))
            own_order.link(dve.memset(hp[:, :, 0:8], 0.0))
            own_order.step(dve.memset(hp[:, :, S + 8:S + 16], 0.0))
            norm_dve(dve, (L, "pre"))
            dve.wait_ge(stage_loaded, 16)
            body = slice(8, S + 8)

            def lo_half(c):
                dve.wait_ge(part_hi.sem, part_hi.at((L, c)))
                h_ready.give(dve.tensor_tensor(h_lo[:, c], tb[:, c % 2], h_hi[:, c].bitcast(F32),
                                               ALU.subtract), (L, c))
            for c in range(NC):
                h = hp[:, c % 2]
                own_order.step(dve.scalar_tensor_tensor(out=ta[:, 0], in0=X[:, c], scalar=acol[:, c:c + 1],
                                                        in1=rstd[:], op0=ALU.mult, op1=ALU.mult))
                own_order.step(dve.tensor_scalar(h[:, body], ta[:, 0], mod[:, 3, c:c + 1], None, ALU.add))
                own_order.step(dve.tensor_tensor(win[:, 0, 1:S + 16], h[:, 0:S + 15], h[:, 1:S + 16], ALU.add))
                have, first, end = 0, 1, S + 16
                for level in range(c // 2):
                    half = 1 << level
                    first, end = first + half, end - half
                    own_order.step(dve.tensor_tensor(win[:, 1 - have, first:end],
                                                     win[:, have, first - half:end - half],
                                                     win[:, have, first + half:end + half], ALU.add))
                    have = 1 - have
                own_order.step(dve.tensor_tensor(ta[:, 1], win[:, have, body], cnt[:, c // 2], ALU.mult))
                scaled.give(dve.tensor_tensor(tb[:, c % 2], ta[:, 1], h[:, body], ALU.subtract), (L, c))
                if c:
                    lo_half(c - 1)
            lo_half(NC - 1)
            u, g = own[L, "u"], own[L, "g"]
            split_lo(dve, u + 2)
            split_lo(dve, u + 3)
            q0, y0 = sq_ready.at((L, "post")), ysum.at((L, "post"))
            ysum.give(dve.memset(std[:], 0.0), ((L, "post"), "zero"))
            b, s = col.at["pool_b"], col.at["pool_scale"]
            for c in range(NC):
                dve.wait_ge(prod.sem, prod.at(("g", g + c)))
                evac.give(dve.tensor_scalar(y_pool[:, c], bank(g + c), par[:, b + c:b + c + 1],
                                            par[:, s + c:s + c + 1], ALU.add, ALU.mult), ("g", g + c))
                if c:
                    add_square(dve, c - 1, q0, y0)
            add_square(dve, NC - 1, q0, y0)
            ysum.give_loop((L, "post"), NC)
            post_dve(dve, own_order, L, y_pool, gains(1), 5, 1.0)

        def plan_softmax(L, A):
            for k in range(4 * A["tasks"]):
                for signal in (scores, peak, probs, probs_scaled, turned, turned_hi, turned_lo):
                    signal.plan((L, k))

        def softmax_pe(pe, L, A, extra):
            last = 4 * A["tasks"]

            def do_scores(k):
                if k >= last:
                    return
                t, i = divmod(k, 4)
                if k >= 2:
                    pe.wait_ge(probs.sem, probs.at((L, k - 2)))
                scores.give(A["scores"](pe, t, i, psum[:, 4 + k % 2, 0:A["width"](t, i)]), (L, k))

            def turn(k):
                t, i = divmod(k, 4)
                pe.wait_ge(probs_scaled.sem, probs_scaled.at((L, k)))
                if k >= 2:
                    pe.wait_ge(turned_lo.sem, turned_lo.at((L, k - 2)))
                elif A["bank7"] and k == 1:
                    pe.wait_ge(std_ready.sem, std_ready.at(A["bank7"]))
                w = A["width"](t, i)
                n = -(-w // P)
                for b in range(n):
                    m = min(P, w - b * P)
                    mm = pe.transpose(psum[0:m, 6 + k % 2, b * P:b * P + P],
                                      A["p"][:, k % 2, b * P:b * P + m], A["ident"])
                turned.give(mm, (L, k))

            extra(pe, "pe", -1)
            do_scores(0)
            do_scores(1)
            for k in range(last):
                do_scores(k + 2)
                extra(pe, "pe", k, 0)
                turn(k)
                if k >= 4 and k % 4:
                    values_pe(pe, L, A, k // 4 - 1, A["parts"].get(k % 4, ()))
                extra(pe, "pe", k, 1)
            values_pe(pe, L, A, A["tasks"] - 1, range(3))
            extra(pe, "pe", last)

        def values_pe(pe, L, A, t, passes):
            g, first, final = A["group"](t)
            if 0 in passes:
                pe.wait_ge(turned_lo.sem, turned_lo.at((L, 4 * t + 3)))
                if first:
                    free_bank(pe, g)
            rows = A["rows"](t)
            n = A["blocks"](t)
            for n_pass in passes:
                wi, mi = ((0, 0), (1, 0), (0, 1))[n_pass]
                for j in range(n):
                    q, count = A["start"](t, j), n * n_pass + j
                    mm = pe.matmul(bank(g)[:, q:S], A["values"](t, j)[wi],
                                   A["moving"](mi, t, rows, j), start=(first and count == 0),
                                   stop=(final and count == 3 * n - 1), skip_group_check=True)
            if 2 in passes:
                prod.give(mm, ("pv", L, t))

        def softmax_act(act, L, A, extra):
            last = 4 * A["tasks"]

            def hi(k):
                t, i = divmod(k, 4)
                act.wait_ge(turned.sem, turned.at((L, k)))
                if i == 0 and t >= A["slots"]:
                    act.wait_ge(prod.sem, prod.at(("pv", L, t - A["slots"])))
                rows = A["rows"](t)
                n = -(-A["width"](t, i) // P)
                turned_hi.give(act.activation(
                    A["place"](0, t, rows, n, i),
                    psum[0:rows, 6 + k % 2, 0:n * P].rearrange("p (a n) -> p a n", n=P), ACT.Copy), (L, k))
            extra(act, "act", -1)
            for k in range(last):
                t, i = divmod(k, 4)
                w = A["width"](t, i)
                act.wait_ge(peak.sem, peak.at((L, k)))
                if k >= 2:
                    act.wait_ge(turned.sem, turned.at((L, k - 2)))
                probs.give(act.activation(A["p"][:, k % 2, 0:w], psum[:, 4 + k % 2, 0:w], ACT.Exp,
                                          bias=small[:, 1, k % 4:k % 4 + 1],
                                          accum_out=small[:, 2, k % 4:k % 4 + 1]), (L, k))
                extra(act, "act", k, 0)
                if k:
                    hi(k - 1)
                extra(act, "act", k, 1)
            hi(last - 1)
            extra(act, "act", last)

        def softmax_dve(dve, order, L, A, extra):
            last = 4 * A["tasks"]

            def maximum(k):
                if k >= last:
                    return
                t, i = divmod(k, 4)
                dve.wait_ge(scores.sem, scores.at((L, k)))
                if k >= 4:
                    dve.wait_ge(probs.sem, probs.at((L, k - 4)))
                peak.give(dve.tensor_reduce(small[:, 1, k % 4:k % 4 + 1], psum[:, 4 + k % 2, 0:A["width"](t, i)],
                                            AXX, ALU.max, negate=True), (L, k))

            def scale(k):
                t, i = divmod(k, 4)
                w = A["width"](t, i)
                dve.wait_ge(probs.sem, probs.at((L, k)))
                r = small[:, 3, k % 4:k % 4 + 1]
                order.step(dve.reciprocal(r, small[:, 2, k % 4:k % 4 + 1]))
                g = A["gate"](t, i)
                p = A["p"][:, k % 2, 0:w]
                probs_scaled.give(dve.tensor_scalar(p, p, r, g, ALU.mult, ALU.mult if g is not None
                                                    else ALU.bypass), (L, k))

            def lo(k):
                t, i = divmod(k, 4)
                dve.wait_ge(turned_hi.sem, turned_hi.at((L, k)))
                rows = A["rows"](t)
                n = -(-A["width"](t, i) // P)
                turned_lo.give(dve.tensor_tensor(
                    A["place"](1, t, rows, n, i), psum[0:rows, 6 + k % 2, 0:n * P].rearrange("p (a n) -> p a n", n=P),
                    A["place"](0, t, rows, n, i).bitcast(F32), ALU.subtract), (L, k))
            extra(dve, "dve", -1)
            maximum(0)
            for k in range(last):
                maximum(k + 1)
                scale(k)
                extra(dve, "dve", k, 0)
                if k:
                    lo(k - 1)
                extra(dve, "dve", k, 1)
            lo(last - 1)
            extra(dve, "dve", last)

        scores = Signal(sem("scores"))
        peak = Signal(sem("peaks"))
        probs = Signal(sem("probabilities"))
        probs_scaled = Signal(sem("probabilities_scaled"))
        turned = Signal(sem("turned"))
        turned_hi = Signal(sem("turned_hi"))
        turned_lo = Signal(sem("turned_lo"))

        def evac_split_act(act, g, hi, factor=1.0):
            act.wait_ge(prod.sem, prod.at(("g", g)))
            evac_hi.give(act.activation(hi, bank(g), ACT.Copy, scale=factor), g)

        def evac_split_dve(dve, g, hi, lo, factor=1.0):
            dve.wait_ge(evac_hi.sem, evac_hi.at(g))
            evac.give(dve.scalar_tensor_tensor(out=lo, in0=bank(g), scalar=factor, in1=hi.bitcast(F32),
                                               op0=ALU.mult, op1=ALU.subtract), ("g", g))

        top[0] = region
        lat = at("lat", [P, 4, S])
        top[0] = region
        ql_hi = at("ql_hi", [P, 2, S], F32R)
        ql_lo = at("ql_lo", [P, 2, S], F32R)
        cq_hi = at("cq_hi", [P, 2, S], F32R)
        cq_lo = at("cq_lo", [P, 2, S], F32R)
        kv_hi = at("kv_hi", [P, S], F32R)
        kv_lo = at("kv_lo", [P, S], F32R)
        kr_hi = at("kr_hi", [P, S], F32R)
        kr_lo = at("kr_lo", [P, S], F32R)
        v_hi = at("v_hi", [P, 4, P], F32R)
        v_lo = at("v_lo", [P, 4, P], F32R)
        qn_hi = at("qn_hi", [P, 8, S], F32R)
        qn_lo = at("qn_lo", [P, 8, S], F32R)
        qr_hi = at("qr_hi", [P, 4, S], F32R)
        qr_lo = at("qr_lo", [P, 4, S], F32R)
        pm = at("pm", [P, 2, S])
        ol_hi = at("ol_hi", [P, 2, S], F32R)
        ol_lo = at("ol_lo", [P, 2, S], F32R)
        mrope = at("mrope", [P, 2, S])
        mconst = at("mconst", [P, 2, P])
        assert top[0] <= nc.sbuf_usable_end, (top[0], nc.sbuf_usable_end)

        stage_loads = [1]

        def plan_mla(L):
            u, g = cur.u, cur.g
            own[L, "u"], own[L, "g"] = u, g
            plan_pre(L)
            own[L, "loaded"] = 16 * (stage_loads[0] + 3)
            stage_loads[0] += 3
            for k in range(4):
                plan_unit(cur.g)
                evac.plan(("g", cur.g))
                cur.g += 1
            plan_norm((L, "nq"), 2)
            plan_norm((L, "nkv"), 1)
            for c in range(2):
                scaled.plan((L, "cq", c))
                part_hi.plan((L, "cq", c))
                h_ready.plan((L, "cq", c))
            scaled.plan((L, "kv"))
            part_hi.plan((L, "kv"))
            h_ready.plan((L, "kv"))
            sums.plan((L, "turned_kv"), (L, "rot", "k"))
            part_hi.plan((L, "v"))
            h_ready.plan((L, "v"))
            scaled.plan((L, "rot", "k"))
            part_hi.plan((L, "rot", "k"))
            h_ready.plan((L, "rot", "k"))
            for c in range(4):
                if c == 3:
                    plan_unit(cur.g)
                else:
                    prod.plan(("g", cur.g))
                evac.plan(("g", cur.g))
                cur.g += 1
            for c in range(8):
                if c % 4 == 3:
                    plan_unit(cur.g)
                else:
                    prod.plan(("g", cur.g))
                evac_hi.plan(cur.g)
                evac.plan(("g", cur.g))
                cur.g += 1
            for c in range(4):
                sums.plan((L, "rot", c))
                scaled.plan((L, "rot", c))
                part_hi.plan((L, "rot", c))
                h_ready.plan((L, "rot", c))
            events = own[L, "events"] = {}
            uk, uv = cur.u, cur.u + 1

            def group(kind, n, unit_end=None):
                label = cur.g
                if unit_end is not None:
                    prod.plan(("u", unit_end))
                    prod.values[("g", label)] = prod.planned
                else:
                    prod.plan(("g", label))
                if kind == "pv":
                    prod.values[("pv", L, n)] = prod.planned
                evac_hi.plan(label)
                evac.plan(("g", label))
                events[kind, n] = label
                cur.g += 1
            group("ql", 0)
            for k in range(4 * HEADS):
                t, i = divmod(k, 4)
                if i == 0 and t + 1 < HEADS:
                    group("ql", t + 1, uk + 2 * ((t + 1) // 8) if (t + 1) % 8 == 7 else None)
                if i == 1 and t >= 1:
                    group("pv", t - 1)
                if i == 3 and t >= 1 and (t - 1) % 2 == 1:
                    p = (t - 1) // 2
                    group("uv", p, uv + 2 * (p // 4) if p % 4 == 3 else None)
            group("pv", HEADS - 1)
            group("uv", HEADS // 2 - 1, uv + 2)
            own[L, "uk"], own[L, "uv"] = uk, uv
            cur.u += 4
            plan_softmax(L, {"tasks": HEADS})
            own[L, "wo"], own[L, "wog"] = cur.u, cur.g
            plan_ynorm((L, "post"))
            for n in range(NC):
                plan_unit(cur.g)
                evac.plan(("g", cur.g))
                cur.g += 1
            plan_post(L)

        def mla_scores(pe, t, i, dst):
            q = slice(i * P, (i + 1) * P)
            r, row = t // 4, 32 * (t % 4)
            if i == 0:
                pe.wait_ge(evac.sem, evac.at(("g", own["mla", "events"]["ql", t])))
            three_passes(pe, dst, [(ql_hi[:, t % 2, q], ql_lo[:, t % 2, q])], [(kv_hi[:], kv_lo[:])],
                         last=False, skip=True)
            rows = slice(row, row + 32)
            return three_passes(pe, dst, [(qr_hi[rows, r, q], qr_lo[rows, r, q])],
                                [(kr_hi[rows, :], kr_lo[rows, :])], first=False, skip=True)

        mla_attention = {
            "tasks": HEADS, "width": lambda t, i: S, "scores": mla_scores,
            "gate": lambda t, i: None, "p": pm, "slots": 2,
            "place": lambda m, t, rows, n, i: (pt2_hi, pt2_lo)[m][0:rows, t % 2, 0:n, i * P:(i + 1) * P],
            "moving": lambda m, t, rows, j: (pt2_hi, pt2_lo)[m][0:rows, t % 2, j, :],
            "rows": lambda t: P, "blocks": lambda t: 4, "start": lambda t, j: 0,
            "values": lambda t, j: (v_hi[:, j], v_lo[:, j]), "ident": mconst[:, 0],
            "parts": {1: (0, 1, 2)},
            "group": lambda t: (own["mla", "events"]["pv", t], True, True),
            "bank7": ("mla", "nkv"),
        }

        def mla_extra(L):
            def run(eng, who, k, phase=0):
                ev, uk, uv = own[L, "events"], own[L, "uk"], own[L, "uv"]
                todo = []
                if k == -1:
                    todo.append(("ql", 0))
                elif k == 4 * HEADS:
                    if who != "pe":
                        todo.append(("pv", HEADS - 1))
                    todo.append(("uv", HEADS // 2 - 1))
                else:
                    t, i = divmod(k, 4)
                    if who == "pe":
                        if phase == 0 and i == 0 and t + 1 < HEADS:
                            todo.append(("ql", t + 1))
                        if phase == 1 and i == 3 and t >= 2 and t % 2 == 0:
                            todo.append(("uv", t // 2 - 1))
                    else:
                        if phase == 1 and i == 0 and t >= 3 and t % 2 == 1:
                            todo.append(("uv", (t - 3) // 2))
                        if phase == 0 and i == 1 and t + 1 < HEADS:
                            todo.append(("ql", t + 1))
                        if phase == 1 and i == 2 and t >= 1:
                            todo.append(("pv", t - 1))
                for kind, n in todo:
                    g = ev[kind, n]
                    if who == "pe":
                        free_bank(eng, g)
                        if kind == "ql":
                            u = uk + 2 * (n // 8)
                            eng.wait_ge(lo_ready, u + 1)
                            mm = three_passes(eng, bank(g), unit_blocks(u, [n % 8]),
                                              chunks_of(qn_hi, qn_lo, [n // 2]))
                            prod.give(mm, ("g", g) if n % 8 != 7 else ("u", u))
                        else:
                            u = uv + 2 * (n // 4)
                            eng.wait_ge(lo_ready, u + 1)
                            eng.wait_ge(evac.sem, evac.at(("g", ev["pv", 2 * n + 1])))
                            mm = three_passes(eng, bank(g), unit_blocks(u, [2 * (n % 4), 2 * (n % 4) + 1]),
                                              chunks_of(ol_hi, ol_lo, [0, 1]))
                            prod.give(mm, ("g", g) if n % 4 != 3 else ("u", u))
                        continue
                    if kind == "ql":
                        dst = (ql_hi[:, n % 2], ql_lo[:, n % 2])
                        if n >= 2 and who == "act":
                            eng.wait_ge(scores.sem, scores.at((L, 4 * (n - 2) + 3)))
                    elif kind == "pv":
                        dst = (ol_hi[:, n % 2], ol_lo[:, n % 2])
                        if n >= 2 and who == "act":
                            eng.wait_ge(prod.sem, prod.at(("g", ev["uv", n // 2 - 1])))
                    else:
                        dst = (qn_hi[:, n], qn_lo[:, n])
                    factor = ATTN_SCALE if kind == "ql" else 1.0
                    if who == "act":
                        evac_split_act(eng, g, dst[0], factor)
                    else:
                        evac_split_dve(eng, g, *dst, factor)
            return run

        def rotary(r):
            return ta[:, r] if r < 2 else pm[:, r - 2]

        def mla_pe(pe, L):
            u, g = own[L, "u"], own[L, "g"]
            norm_pe(pe, (L, "pre"), NC, ones[:])
            dense_first(pe, L, u, g)
            for k in range(2, 4):
                dense(pe, u + k, g + k)
            norm_pe(pe, (L, "nq"), 2, ones[:])
            norm_pe(pe, (L, "nkv"), 1, ones[:])
            pe.wait_ge(stage_loaded, own[L, "loaded"])
            pe.wait_ge(scaled.sem, scaled.at((L, "kv")))
            for j in range(4):
                mm = pe.transpose(psum[:, 6, j * P:(j + 1) * P], tb[:, 0, j * P:(j + 1) * P], mconst[:, 0])
            sums.give(mm, (L, "turned_kv"))
            sums.give(pe.matmul(psum[:, 5], mconst[:, 1], lat[:, 3], start=True, stop=True), (L, "rot", "k"))
            u, g = u + 4, g + 4
            pe.wait_ge(h_ready.sem, h_ready.at((L, "cq", 1)))
            for c in range(12):
                if c % 4 == 0:
                    pe.wait_ge(lo_ready, u + c // 4 + 1)
                free_bank(pe, g + c)
                mm = three_passes(pe, bank(g + c), unit_blocks(u + c // 4, (2 * (c % 4), 2 * (c % 4) + 1)),
                                  chunks_of(cq_hi, cq_lo, (0, 1)))
                prod.give(mm, ("u", u + c // 4) if c % 4 == 3 else ("g", g + c))
                if c >= 5 and c % 2 == 1:
                    r = (c - 5) // 2
                    pe.wait_ge(evac.sem, evac.at(("g", g + r)))
                    if r:
                        pe.wait_ge(scaled.sem, scaled.at((L, "rot", r - 1)))
                    else:
                        pe.wait_ge(scaled.sem, scaled.at((L, "rot", "k")))
                    sums.give(pe.matmul(psum[:, 5], mconst[:, 1], rotary(r), start=True, stop=True),
                              (L, "rot", r))
            pe.wait_ge(h_ready.sem, h_ready.at((L, "rot", 3)))
            softmax_pe(pe, L, mla_attention, mla_extra(L))
            u, g = own[L, "wo"], own[L, "wog"]
            pe.wait_ge(evac.sem, evac.at(("g", own[L, "events"]["uv", 7])))
            for n in range(NC):
                pe.wait_ge(lo_ready, u + n + 1)
                free_bank(pe, g + n)
                mm = three_passes(pe, bank(g + n), unit_blocks(u + n, range(NC)),
                                  chunks_of(qn_hi, qn_lo, range(NC)))
                prod.give(mm, ("u", u + n))
            ynorm_pe(pe, (L, "post"))

        def split_value_act(act, label, src, hi):
            act.wait_ge(scaled.sem, scaled.at(label))
            part_hi.give(act.activation(hi, src, ACT.Copy), label)

        def split_value_dve(dve, label, src, hi, lo):
            dve.wait_ge(part_hi.sem, part_hi.at(label))
            h_ready.give(dve.tensor_tensor(lo, src, hi.bitcast(F32), ALU.subtract), label)

        def mla_act(act, order, L, before):
            u, g = own[L, "u"], own[L, "g"]
            act.wait_ge(x_ready.sem, x_ready.at((before, 0)))
            act.dma_start(mrope[:], mla_rope).then_inc(stage_loaded, 16)
            act.dma_start(mconst[:, 0], consts[:, IDENT * P:(IDENT + 1) * P]).then_inc(stage_loaded, 16)
            act.dma_start(mconst[:, 1], consts[:, PERM32 * P:(PERM32 + 1) * P]).then_inc(stage_loaded, 16)
            pre_act(act, L, before, 12)
            for k in range(4):
                split_hi(act, u + k + LEAD)
            norm_act(act, (L, "nq"), [(lat[:, c], (evac.sem, evac.at(("g", g + c)))) for c in range(2)], 256)
            norm_act(act, (L, "nkv"), [(lat[:, 2], (evac.sem, evac.at(("g", g + 2))))], P)
            for c in range(2):
                split_value_act(act, (L, "cq", c), ta[:, c], cq_hi[:, c])
            split_value_act(act, (L, "kv"), tb[:, 0], kv_hi[:])
            act.wait_ge(sums.sem, sums.at((L, "turned_kv")))
            part_hi.give(act.activation(v_hi[:], psum[:, 6].rearrange("p (a n) -> p a n", n=P), ACT.Copy), (L, "v"))
            split_value_act(act, (L, "rot", "k"), tb[:, 1], kr_hi[:])
            u, g = u + 4, g + 4
            split_hi(act, u + 2)
            split_hi(act, u + 3)
            for c in range(8):
                if c == 4:
                    split_hi(act, u + 4)
                evac_split_act(act, g + 4 + c, qn_hi[:, c])
                if c % 2 == 1:
                    r = c // 2
                    split_value_act(act, (L, "rot", r), tb[:, r % 2], qr_hi[:, r])
            split_hi(act, u + 5)
            split_hi(act, u + 6)
            softmax_act(act, L, mla_attention, mla_extra(L))
            u, g = own[L, "wo"], own[L, "wog"]
            split_hi(act, u)
            split_hi(act, u + 1)
            out_act(act, L, u, g, y_ffn)

        def out_act(act, L, u, g, y):
            q0, y0 = sq_ready.at((L, "post")), ysum.at((L, "post"))
            preload(act, ACT.Sqrt)
            for n in range(NC):
                split_hi(act, u + n + LEAD)
                act.wait_ge(evac.sem, evac.at(("g", g + n)))
                if n >= 2:
                    act.wait_ge(ysum.sem, y0 + n - 1)
                act.activation(sq[:, (q0 + n) % 2], y[:, n], ACT.Square).then_inc(sq_ready.sem, 1)
            sq_ready.give_loop((L, "post"), NC)
            post_act(act, L)

        def rotate_dve(dve, order, label, src, cos, sin, swapped, dst):
            order.step(dve.tensor_tensor(dst, src, cos, ALU.mult))
            dve.wait_ge(sums.sem, sums.at(label))
            order.step(dve.tensor_tensor(std[:, :dst.shape[1]], swapped, sin, ALU.mult))
            scaled.give(dve.tensor_tensor(dst, dst, std[:, :dst.shape[1]], ALU.add), label)

        def mla_dve(dve, order, L, gains):
            u, g = own[L, "u"], own[L, "g"]
            pre_dve(dve, order, L, gains(0), scale=13, shift=12)
            for k in range(4):
                split_lo(dve, u + k + LEAD)
            for k in range(4):
                dve.wait_ge(prod.sem, prod.at(("g", g + k)))
                evac.give(dve.tensor_copy(lat[:, k], bank(g + k)), ("g", g + k))
            qn, kn = col.at["q_norm"], col.at["kv_norm"]
            norm_dve(dve, (L, "nq"))
            for c in range(2):
                scaled.give(dve.scalar_tensor_tensor(out=ta[:, c], in0=lat[:, c], scalar=par[:, qn + c:qn + c + 1],
                                                     in1=rstd[:], op0=ALU.mult, op1=ALU.mult), (L, "cq", c))
            for c in range(2):
                split_value_dve(dve, (L, "cq", c), ta[:, c], cq_hi[:, c], cq_lo[:, c])
            dve.wait_ge(h_ready.sem, h_ready.at((L, "cq", 1)))
            norm_dve(dve, (L, "nkv"))
            scaled.give(dve.scalar_tensor_tensor(out=tb[:, 0], in0=lat[:, 2], scalar=par[:, kn:kn + 1],
                                                 in1=rstd[:], op0=ALU.mult, op1=ALU.mult), (L, "kv"))
            split_value_dve(dve, (L, "kv"), tb[:, 0], kv_hi[:], kv_lo[:])
            dve.wait_ge(part_hi.sem, part_hi.at((L, "v")))
            h_ready.give(dve.tensor_tensor(v_lo[:], psum[:, 6].rearrange("p (a n) -> p a n", n=P),
                                           v_hi[:].bitcast(F32), ALU.subtract), (L, "v"))
            dve.wait_ge(stage_loaded, own[L, "loaded"])
            rotate_dve(dve, order, (L, "rot", "k"), lat[:, 3], mrope[:, 0], mrope[:, 1], psum[:, 5], tb[:, 1])
            split_value_dve(dve, (L, "rot", "k"), tb[:, 1], kr_hi[:], kr_lo[:])
            u, g = u + 4, g + 4
            for r in range(4):
                dve.wait_ge(prod.sem, prod.at(("g", g + r)))
                evac.give(dve.tensor_scalar(rotary(r), bank(g + r), ATTN_SCALE, None, ALU.mult), ("g", g + r))
            split_lo(dve, u + 2)
            split_lo(dve, u + 3)
            for c in range(8):
                if c == 4:
                    split_lo(dve, u + 4)
                evac_split_dve(dve, g + 4 + c, qn_hi[:, c], qn_lo[:, c])
                if c % 2 == 0:
                    continue
                r = c // 2
                dve.wait_ge(evac.sem, evac.at(("g", g + r)))
                dve.wait_ge(h_ready.sem, h_ready.at((L, "rot", r - 2 if r >= 2 else "k")))
                rotate_dve(dve, order, (L, "rot", r), rotary(r), mrope[:, 0], mrope[:, 1], psum[:, 5],
                           tb[:, r % 2])
                split_value_dve(dve, (L, "rot", r), tb[:, r % 2], qr_hi[:, r], qr_lo[:, r])
            split_lo(dve, u + 5)
            split_lo(dve, u + 6)
            softmax_dve(dve, order, L, mla_attention, mla_extra(L))
            u, g = own[L, "wo"], own[L, "wog"]
            split_lo(dve, u)
            split_lo(dve, u + 1)
            out_dve(dve, L, u, g, y_ffn)
            post_dve(dve, order, L, y_ffn, gains(1), 14, 1.0)

        def out_dve(dve, L, u, g, y):
            q0, y0 = sq_ready.at((L, "post")), ysum.at((L, "post"))
            ysum.give(dve.memset(std[:], 0.0), ((L, "post"), "zero"))
            for n in range(NC):
                split_lo(dve, u + n + LEAD)
                dve.wait_ge(prod.sem, prod.at(("g", g + n)))
                evac.give(dve.tensor_copy(y[:, n], bank(g + n)), ("g", g + n))
                add_square(dve, n, q0, y0)
            ysum.give_loop((L, "post"), NC)

        TAB = S + 32
        top[0] = region
        ya_hi = at("ya_hi", [P, 4, S], F32R)
        ya_lo = at("ya_lo", [P, 4, S], F32R)
        crr = at("crr", [P, NCONSTR, P], F32R)
        crf = at("crf", [P, 3, P])
        hybrid = top[0]
        ka_hi = at("ka_hi", [P, 4, S], F32R)
        ka_lo = at("ka_lo", [P, 4, S], F32R)
        va_hi = at("va_hi", [P, 4, 4, 3, 64], F32R)
        va_lo = at("va_lo", [P, 4, 4, 3, 64], F32R)
        za = at("za", [P, 4, S])
        SB_AT, SB_ALL = {3: 0, 2: P, 1: 3 * P, 0: 6 * P}, 10 * P
        sp_hi = at("sp_hi", [P, 2, SB_ALL], F32R)
        sp_lo = at("sp_lo", [P, 2, SB_ALL], F32R)
        wt_hi = at("wt_hi", [P, SB_ALL], F32R)
        wt_lo = at("wt_lo", [P, SB_ALL], F32R)
        sb_t = nc.alloc_sbuf_tensor_at("sb_t", [P, SB_ALL], F32, offset=ta_base)
        sb_w = nc.alloc_sbuf_tensor_at("sb_w", [P, SB_ALL], F32, offset=sq_base)
        assert top[0] <= nc.sbuf_usable_end, (top[0], nc.sbuf_usable_end)
        top[0] = hybrid
        cload = at("cload", [P, NCONSTR, P])
        top[0] = hybrid
        nq_hi = at("nq_hi", [P, 4, S], F32R)
        nq_lo = at("nq_lo", [P, 4, S], F32R)
        after_q = top[0]
        nk_hi = at("nk_hi", [P, 2, S], F32R)
        nk_lo = at("nk_lo", [P, 2, S], F32R)
        nv_hi = at("nv_hi", [P, 4, 2, 3, 64], F32R)
        nv_lo = at("nv_lo", [P, 4, 2, 3, 64], F32R)
        zb = at("zb", [P, 4, S])
        rope_base = top[0]
        rcos = at("rcos", [P, TAB])
        rsin = at("rsin", [P, TAB])
        f_hi = at("f_hi", [P, 992], F32R)
        f_lo = at("f_lo", [P, 992], F32R)
        hid = at("hid", [P, 2, 62])
        w2s = at("w2s", [P, 2, 256])
        kc_base = top[0]
        kc_hi = at("kc_hi", [P, 32], F32R)
        kc_lo = at("kc_lo", [P, 32], F32R)
        vc_hi = at("vc_hi", [P, 3, 64], F32R)
        vc_lo = at("vc_lo", [P, 3, 64], F32R)
        rc = at("rc", [P, 6])
        pn = at("pn", [P, 2, S])
        pt_base = top[0]
        nf = at("nf", [P, 6, S])
        zk = at("zk", [P, 2, 2, S // 2])
        top[0] = pt_base
        pt1 = [[at("pt1_hi", [P, 13, P], F32R), at("pt1_lo", [P, 13, P], F32R)]]
        pt_end = top[0]
        top[0] = rope_base
        pt1.append([at("pt1b_hi", [P, 13, P], F32R), at("pt1b_lo", [P, 13, P], F32R)])
        assert top[0] <= kc_base
        top[0] = mod_base
        gt = at("gt", [P, 4, 24])
        kcf = at("kcf", [P, 32])
        qgain = at("qgain", [P, 1])
        top[0] = pt_base
        posi = at("posi", [P, S], I32)
        assert top[0] <= nc.sbuf_usable_end
        assert pt_end <= nc.sbuf_usable_end
        top[0] = after_q
        mg_hi = at("mg_hi", [P, NC, S], F32R)
        mg_lo = at("mg_lo", [P, NC, S], F32R)

        zs = Signal(sem("sb_scores"))
        magnitude = Signal(sem("sb_magnitudes"))
        logs = Signal(sem("sb_logs"))
        softplus = Signal(sem("sb_softplus"))
        exponent = Signal(sem("sb_exponents"))
        weights = Signal(sem("sb_weights"))
        weights_lo = Signal(sem("sb_weights_split"))

        def flat(t, n):
            return t[:].rearrange("p a n -> p (a n)")[:, 0:n]

        NORM_AT = {s: n for n, s in enumerate((3, 5, 7, 8, 10, 12))}
        ROTATE_AT = {s: n for n, s in enumerate((5, 7, 8, 10, 12, 13))}

        def plan_hybrid(l):
            L = ("hy", l)

            def group():
                cur.g += 1
                return cur.g - 1
            own[L, "loaded0"] = 16 * (stage_loads[0] + 4) if l == 0 else 16 * stage_loads[0]
            if l == 0:
                stage_loads[0] += 4
            own[L, "loaded1"] = 16 * (stage_loads[0] + 3)
            stage_loads[0] += 3
            plan_pre(L)
            if l == 0:
                part_hi.plan("crr")
            own[L, "ua"], own[L, "ga"] = cur.u, cur.g
            for c in range(8):
                plan_unit(cur.g)
                evac_hi.plan(cur.g)
                evac.plan(("g", group()))
            for m in range(3):
                plan_unit()
            for t in range(3):
                prod.plan(("g", cur.g + t))
            plan_unit(cur.g + 3)
            for t in range(4):
                evac_hi.plan(cur.g)
                evac.plan(("g", group()))
            for c in range(4):
                plan_unit(cur.g)
                evac.plan(("g", group()))
                value.plan((L, "za", c))
            for k in range(16):
                for signal in (zs, magnitude, logs, softplus, exponent, weights, weights_lo):
                    signal.plan((L, k))
            for h in range(8):
                if h % 2 == 0:
                    prod.plan(("sb", L, h))
                else:
                    prod.plan(("g", cur.g))
                    prod.values["sb", L, h] = prod.planned
                    evac.plan(("g", cur.g))
                    part_hi.plan((L, "ya", h // 2))
                    h_ready.plan((L, "ya", h // 2))
                    own[L, "sbg", h // 2] = group()
            own[L, "ub"], own[L, "gb"] = cur.u, cur.g
            scaled.plan((L, "angle", 0), (L, "angle", 1))
            value.plan((L, "trig", 0), (L, "trig", 1))
            for s in range(14):
                plan_unit(cur.g)
                evac.plan(("g", group()))
                if s in NORM_AT:
                    plan_norm((L, "n", NORM_AT[s]), 1)
                    scaled.plan((L, "xn", NORM_AT[s]))
                if s in ROTATE_AT:
                    for signal in (sums, scaled, part_hi, h_ready):
                        signal.plan((L, "rot", ROTATE_AT[s]))
                if s >= 10:
                    value.plan((L, "zb", s - 10))
            for m in range(2):
                plan_unit()
            for t in range(3):
                prod.plan(("g", cur.g + t))
            plan_unit(cur.g + 3)
            for t in range(4):
                evac_hi.plan(cur.g)
                evac.plan(("g", group()))
            value.plan((L, "gates"))
            scaled.plan((L, "gates"))
            for kv in range(2):
                scaled.plan((L, "f", kv))
                part_hi.plan((L, "f", kv))
                h_ready.plan((L, "f", kv))
                for m in range(3):
                    plan_unit()
                plan_unit(cur.g)
                prod.plan(("g", cur.g + 1))
                evac.plan(("g", group()))
                evac.plan(("g", group()))
                value.plan((L, "hid", kv))
                prod.plan(("g", cur.g))
                if kv == 1:
                    evac_hi.plan(cur.g)
                else:
                    own[L, "kcg"] = cur.g
                evac.plan(("g", group()))
                if kv == 0:
                    plan_norm((L, "n", 6), 1)
                    scaled.plan((L, "xn", 6))
                    sums.plan((L, "rot", 6))
                    scaled.plan((L, "rot", 6))
                    part_hi.plan((L, "rot", 6))
                    h_ready.plan((L, "rot", 6))
                    scaled.plan((L, "vc"))
            plan_softmax(L, {"tasks": 24})
            for t in range(24):
                if t % 6 == 5:
                    prod.plan(("g", cur.g))
                    prod.values["pv", L, t] = prod.planned
                    evac.plan(("g", cur.g))
                    part_hi.plan((L, "yb", t // 6))
                    h_ready.plan((L, "yb", t // 6))
                    own[L, "ng", t // 6] = group()
                else:
                    prod.plan(("pv", L, t))
            own[L, "uc"], own[L, "gc"] = cur.u, cur.g
            for n in range(NC):
                for m, e in enumerate((1, 2, 4)):
                    prod.values["u", cur.u + 3 * n + m] = prod.planned + 4 * n + e
                for m in range(4):
                    prod.values["g", cur.g + 4 * n + m] = prod.planned + 4 * n + m + 1
                    evac.values["g", cur.g + 4 * n + m] = evac.planned + 4 * n + m + 1
            prod.plan_loop((L, "up"), 32)
            evac.plan_loop((L, "up"), 32)
            value.plan_loop((L, "up"), 16)
            part_hi.plan_loop((L, "up"), NC)
            cur.u += 24
            cur.g += 32
            own[L, "ud"], own[L, "gd"] = cur.u, cur.g
            for n in range(NC):
                plan_unit(cur.g)
                evac.plan(("g", group()))
            own[L, "after"] = cur.g - NC

        def stream_ready(before, c):
            if isinstance(before, tuple):
                return evac.sem, evac.at(("g", own[before, "after"] + c))
            return x_ready.sem, x_ready.at((before, c))

        def natural_pe(pe, u, g, per_unit, width, units_of):
            for t in range(4):
                free_bank(pe, g + t)
            for m in range(units_of):
                pe.wait_ge(lo_ready, u + m + 1)
                s = (u + m) % RING
                ks = range(per_unit * m, min(per_unit * (m + 1), NC))
                for t in range(4):
                    tok = slice(t * P, (t + 1) * P)
                    mm = three_passes(
                        pe, bank(g + t)[:, 0:width], [(h_hi[:, k, tok], h_lo[:, k, tok]) for k in ks],
                        [(w_hi[:, s, (k - ks[0]) * width:(k - ks[0] + 1) * width],
                          w_lo[:, s, (k - ks[0]) * width:(k - ks[0] + 1) * width]) for k in ks],
                        first=(m == 0), last=(m == units_of - 1))
                    if m == units_of - 1 and t < 3:
                        prod.give(mm, ("g", g + t))
                prod.give(mm, ("u", u + m))

        def sb_blocks(L, m):
            h, e = divmod(m, 2)
            if e == 0:
                return [(3, slice(3 * P, S), 4 + h % 2, 0), (2, slice(2 * P, S), 4 + h % 2, P)]
            g = own[L, "sbg", 0] + h // 2 + (2 if h % 2 else 0)
            return [(1, slice(P, S), 6 + h % 2, 0), (0, slice(0, S), g % 4, 0)]

        def sb_spans(L, m):
            blocks_of = sb_blocks(L, m)
            if m % 2 == 0:
                return [(psum[:, blocks_of[0][2], 0:3 * P], slice(0, 3 * P))]
            return [(psum[:, b, 0:S - j * P], slice(SB_AT[j], SB_AT[j] + S - j * P)) for j, _, b, _ in blocks_of]

        def sb_all(m):
            return slice(0, 3 * P) if m % 2 == 0 else slice(3 * P, SB_ALL)

        def sb_pe(pe, L):
            def z(m):
                if m >= 16:
                    return
                h = m // 2
                if m >= 4:
                    pe.wait_ge(weights.sem, weights.at((L, m - 4)))
                if m % 4 == 3 and h // 2 >= 2:
                    pe.wait_ge(evac.sem, evac.at(("g", own[L, "sbg", h // 2 - 2])))
                rows = slice(64 * (h % 2), 64 * (h % 2) + 64)
                for j, q, b, at_ in sb_blocks(L, m):
                    keys = slice(j * P, (j + 1) * P)
                    three_passes(pe, psum[:, b, at_:at_ + S - j * P],
                                 [(ka_hi[rows, h // 2, keys], ka_lo[rows, h // 2, keys])],
                                 [(ya_hi[rows, h // 2, q], ya_lo[rows, h // 2, q])],
                                 first=(at_ == 0), last=False, skip=True)
                    mm = pe.matmul(psum[:, b, at_:at_ + P], crr[:, R_IDENT], crr[:, R_STRICT_T], start=False,
                                   stop=True, skip_group_check=True)
                zs.give(mm, (L, m))

            def accumulate(m):
                pe.wait_ge(softplus.sem, softplus.at((L, m)))
                for j, q, b, at_ in sb_blocks(L, m):
                    for jj in range(j, 4):
                        dst = psum[:, b, at_ + (jj - j) * P:at_ + S - j * P]
                        for part in (sp_hi, sp_lo):
                            mm = pe.matmul(dst, crr[:, R_NEGTRI if jj == j else R_NEGONES],
                                           part[:, m // 2 % 2, SB_AT[jj]:SB_AT[jj] + S - jj * P],
                                           start=False, stop=True, skip_group_check=True)
                exponent.give(mm, (L, m))

            def values(h):
                g = own[L, "sbg", h // 2]
                pe.wait_ge(weights_lo.sem, weights_lo.at((L, 2 * h + 1)))
                if h % 2 == 0:
                    free_bank(pe, g)
                n = 0
                for wi, mi in ((0, 0), (1, 0), (0, 1)):
                    for j in range(4):
                        v = (va_hi, va_lo)[wi][:, j, h // 2, h % 2:h % 2 + 2, :].rearrange("p a n -> p (a n)")
                        mm = pe.matmul(bank(g)[:, j * P:S], v, (wt_hi, wt_lo)[mi][:, SB_AT[j]:SB_AT[j] + S - j * P],
                                       start=(n == 0 and h % 2 == 0), stop=(n == 11 and h % 2 == 1),
                                       skip_group_check=True)
                        n += 1
                prod.give(mm, ("sb", L, h))
            z(0)
            z(1)
            for m in range(16):
                z(m + 2)
                if m % 2 == 1 and m >= 3:
                    values((m - 3) // 2)
                accumulate(m)
            values(7)

        def sb_act(act, order, L):
            def exps(m):
                if m < 16:
                    act.wait_ge(magnitude.sem, magnitude.at((L, m)))
                    order.link(act.activation(sb_t[:, sb_all(m)], sb_t[:, sb_all(m)], ACT.Exp))

            def logarithms(m):
                if m < 16:
                    order.sync()
                    logs.give(act.activation(sb_t[:, sb_all(m)], sb_t[:, sb_all(m)], ACT.Ln, bias=1.0), (L, m))

            def weigh(m):
                act.wait_ge(exponent.sem, exponent.at((L, m)))
                if m >= 2:
                    act.wait_ge(weights_lo.sem, weights_lo.at((L, m - 2)))
                spans = sb_spans(L, m)
                for n, (src, to) in enumerate(spans):
                    op = act.activation(sb_w[:, to], src, ACT.Exp)
                    if n + 1 < len(spans):
                        order.link(op)
                    else:
                        weights.give(op, (L, m))
            exps(0)
            logarithms(0)
            for m in range(16):
                exps(m + 1)
                if m:
                    weigh(m - 1)
                logarithms(m + 1)
                if m % 4 == 2 and m >= 6:
                    sb_out_act(act, L, (m - 6) // 4)
            weigh(15)
            sb_out_act(act, L, 3)

        def sb_out_act(act, L, p):
            act.wait_ge(evac.sem, evac.at(("g", own[L, "sbg", p])))
            part_hi.give(act.activation(ya_hi[:, p], rstd[:], ACT.Copy), (L, "ya", p))

        def sb_dve(dve, order, L):
            def magnitudes(m):
                if m >= 16:
                    return
                dve.wait_ge(zs.sem, zs.at((L, m)))
                if m >= 2:
                    dve.wait_ge(softplus.sem, softplus.at((L, m - 2)))
                spans = sb_spans(L, m)
                for src, to in spans:
                    order.link(dve.tensor_scalar(sb_t[:, to], src, -1.0, None, ALU.mult))
                order.sync()
                for n, (src, to) in enumerate(spans):
                    op = dve.tensor_tensor(sb_t[:, to], sb_t[:, to], src, ALU.min)
                    if n + 1 < len(spans):
                        order.link(op)
                    else:
                        magnitude.give(op, (L, m))

            def softpluses(m):
                dve.wait_ge(logs.sem, logs.at((L, m)))
                if m >= 4:
                    dve.wait_ge(exponent.sem, exponent.at((L, m // 2 * 2 - 3)))
                for src, to in sb_spans(L, m):
                    order.link(dve.scalar_tensor_tensor(out=sb_t[:, to], in0=src, scalar=0.0,
                                                        in1=sb_t[:, to], op0=ALU.max, op1=ALU.add))
                order.sync()
                t, hi, lo = sb_t[:, sb_all(m)], sp_hi[:, m // 2 % 2, sb_all(m)], sp_lo[:, m // 2 % 2, sb_all(m)]
                order.step(dve.tensor_copy(hi, t))
                softplus.give(dve.tensor_tensor(lo, t, hi.bitcast(F32), ALU.subtract), (L, m))

            def split_weights(m):
                if m % 2 == 0 and m:
                    dve.wait_ge(prod.sem, prod.at(("sb", L, m // 2 - 1)))
                dve.wait_ge(weights.sem, weights.at((L, m)))
                w, hi, lo = sb_w[:, sb_all(m)], wt_hi[:, sb_all(m)], wt_lo[:, sb_all(m)]
                order.step(dve.tensor_copy(hi, w))
                weights_lo.give(dve.tensor_tensor(lo, w, hi.bitcast(F32), ALU.subtract), (L, m))

            def out(p, phase):
                g = own[L, "sbg", p]
                if phase == 0:
                    dve.wait_ge(prod.sem, prod.at(("g", g)))
                    if p:
                        dve.wait_ge(h_ready.sem, h_ready.at((L, "ya", p - 1)))
                    dve.wait_ge(value.sem, value.at((L, "za", p)))
                    evac.give(dve.tensor_tensor(rstd[:], bank(g), za[:, p], ALU.mult), ("g", g))
                else:
                    dve.wait_ge(part_hi.sem, part_hi.at((L, "ya", p)))
                    h_ready.give(dve.tensor_tensor(ya_lo[:, p], rstd[:], ya_hi[:, p].bitcast(F32),
                                                   ALU.subtract), (L, "ya", p))
            magnitudes(0)
            magnitudes(1)
            for m in range(16):
                softpluses(m)
                magnitudes(m + 2)
                if m:
                    split_weights(m - 1)
                if m % 4 in (2, 3) and m >= 6:
                    out((m - 6) // 4, m % 4 - 2)
            split_weights(15)
            out(3, 0)
            out(3, 1)

        def nsa_attention(l):
            L = ("hy", l)

            def parts(t):
                return t // 6, t % 6 // 3, t % 3

            def run(pe, t, i, dst):
                c, side, b = parts(t)
                rows, q = slice(64 * side, 64 * side + 64), slice(i * P, (i + 1) * P)
                w = (i + 1) * P if b < 2 else 32
                moving = ((nk_hi[rows, b, 0:w], nk_lo[rows, b, 0:w]) if b < 2 else
                          (kc_hi[rows, :], kc_lo[rows, :]))
                three_passes(pe, dst, [(nq_hi[rows, c, q], nq_lo[rows, c, q])], [moving], last=False,
                             skip=True)
                if b < 2:
                    return pe.matmul(dst[:, i * P:(i + 1) * P], crr[:, R_IDENT], crr[:, R_CAUSAL],
                                     start=False, stop=True, skip_group_check=True)
                return pe.matmul(dst, crr[:, R_IDENT], crr[:, R_NEG31, 32 * i:32 * i + 32],
                                 start=False, stop=True, skip_group_check=True)

            def values(t, j):
                c, side, b = parts(t)
                pick = ((lambda v: v[:, j, b, side:side + 2, :]) if b < 2 else
                        (lambda v: v[0:32, side:side + 2, :]))
                pair = (nv_hi, nv_lo) if b < 2 else (vc_hi, vc_lo)
                return tuple(pick(v).rearrange("p a n -> p (a n)") for v in pair)

            def gate(t, i):
                c, side, b = parts(t)
                g = 8 * (1, 2, 0)[b] + 4 * side + c
                return gt[:, i, g:g + 1]
            return {
                "tasks": 24, "width": lambda t, i: (i + 1) * P if t % 3 < 2 else 32, "scores": run,
                "gate": gate, "parts": {1: (0,), 2: (1,), 3: (2,)}, "p": pn, "slots": 2,
                "place": lambda m, t, rows, n, i: pt1[t % 2][m][0:rows, i:i + 3 * n - 2:3, :],
                "moving": lambda m, t, rows, j: pt1[t % 2][m][0:rows, 4 * j:3 * j + 4, :]
                .rearrange("p a n -> p (a n)"),
                "rows": lambda t: P if t % 3 < 2 else 32, "blocks": lambda t: 4 if t % 3 < 2 else 1,
                "start": lambda t, j: j * P, "values": values, "ident": crf[:, 0],
                "group": lambda t: (own[L, "ng", t // 6], t % 6 == 0, t % 6 == 5),
                "bank7": (L, "n", 6),
            }

        def nsa_extra(L):
            def run(eng, who, k, phase=0):
                if who == "pe" or k == -1:
                    return
                if k == 96:
                    c, steps = 3, (0, 1)
                else:
                    c, at_ = k // 24 - 1, k % 24
                    if c < 0 or phase != 1 or at_ not in (5, 6, 7):
                        return
                    if who == "act":
                        if at_ != 6:
                            return
                        steps = (1,)
                    else:
                        if at_ == 6:
                            return
                        steps = (0,) if at_ == 5 else (1,)
                g = own[L, "ng", c]
                if who == "act":
                    eng.wait_ge(evac.sem, evac.at(("g", g)))
                    part_hi.give(eng.activation(nq_hi[:, c], rstd[:], ACT.Copy), (L, "yb", c))
                    return
                for s in steps:
                    if s == 0:
                        eng.wait_ge(prod.sem, prod.at(("g", g)))
                        if c:
                            eng.wait_ge(h_ready.sem, h_ready.at((L, "yb", c - 1)))
                        eng.wait_ge(value.sem, value.at((L, "zb", c)))
                        evac.give(eng.tensor_tensor(rstd[:], bank(g), zb[:, c], ALU.mult), ("g", g))
                    else:
                        eng.wait_ge(part_hi.sem, part_hi.at((L, "yb", c)))
                        h_ready.give(eng.tensor_tensor(nq_lo[:, c], rstd[:], nq_hi[:, c].bitcast(F32),
                                                       ALU.subtract), (L, "yb", c))
            return run

        def item(n):
            if n < 4:
                return nf[:, n], nq_hi[:, n], nq_lo[:, n], S, 0
            if n < 6:
                return nf[:, n], nk_hi[:, n - 4], nk_lo[:, n - 4], S, 0
            return kcf[:], kc_hi[:], kc_lo[:], 32, S

        def item_gain(l, n):
            if n < 4:
                return qgain[:]
            c = col.at["k_norm_2"] + 3 * l + (1, 2, 0)[n - 4]
            return par[:, c:c + 1]

        def item_rotate_pe(pe, L, n):
            w = item(n)[3]
            pe.wait_ge(scaled.sem, scaled.at((L, "xn", n)))
            if n >= 2:
                pe.wait_ge(scaled.sem, scaled.at((L, "rot", n - 2)))
            sums.give(pe.matmul(psum[:, 4 + n % 2, 0:w], crf[:, 2], ta[:, n % 2, 0:w], start=True,
                                stop=True), (L, "rot", n))

        def item_norm_act(act, l, n):
            L = ("hy", l)
            src, _, _, w, _ = item(n)
            g = own[L, "gb"] + n if n < 6 else own[L, "kcg"]
            norm_act(act, (L, "n", n), [(src, (evac.sem, evac.at(("g", g))))], 64, w)

        def item_hi_act(act, L, n):
            src, hi, _, w, _ = item(n)
            split_value_act(act, (L, "rot", n), tb[:, n % 2, 0:w], hi)

        def item_norm_dve(dve, l, n):
            L = ("hy", l)
            src, _, _, w, _ = item(n)
            if n:
                dve.wait_ge(scaled.sem, scaled.at((L, "xn", n - 1)))
            norm_dve(dve, (L, "n", n), w)
            if n >= 2:
                dve.wait_ge(sums.sem, sums.at((L, "rot", n - 2)))
                dve.wait_ge(scaled.sem, scaled.at((L, "rot", n - 2)))
            scaled.give(dve.scalar_tensor_tensor(out=ta[:, n % 2, 0:w], in0=src, scalar=item_gain(l, n),
                                                 in1=rstd[:, 0:w], op0=ALU.mult, op1=ALU.mult),
                        (L, "xn", n))

        def item_rotate_dve(dve, order, L, n):
            src, hi, lo, w, off = item(n)
            dve.wait_ge(scaled.sem, scaled.at((L, "xn", n)))
            if n >= 2:
                dve.wait_ge(h_ready.sem, h_ready.at((L, "rot", n - 2)))
            dst = tb[:, n % 2, 0:w]
            order.step(dve.tensor_tensor(dst, ta[:, n % 2, 0:w], rcos[:, off:off + w], ALU.mult))
            dve.wait_ge(sums.sem, sums.at((L, "rot", n)))
            order.step(dve.tensor_tensor(pn[:, 0, 0:w], psum[:, 4 + n % 2, 0:w], rsin[:, off:off + w],
                                         ALU.mult))
            scaled.give(dve.tensor_tensor(dst, dst, pn[:, 0, 0:w], ALU.add), (L, "rot", n))
            split_value_dve(dve, (L, "rot", n), dst, hi, lo)

        def hybrid_pe(pe, l):
            L = ("hy", l)
            attention = nsa_attention(l)
            norm_pe(pe, (L, "pre"), NC, ones[:])
            u, g = own[L, "ua"], own[L, "ga"]
            dense_first(pe, L, u, g)
            for c in range(2, 8):
                dense(pe, u + c, g + c)
            natural_pe(pe, u + 8, g + 8, 2, S, 4)
            for c in range(4):
                dense(pe, u + 12 + c, g + 12 + c)
            if l == 0:
                pe.wait_ge(part_hi.sem, part_hi.at("crr"))
                pe.wait_ge(stage_loaded, own[L, "loaded0"])
            pe.wait_ge(evac.sem, evac.at(("g", g + 15)))
            sb_pe(pe, L)
            u, g = own[L, "ub"], own[L, "gb"]
            for s in range(14):
                dense(pe, u + s, g + s)
                if s in NORM_AT:
                    norm_pe(pe, (L, "n", NORM_AT[s]), 1, crf[:, 1])
                if s in ROTATE_AT:
                    item_rotate_pe(pe, L, ROTATE_AT[s])
            natural_pe(pe, u + 14, g + 14, 3, NAT2, 3)
            u, g = u + 17, g + 18
            for kv in range(2):
                pe.wait_ge(h_ready.sem, h_ready.at((L, "f", kv)))
                free_bank(pe, g)
                for m in range(4):
                    pe.wait_ge(lo_ready, u + m + 1)
                    s = (u + m) % RING
                    ws = [tuple(w[:, s, 256 * a:256 * a + 256] for w in (w_hi, w_lo)) for a in range(4)]
                    fs = [tuple(f[:, 62 * (4 * m + a):62 * (4 * m + a) + 62] for f in (f_hi, f_lo))
                          for a in range(4)]
                    mm = three_passes(pe, bank(g)[0:62, 0:256], fs, ws, first=(m == 0), last=(m == 3))
                    prod.give(mm, ("u", u + m))
                free_bank(pe, g + 1)
                pe.wait_ge(evac.sem, evac.at(("g", g)))
                for half in range(2):
                    mm = pe.transpose(bank(g + 1)[:, 62 * half:62 * half + 62],
                                      tb[0:62, 0, P * half:P * half + P], crf[0:62, 0, 0:62])
                prod.give(mm, ("g", g + 1))
                u, g = u + 4, g + 2
                pe.wait_ge(value.sem, value.at((L, "hid", kv)))
                pe.wait_ge(stage_loaded, own[L, "loaded1"])
                free_bank(pe, g)
                for side in range(2):
                    for half in range(2):
                        blocks_of = hid[:, half, 31 * side:31 * side + 31]
                        if kv == 0:
                            mm = pe.matmul(bank(g)[:, 0:NCMP], w2s[:, half, 64 * (1 - side):64 * (1 - side) + P],
                                           blocks_of, start=(side == 0 and half == 0),
                                           stop=(side == 1 and half == 1))
                        else:
                            mm = pe.matmul(bank(g)[0:NCMP, 64 * side:64 * side + 64], blocks_of,
                                           w2s[:, half, 192:256], start=(half == 0), stop=(half == 1))
                prod.give(mm, ("g", g))
                g += 1
                if kv == 0:
                    norm_pe(pe, (L, "n", 6), 1, crf[:, 1], 32)
                    item_rotate_pe(pe, L, 6)
            pe.wait_ge(h_ready.sem, h_ready.at((L, "rot", 6)))
            pe.wait_ge(evac.sem, evac.at(("g", g - 1)))
            pe.wait_ge(scaled.sem, scaled.at((L, "gates")))
            softmax_pe(pe, L, attention, nsa_extra(L))
            u, g = own[L, "uc"], own[L, "gc"]
            pe.wait_ge(h_ready.sem, h_ready.at((L, "yb", 3)))
            with pe.Fori(0, 2) as i:
                for n in range(4):
                    for m in range(4):
                        pe.wait_ge(evac.sem, i * 16 + (g + 4 * n + m - 8 + 1))
                        if m < 3:
                            pe.wait_ge(lo_ready, i * 12 + (u + 3 * n + m + 1))
                        b = psum[:, 4 * (n % 2) + m]
                        if m < 2:
                            mm = three_passes(pe, b, unit_blocks(u + 3 * n + m, range(NC)),
                                              chunks_of(h_hi, h_lo, range(NC)))
                        else:
                            y_hi, y_lo = ((ya_hi, ya_lo), (nq_hi, nq_lo))[m - 2]
                            mm = three_passes(pe, b, unit_blocks(u + 3 * n + 2, range(4 * (m - 2), 4 * (m - 1))),
                                              chunks_of(y_hi, y_lo, range(4)))
                        mm.then_inc(prod.sem, 1)
            prod.give_loop((L, "up"), 32)
            u, g = own[L, "ud"], own[L, "gd"]
            pe.wait_ge(lo_ready, u + 1)
            for k in range(NC):
                pe.wait_ge(evac.sem, evac.at(("g", own[L, "gc"] + 4 * max(k, 6) + 3)))
                mm = three_passes(pe, bank(g), unit_blocks(u, [k]), chunks_of(mg_hi, mg_lo, [k]),
                                  first=(k == 0), last=(k == NC - 1))
            prod.give(mm, ("u", u))
            free_bank(pe, g + 1)
            for n in range(1, NC):
                pe.wait_ge(lo_ready, u + n + 1)
                mm = three_passes(pe, bank(g + n), unit_blocks(u + n, range(NC)),
                                  chunks_of(mg_hi, mg_lo, range(NC)))
                prod.give(mm, ("u", u + n))
                if n + 1 < NC:
                    free_bank(pe, g + n + 1)

        def hybrid_act(act, order, l, before):
            L = ("hy", l)
            attention = nsa_attention(l)
            if l == 0:
                act.wait_ge(*stream_ready(before, 0))
                for k, c in enumerate((IDENT, ONES64, PERM64)):
                    act.dma_start(crf[:, k], consts[:, c * P:(c + 1) * P]).then_inc(stage_loaded, 16)
                act.dma_start(cload[:].rearrange("p a n -> p (a n)"), constsr).then_inc(stage_loaded, 16)
            norm_act(act, (L, "pre"), [(X[:, c], stream_ready(before, c)) for c in range(NC)], D)
            for c in range(NC):
                split_value_act(act, (L, c), tb[:, c % 2], h_hi[:, c])
            if l == 0:
                act.wait_ge(stage_loaded, own[L, "loaded0"])
                part_hi.give(act.activation(crr[:], cload[:], ACT.Copy), "crr")
            u, g = own[L, "ua"], own[L, "ga"]
            for c in range(8):
                split_hi(act, u + c + LEAD)
                hi = (ya_hi if c < 4 else ka_hi)[:, c % 4]
                evac_split_act(act, g + c, hi, 0.125 if c < 4 else 1.0)
            for m in range(4):
                split_hi(act, u + 8 + m + LEAD)
            for t in range(4):
                act.wait_ge(prod.sem, prod.at(("g", g + 8 + t)))
                evac_hi.give(act.activation(
                    va_hi[:, t, :, 0:3:2, :], bank(g + 8 + t).rearrange("p (a b n) -> p a b n", a=4, b=2),
                    ACT.Copy), g + 8 + t)
            for c in range(4):
                split_hi(act, u + 12 + c + LEAD)
                act.wait_ge(evac.sem, evac.at(("g", g + 12 + c)))
                value.give(act.activation(za[:, c], za[:, c], ACT.Silu), (L, "za", c))
            sb_act(act, order, L)
            u, g = own[L, "ub"], own[L, "gb"]
            act.wait_ge(prod.sem, prod.at(("sb", L, 7)))
            act.wait_ge(evac.sem, evac.at(("g", g - 1)))
            act.dma_start(posi[:], pos).then_inc(stage_loaded, 16)
            act.dma_start(w2s[:], w2[l]).then_inc(stage_loaded, 16)
            act.dma_start(rc[:], rope_cst).then_inc(stage_loaded, 16)
            split_hi(act, u + LEAD)
            split_hi(act, u + 1 + LEAD)
            for k in range(2):
                act.wait_ge(scaled.sem, scaled.at((L, "angle", k)))
                value.give(act.activation((rsin, rcos)[k][:], flat((tb, sq)[k], TAB), ACT.Sin), (L, "trig", k))
            for s in range(14):
                if s >= 2:
                    split_hi(act, u + s + LEAD)
                if s == 1:
                    act.wait_ge(value.sem, value.at((L, "trig", 1)))
                if s in NORM_AT:
                    item_norm_act(act, l, NORM_AT[s])
                if s in ROTATE_AT:
                    item_hi_act(act, L, ROTATE_AT[s])
                if s >= 10:
                    act.wait_ge(evac.sem, evac.at(("g", g + s)))
                    value.give(act.activation(zb[:, s - 10], zb[:, s - 10], ACT.Silu), (L, "zb", s - 10))
            for m in range(3):
                split_hi(act, u + 14 + m + LEAD)
            for t in range(4):
                act.wait_ge(prod.sem, prod.at(("g", g + 14 + t)))
                evac_hi.give(act.activation(
                    nv_hi[:, t, :, 0:3:2, :], bank(g + 14 + t)[:, 0:256].rearrange("p (a b n) -> p a b n", a=2, b=2),
                    ACT.Copy), g + 14 + t)
            act.wait_ge(evac.sem, evac.at(("g", g + 17)))
            value.give(act.activation(gt[:], gt[:], ACT.Sigmoid), (L, "gates"))
            u, g = u + 17, g + 18
            for kv in range(2):
                split_value_act(act, (L, "f", kv), flat(ta, 992), f_hi[:])
                for m in range(4):
                    split_hi(act, u + m + LEAD)
                b1 = col.at["cmp_b1"] + 4 * l + 2 * kv
                act.wait_ge(evac.sem, evac.at(("g", g + 1)))
                order.link(act.activation(hid[:, 0], hid[:, 0], ACT.Silu, bias=par[:, b1:b1 + 1]))
                value.give(act.activation(hid[:, 1], hid[:, 1], ACT.Silu, bias=par[:, b1 + 1:b1 + 2]),
                           (L, "hid", kv))
                u, g = u + 4, g + 2
                if kv == 0:
                    item_norm_act(act, l, 6)
                    item_hi_act(act, L, 6)
                else:
                    act.wait_ge(prod.sem, prod.at(("g", g)))
                    act.wait_ge(scaled.sem, scaled.at((L, "vc")))
                    evac_hi.give(act.activation(vc_hi[0:NCMP, 0:3:2, :],
                                                bank(g)[0:NCMP, 0:P].rearrange("p (a n) -> p a n", a=2),
                                                ACT.Copy), g)
                g += 1
            softmax_act(act, L, attention, nsa_extra(L))
            u, g = own[L, "uc"], own[L, "gc"]
            base = prod.at((L, "up"))
            with act.Fori(0, 2) as i:
                for n in range(4):
                    for m in range(3):
                        split_hi_loop(act, i, 12, u + 3 * n + m + LEAD, i * 16 + (base + 4 * n + (-1, 0, 1)[m]))
                    for m in range(2):
                        act.wait_ge(prod.sem, i * 16 + (base + 4 * n + m + 1))
                        act.wait_ge(evac.sem, i * 16 + (g + 4 * n - 1))
                        act.activation(ta[:, m], psum[:, 4 * (n % 2) + m], ACT.Sigmoid).then_inc(value.sem, 1)
                    act.wait_ge(evac.sem, i * 16 + (g + 4 * n + 3))
                    act.activation(mg_hi[:, bass.ds(i * 4 + n, 1), :].rearrange("p a n -> p (a n)"),
                                   tb[:, 0], ACT.Copy).then_inc(part_hi.sem, 1)
            value.give_loop((L, "up"), 16)
            part_hi.give_loop((L, "up"), NC)
            u = own[L, "ud"]
            preload(act, ACT.Sqrt)
            for n in range(NC):
                split_hi(act, u + n + LEAD)

        def tables_dve(dve, order, L):
            a, t = flat(ta, TAB), flat(pn, TAB)
            dve.wait_ge(stage_loaded, own[L, "loaded1"])
            order.step(dve.tensor_copy(a[:, 0:S], posi[:]))
            order.step(dve.tensor_reduce(t[:, 0:32], a[:, 0:S].rearrange("p (a b) -> p a b", b=16), AXX, ALU.add))
            order.link(dve.tensor_scalar(a[:, S + 31:S + 32], t[:, 31:32], 1.0 / 32, None, ALU.mult))
            order.step(dve.tensor_tensor(a[:, S:S + 31], t[:, 0:31], t[:, 1:32], ALU.add))
            order.step(dve.tensor_scalar(a[:, S:S + 31], a[:, S:S + 31], 1.0 / 32, None, ALU.mult))
            order.step(dve.tensor_scalar(a, a, rc[:, 0:1], None, ALU.mult))
            magic = 1.5 * 2 ** 23
            two_pi = 6.283185307179586
            c1 = 6.28125
            c2 = 2029.0 / 2 ** 20
            c3 = two_pi - c1 - c2
            for k in range(2):
                r = flat((tb, sq)[k], TAB)
                order.step(dve.tensor_scalar(t, a, 1 / two_pi, 0.25 * k, ALU.mult, ALU.add))
                order.step(dve.tensor_scalar(t, t, magic, None, ALU.add))
                order.step(dve.tensor_scalar(t, t, magic, None, ALU.subtract))
                order.step(dve.scalar_tensor_tensor(out=r, in0=t, scalar=-c1, in1=a, op0=ALU.mult, op1=ALU.add))
                order.step(dve.scalar_tensor_tensor(out=r, in0=t, scalar=-c2, in1=r, op0=ALU.mult, op1=ALU.add))
                order.step(dve.scalar_tensor_tensor(out=r, in0=t, scalar=-c3, in1=r, op0=ALU.mult, op1=ALU.add))
                if k:
                    order.step(dve.tensor_scalar(r, r, two_pi / 4, None, ALU.add))
                scaled.give(dve.tensor_scalar(r, r, 3.1415925, -3.1415925, ALU.min, ALU.max), (L, "angle", k))
            dve.wait_ge(value.sem, value.at((L, "trig", 1)))
            order.step(dve.tensor_scalar(rsin[:], rsin[:], rc[:, 1:2], None, ALU.mult))

        def hybrid_dve(dve, order, l):
            L = ("hy", l)
            attention = nsa_attention(l)
            ng = col.at["norm_g_2"] + 8 * l
            pre_dve(dve, order, L, par[:, ng:ng + 8])
            u, g = own[L, "ua"], own[L, "ga"]
            order.link(dve.memset(va_hi[:, :, :, 1, :].bitcast(F32), 0.0))
            order.step(dve.memset(va_lo[:, :, :, 1, :].bitcast(F32), 0.0))
            for c in range(8):
                split_lo(dve, u + c + LEAD)
                hi, lo = ((ya_hi, ya_lo) if c < 4 else (ka_hi, ka_lo))
                evac_split_dve(dve, g + c, hi[:, c % 4], lo[:, c % 4], 0.125 if c < 4 else 1.0)
            for m in range(4):
                split_lo(dve, u + 8 + m + LEAD)
            for t in range(4):
                dve.wait_ge(evac_hi.sem, evac_hi.at(g + 8 + t))
                evac.give(dve.tensor_tensor(
                    va_lo[:, t, :, 0:3:2, :], bank(g + 8 + t).rearrange("p (a b n) -> p a b n", a=4, b=2),
                    va_hi[:, t, :, 0:3:2, :].bitcast(F32), ALU.subtract), ("g", g + 8 + t))
            for c in range(4):
                split_lo(dve, u + 12 + c + LEAD)
                dve.wait_ge(prod.sem, prod.at(("g", g + 12 + c)))
                evac.give(dve.tensor_copy(za[:, c], bank(g + 12 + c)), ("g", g + 12 + c))
            sb_dve(dve, order, L)
            u, g = own[L, "ub"], own[L, "gb"]
            order.link(dve.memset(nv_hi[:, :, :, 1, :].bitcast(F32), 0.0))
            order.link(dve.memset(nv_lo[:, :, :, 1, :].bitcast(F32), 0.0))
            order.link(dve.memset(kcf[:], 0.0))
            order.link(dve.memset(vc_lo[:].bitcast(F32), 0.0))
            c = col.at["q_norm_2"] + l
            order.link(dve.tensor_scalar(qgain[:], par[:, c:c + 1], 0.125, None, ALU.mult))
            order.sync()
            split_lo(dve, u + LEAD)
            split_lo(dve, u + 1 + LEAD)
            tables_dve(dve, order, L)
            for s in range(14):
                if s >= 2:
                    split_lo(dve, u + s + LEAD)
                dve.wait_ge(prod.sem, prod.at(("g", g + s)))
                b = bank(g + s)
                if s < 6:
                    evac.give(dve.tensor_copy(nf[:, s], b), ("g", g + s))
                elif s < 10:
                    kv, side = divmod(s - 6, 2)
                    order.link(dve.tensor_copy(zk[0:64, kv, side], b[0:64, 0:S:2]))
                    evac.give(dve.tensor_copy(zk[64:128, kv, side], b[64:128, 1:S:2]), ("g", g + s))
                else:
                    evac.give(dve.tensor_copy(zb[:, s - 10], b), ("g", g + s))
                if s in NORM_AT:
                    item_norm_dve(dve, l, NORM_AT[s])
                if s in ROTATE_AT:
                    item_rotate_dve(dve, order, L, ROTATE_AT[s])
            for m in range(3):
                split_lo(dve, u + 14 + m + LEAD)
            for t in range(4):
                dve.wait_ge(evac_hi.sem, evac_hi.at(g + 14 + t))
                order.link(dve.tensor_tensor(
                    nv_lo[:, t, :, 0:3:2, :], bank(g + 14 + t)[:, 0:256].rearrange("p (a b n) -> p a b n", a=2, b=2),
                    nv_hi[:, t, :, 0:3:2, :].bitcast(F32), ALU.subtract))
                evac.give(dve.tensor_copy(gt[:, t], bank(g + 14 + t)[:, 256:NAT2]), ("g", g + 14 + t))
            dve.wait_ge(value.sem, value.at((L, "gates")))
            for t in range(4):
                op = dve.tensor_scalar(gt[:, t, 0:8], gt[:, t, 0:8], rc[:, 2 + t:3 + t], None, ALU.mult)
                if t < 3:
                    order.link(op)
                else:
                    scaled.give(op, (L, "gates"))
            u, g = u + 17, g + 18
            for kv in range(2):
                pe_col = col.at["cmp_pe"] + 32 * l + 16 * kv
                dve.wait_ge(h_ready.sem, h_ready.at((L, "rot", 6 if kv else 5)))
                if kv == 0:
                    dve.wait_ge(sums.sem, sums.at((L, "rot", 5)))
                else:
                    dve.wait_ge(prod.sem, prod.at(("g", g - 1)))
                for side in range(2):
                    for a in range(2):
                        blocks_of = zk[:, kv, side].rearrange("p (j b) -> p b j", b=8)[:, :, a:a + 31]
                        dst = flat(ta, 992).rearrange("p (q s j) -> p q s j", q=16, s=2)[:, 8 * a:8 * a + 8, side]
                        op = dve.tensor_tensor(dst, blocks_of,
                                               par[:, pe_col + 8 * a:pe_col + 8 * a + 8].unsqueeze(2).broadcast_to((P, 8, 31)),
                                               ALU.add)
                        if side == 1 and a == 1:
                            scaled.give(op, (L, "f", kv))
                        else:
                            order.link(op)
                order.sync()
                split_value_dve(dve, (L, "f", kv), flat(ta, 992), f_hi[:], f_lo[:])
                for m in range(4):
                    split_lo(dve, u + m + LEAD)
                dve.wait_ge(prod.sem, prod.at(("g", g)))
                evac.give(dve.tensor_copy(tb[0:62, 0, 0:256], bank(g)[0:62, 0:256]), ("g", g))
                dve.wait_ge(prod.sem, prod.at(("g", g + 1)))
                evac.give(dve.tensor_copy(flat(hid, 124), bank(g + 1)[:, 0:124]), ("g", g + 1))
                u, g = u + 4, g + 2
                if kv == 0:
                    dve.wait_ge(prod.sem, prod.at(("g", g)))
                    evac.give(dve.tensor_copy(kcf[:, 0:NCMP], bank(g)[:, 0:NCMP]), ("g", g))
                    item_norm_dve(dve, l, 6)
                    item_rotate_dve(dve, order, L, 6)
                    scaled.give(dve.memset(vc_hi[:].bitcast(F32), 0.0), (L, "vc"))
                else:
                    dve.wait_ge(evac_hi.sem, evac_hi.at(g))
                    evac.give(dve.tensor_tensor(
                        vc_lo[0:NCMP, 0:3:2, :], bank(g)[0:NCMP, 0:P].rearrange("p (a n) -> p a n", a=2),
                        vc_hi[0:NCMP, 0:3:2, :].bitcast(F32), ALU.subtract), ("g", g))
                g += 1
            dve.wait_ge(scaled.sem, scaled.at((L, "gates")))
            softmax_dve(dve, order, L, attention, nsa_extra(L))
            u, g = own[L, "uc"], own[L, "gc"]
            base, v0, p0 = prod.at((L, "up")), value.at((L, "up")), part_hi.at((L, "up"))
            with dve.Fori(0, 2) as i:
                for n in range(4):
                    for m in range(3):
                        split_lo_loop(dve, i, 12, u + 3 * n + m + LEAD)
                    dve.wait_ge(value.sem, i * 8 + (v0 + 2 * n + 2))
                    dve.wait_ge(prod.sem, i * 16 + (base + 4 * n + 4))
                    dve.wait_ge(evac.sem, i * 16 + (g + 4 * n))
                    b = 4 * (n % 2)
                    dve.tensor_tensor(tb[:, 0], ta[:, 0], psum[:, b + 2], ALU.mult).then_inc(evac.sem, 1)
                    dve.tensor_tensor(tb[:, 1], ta[:, 1], psum[:, b + 3], ALU.mult).then_inc(evac.sem, 1)
                    dve.wait_ge(evac.sem, i * 16 + (g + 4 * n + 2))
                    dve.tensor_tensor(tb[:, 0], tb[:, 0], tb[:, 1], ALU.add).then_inc(evac.sem, 1)
                    dve.wait_ge(part_hi.sem, i * 4 + (p0 + n + 1))
                    c = bass.ds(i * 4 + n, 1)
                    dve.tensor_tensor(mg_lo[:, c, :].rearrange("p a n -> p (a n)"), tb[:, 0],
                                      mg_hi[:, c, :].bitcast(F32).rearrange("p a n -> p (a n)"),
                                      ALU.subtract).then_inc(evac.sem, 1)
            evac.give_loop((L, "up"), 32)
            u, g = own[L, "ud"], own[L, "gd"]
            for n in range(NC):
                split_lo(dve, u + n + LEAD)
                dve.wait_ge(prod.sem, prod.at(("g", g + n)))
                evac.give(dve.tensor_tensor(X[:, n], X[:, n], bank(g + n), ALU.add), ("g", g + n))

        value.plan("silu_c")
        plan_ffn("ffn0")
        plan_pool("pool")
        plan_ffn("ffn1")
        plan_ffn("ffn2")
        plan_mla("mla")
        plan_ffn("ffn3")
        plan_hybrid(0)
        plan_hybrid(1)
        last = ("hy", 1)
        assert cur.u == NU, (cur.u, NU)

        def gains(layer, sub):
            g = col.at["norm_g"] + 48 * layer + 16 * sub
            return lambda k: par[:, g + 8 * k:g + 8 * k + 8]

        with_ada = {"ffn0": [(5, 2)], "ffn1": [(5, 9)], "ffn2": [(2, 16), (3, None)], "ffn3": [(5, None)]}
        down_ada = {"ffn0": 7, "ffn1": 14, "ffn2": None, "ffn3": None}

        block = ctx.enter_context(nc.Block())

        @block.sync
        def _(sp):
            sp.dma_start(par[:], params).then_inc(small_loaded, 16)
            sp.dma_start(ones[:], consts[:, ONES * P:(ONES + 1) * P]).then_inc(small_loaded, 16)
            rows = [ada[4 * k:4 * k + 4].rearrange("t p n -> p t n") for k in range(4)]
            sp.dma_start(ada_first[:, 0:4], rows[0]).then_inc(first_loaded[0], 16)
            sp.dma_start(ada_first[:, 12:16], rows[3]).then_inc(first_loaded[3], 16)
            for u in range(RAW):
                sp.dma_start(raw[:, u], stream[u]).then_inc(raw_loaded[u], 16)
            with sp.Fori(0, (NU - RAW) // RAW) as i:
                for k in range(RAW):
                    sp.wait_ge(lo_ready, i * RAW + (k + 1))
                    sp.dma_start(raw[:, k], stream[bass.ds(i * RAW + (k + RAW), 1)]
                                 .rearrange("a p n -> p (a n)")).then_inc(raw_loaded[k], 16)
            if NU % RAW:
                sp.wait_ge(lo_ready, NU - RAW)
                sp.dma_start(raw[:, (NU - 1) % RAW], stream[NU - 1]).then_inc(raw_loaded[(NU - 1) % RAW], 16)
            for c in range(NC):
                sp.wait_ge(*stream_ready(last, c))
                sp.dma_start(out[:, c], X[:, c]).then_inc(stored, 16)
            sp.wait_ge(stored, 16 * NC)

        @block.gpsimd
        def _(pool):
            for k in (1, 2):
                pool.dma_start(ada_first[:, 4 * k:4 * k + 4], ada[4 * k:4 * k + 4]
                               .rearrange("t p n -> p t n")).then_inc(first_loaded[k], 16)
            first = 2 * NC
            for k in range(2):
                pool.dma_start(ada_raw[:, k], ada[first + k]).then_inc(ada_loaded[k], 16)
            pieces = 18 * NC
            with pool.Fori(0, (pieces - first - 2) // 2) as i:
                for k in range(2):
                    pool.wait_ge(ada_used, i * 2 + (first + k + 1))
                    pool.dma_start(ada_raw[:, k], ada[bass.ds(i * 2 + (first + k + 2), 1)]
                                   .rearrange("a p n -> p (a n)")).then_inc(ada_loaded[k], 16)

        @block.tensor
        def _(pe):
            pe.wait_ge(small_loaded, 32)
            ffn_pe(pe, "ffn0", with_ada["ffn0"], down_ada["ffn0"])
            pool_pe(pe, "pool")
            ffn_pe(pe, "ffn1", with_ada["ffn1"], down_ada["ffn1"])
            ffn_pe(pe, "ffn2", with_ada["ffn2"], down_ada["ffn2"])
            mla_pe(pe, "mla")
            ffn_pe(pe, "ffn3", with_ada["ffn3"], down_ada["ffn3"])
            hybrid_pe(pe, 0)
            hybrid_pe(pe, 1)

        @block.scalar
        def _(act):
            order = Chain(act, act_own)
            act.dma_start(X[:], xT).then_inc(x_loaded, 16)
            act.wait_ge(small_loaded, 32)
            value.give(act.activation(silu_c[:], par[:, 0:8], ACT.Silu), "silu_c")
            act.wait_ge(evac.sem, 4)
            act.wait_ge(x_loaded, 16)
            norm_act(act, ("ffn0", "pre"), [(X[:, c], None) for c in range(NC)], D)
            split_hi(act, 0)
            split_hi(act, 1)
            ffn_act(act, "ffn0", None, 0, with_ada["ffn0"])
            pool_act(act, "pool", "ffn0")
            ffn_act(act, "ffn1", "pool", 6, with_ada["ffn1"])
            ffn_act(act, "ffn2", "ffn1", 9, with_ada["ffn2"])
            mla_act(act, order, "mla", "ffn2")
            ffn_act(act, "ffn3", "mla", 15, with_ada["ffn3"])
            hybrid_act(act, order, 0, "ffn3")
            hybrid_act(act, order, 1, ("hy", 0))

        @block.vector
        def _(dve):
            order = Chain(dve, dve_own)
            for g in range(4):
                evac.give(dve.memset(eps[:, 2 * g:2 * g + 2], EPS), ("g", g))
            ysum.give(dve.memset(bcol[:], 0.0), "start")
            dve.wait_ge(small_loaded, 32)
            dve.wait_ge(value.sem, value.at("silu_c"))
            for j in range(2):
                ada_rows(dve, j, None, range(NC))
                ada_close_dve(dve, j, None)
                if j == 0:
                    norm_dve(dve, ("ffn0", "pre"))
            split_lo(dve, 0)
            split_lo(dve, 1)
            ffn_dve(dve, order, "ffn0", gains(0, 0), 0, with_ada["ffn0"], down_ada["ffn0"])
            pool_dve(dve, order, "pool", gains(0, 1))
            ffn_dve(dve, order, "ffn1", gains(0, 2), 6, with_ada["ffn1"], down_ada["ffn1"])
            ffn_dve(dve, order, "ffn2", gains(1, 0), 9, with_ada["ffn2"], down_ada["ffn2"])
            mla_dve(dve, order, "mla", gains(1, 1))
            ffn_dve(dve, order, "ffn3", gains(1, 2), 15, with_ada["ffn3"], down_ada["ffn3"])
            hybrid_dve(dve, order, 0)
            hybrid_dve(dve, order, 1)



def mla_units(units, blocks, w_in, w_uq, w_uk, w_uv, w_o):
    f = np.float32
    rotary = np.tile(w_in[:, 384:416], (1, 4))
    latents = blocks(np.concatenate([w_in[:, :384], rotary], 1))
    nope = w_uq[:, :, :64].reshape(256, 1024)
    rope = w_uq[:, :, 64:].reshape(256, 512)
    lift = np.zeros((HEADS, P, P), f)
    project = np.zeros((HEADS, P, P), f)
    for h in range(HEADS):
        half = slice(64 * (h % 2), 64 * (h % 2) + 64)
        lift[h, half] = w_uk[:, h].T
        project[h, :, half] = w_uv[:, h]
    return [units(latents), units(blocks(rope)), units(blocks(nope)), units(lift[:8]),
            units(project[:8]), units(lift[8:]), units(project[8:]), units(blocks(w_o))]


def hybrid_units(units, blocks, w_in, cmp_w1, w_up_a, w_up_b, w_out):
    f = np.float32
    names = ("sb_q", "sb_k", "sb_v", "sb_z", "n_q", "n_kc", "n_vc", "n_ks", "n_vs", "n_kw", "n_vw",
             "n_gate", "n_z", "gate_a", "gate_b")
    widths = (512, 512, 512, 512, 512, 128, 128, 128, 128, 128, 128, 24, 512, D, D)
    w, start = {}, 0
    for name, n in zip(names, widths):
        w[name] = w_in[:, start:start + n]
        start += n

    def dense(m):
        return units(blocks(m))

    def paired(m):
        return m.reshape(-1, 2, 4, 64).transpose(0, 2, 1, 3).reshape(-1, 512)

    def by_rows(m, per):
        n = m.shape[1]
        b = m.reshape(NC, P, n)
        made = []
        for k in range(0, NC, per):
            part = b[k:k + per].transpose(1, 0, 2).reshape(P, -1)
            made.append(np.concatenate([part, np.zeros((P, UNIT - part.shape[1]), f)], 1))
        return np.stack(made)

    def both_halves(m):
        return np.concatenate([m[:, :64], m[:, :64], m[:, 64:], m[:, 64:]], 1)

    def hidden(m):
        return m.reshape(4, 4, P, 256).transpose(0, 2, 1, 3).reshape(4, P, UNIT)
    up_b = paired(w_up_b.T).T
    gate_a, gate_b, a, b = blocks(w["gate_a"]), blocks(w["gate_b"]), blocks(w_up_a), blocks(up_b)
    merge = units(np.concatenate([gate_a, gate_b, a, b], 1))
    nat2 = np.concatenate([w["n_vs"], w["n_vw"], w["n_gate"]], 1)
    return [dense(w["sb_q"]), dense(w["sb_k"]), by_rows(w["sb_v"], 2), dense(w["sb_z"]),
            dense(paired(w["n_q"])), dense(w["n_ks"]), dense(w["n_kw"]), dense(both_halves(w["n_kc"])),
            dense(both_halves(w["n_vc"])), dense(paired(w["n_z"])), by_rows(nat2, 3),
            hidden(cmp_w1[0]), hidden(cmp_w1[1]), merge, dense(w_out)]


def constants():
    f = np.float32
    eye = np.eye(P, dtype=f)
    r = np.arange(P)

    def rotation(width):
        m = np.zeros((P, P), f)
        m[r // width * width + (r + width // 2) % width, r] = 1
        return m
    same = (r[:, None] // 64 == r[None, :] // 64).astype(f)
    consts = np.concatenate([eye, np.ones((P, P), f), same, rotation(32), rotation(64)], 1)
    k, q = r[:, None], r[None, :]
    cmp_mask = np.zeros((P, 4, 32), f)
    t = np.arange(S).reshape(4, P).T[:, :, None]
    b = np.arange(32)[None, None, :]
    cmp_mask[(16 * b + 31 > t) | (b >= NCMP)] = NEG
    constsr = np.concatenate([eye, np.where(q > k, f(NEG), f(0)),
                              np.where(k >= q, f(NEG), f(0)),
                              np.where(k >= q, f(-1), f(0)), -np.ones((P, P), f),
                              cmp_mask.reshape(P, P)], 1)
    pos = np.arange(S)
    cnt = np.stack([1.0 / (np.minimum(pos + w // 2, S) - np.maximum(pos - w // 2, 0)) for w in (2, 4, 8, 16)])
    pool_count = np.broadcast_to(cnt.astype(f), (P, 4, S))
    inv = (1.0 / (f(10000.0) ** (np.arange(0, 32, 2, dtype=f) / f(32)))).astype(f)
    ang = (pos.astype(f)[:, None] * inv[None, :]).astype(f)
    cos, sin = np.cos(ang).astype(f).T, np.sin(ang).astype(f).T
    mla_rope = np.stack([np.tile(np.concatenate([cos, cos]), (4, 1)),
                         np.tile(np.concatenate([-sin, sin]), (4, 1))], 1)
    inv2 = (f(10000.0) ** (-np.arange(32, dtype=f) / f(32))).astype(f)
    sign = np.tile(np.concatenate([-np.ones(32, f), np.ones(32, f)]), 2)
    visible = (np.arange(S).reshape(4, P).T >= 31).astype(f)
    rope_cst = np.concatenate([np.tile(inv2, 4)[:, None], sign[:, None], visible], 1)
    return {"consts": consts, "constsr": constsr.astype(f), "pool_count": pool_count,
            "mla_rope": mla_rope, "rope_cst": rope_cst}


def kernel(x, c, ada_w, ada_b, norm_g, ffn_w_in, ffn_w_out, pool_w, pool_b, pool_scale, mla_w_in,
           mla_q_norm, mla_kv_norm, mla_w_uq, mla_w_uk, mla_w_uv, mla_w_o, positions_2, norm_g_2,
           w_in_2, q_norm_g_2, k_norm_g_2, cmp_pe_2, cmp_w1_2, cmp_b1_2, cmp_w2_2, w_up_a_2,
           w_up_b_2, w_out_2):
    import concourse.bacc as bacc
    from concourse.bass_utils import run_bass_kernel_spmd

    f = np.float32

    def a_(v):
        return np.asarray(v)

    def blocks(w):
        k, n = w.shape
        return w.reshape(k // P, P, n // P, P).transpose(2, 0, 1, 3)

    def units(b):
        b = b.reshape(-1, P, P)
        n = -(-len(b) // 8)
        if len(b) % 8:
            b = np.concatenate([b, np.zeros((8 * n - len(b), P, P), f)])
        return b.reshape(n, 8, P, P).transpose(0, 2, 1, 3).reshape(n, P, UNIT)

    def ffn_units(layer, sub):
        w_in, w_out = a_(ffn_w_in)[layer, sub], a_(ffn_w_out)[layer, sub]
        gate, up = blocks(w_in[:, :FF]), blocks(w_in[:, FF:])
        first = units(np.stack([gate, up], 1))
        down = blocks(w_out)
        second = np.concatenate([units(down[n]) for n in range(NC)])
        return [first, second]

    def pool_units():
        w = a_(pool_w)[0]
        return [units(np.concatenate([blocks(w[g]) for g in range(4)]))]

    stages = ffn_units(0, 0) + pool_units() + ffn_units(0, 1) + ffn_units(1, 0)
    stages += mla_units(units, blocks, *(a_(v)[0] for v in (mla_w_in, mla_w_uq, mla_w_uk, mla_w_uv, mla_w_o)))
    stages += ffn_units(1, 1)
    for layer in range(2):
        stages += hybrid_units(units, blocks, *(a_(v)[layer] for v in (w_in_2, cmp_w1_2, w_up_a_2, w_up_b_2, w_out_2)))
    stream = np.concatenate(stages)

    def columns(v):
        return a_(v).reshape(-1, P).T

    doubled = lambda v: np.concatenate([v, v], -1)
    params = np.concatenate([
        columns(c), columns(ada_b), columns(norm_g), columns(pool_b), columns(pool_scale),
        columns(mla_q_norm), columns(mla_kv_norm), columns(norm_g_2), columns(doubled(a_(q_norm_g_2))),
        columns(doubled(a_(k_norm_g_2))), columns(cmp_b1_2), columns(cmp_pe_2)], 1)
    ada = a_(ada_w).reshape(2, NC, P, 9, D).transpose(0, 3, 1, 2, 4).reshape(144, P, D)
    xT = a_(x)[0].T.reshape(NC, P, S).transpose(1, 0, 2)

    tables = constants()
    inputs = {"stream": stream, "ada": ada, "xT": xT, "params": params}
    inputs.update(tables)
    inputs["pos"] = np.broadcast_to(a_(positions_2), (P, S))
    w2 = a_(cmp_w2_2).reshape(2, 2, 2, P, 64)
    gap = np.zeros((2, 2, P, 64), f)
    inputs["w2"] = np.concatenate([gap, w2[:, 0], gap, w2[:, 1]], -1).transpose(0, 2, 1, 3)

    nc = bacc.Bacc("TRN2", target_bir_lowering=False, num_devices=1)
    arrays, aps = {}, {}
    for name, v in inputs.items():
        arrays[name + "_in"] = np.ascontiguousarray(v)
        aps[name] = nc.dram_tensor(name + "_in", v.shape, mybir.dt.from_np(v.dtype),
                                   kind="ExternalInput").ap()
    out = nc.dram_tensor("out_x", (P, NC, S), F32, kind="ExternalOutput").ap()
    kernel_program(nc, out=out, NU=len(stream), **aps)
    r = run_bass_kernel_spmd(nc, [arrays], core_ids=[0])
    return r.results[0]["out_x"].transpose(2, 1, 0).reshape(1, S, D)
```
